# Optimizing a Trainium2 kernel written in Bass

```python
import jax, jax.numpy as jnp
from jax import lax
import numpy as np

D_MODEL = 1024
BATCH = 1
SEQ = 1024
DEPTH = 2

D_MIX = D_MODEL
HEAD_DIM = 64
NSA_WIDTH = D_MIX // 2
CONV_WIDTH = D_MIX - NSA_WIDTH
N_HEADS = NSA_WIDTH // HEAD_DIM
N_KV = 2
GROUP = N_HEADS // N_KV
N_CONV_GROUPS = CONV_WIDTH // HEAD_DIM
KV_W = N_KV * HEAD_DIM
N_BRANCH = 3
ROT_DIM = HEAD_DIM // 4
ROPE_THETA = 500000.0
CMP_LEN = 32
CMP_STRIDE = 16
CMP_HIDDEN = 128
SEL_BLOCK = 64
N_SEL = 8
WINDOW = 512
Q_BLOCK = 64
CONV_K = 3
D_FF = 2816
EPS = 1e-6
N_IN = NSA_WIDTH + 6 * KV_W + N_HEADS * N_BRANCH + 3 * CONV_WIDTH

kernel_name = "hymba_nsa_shortconv_convffn_adaln"

def rmsnorm(x, g):
    xf = x.astype(jnp.float32)
    r = lax.rsqrt(jnp.mean(xf * xf, axis=-1, keepdims=True) + EPS)
    return (xf * r).astype(x.dtype) * g

def causal_dwconv(x, w):
    k_taps = w.shape[0]
    s = x.shape[1]
    xp = jnp.pad(x, ((0, 0), (k_taps - 1, 0), (0, 0)))
    return sum(xp[:, k:k + s] * w[k] for k in range(k_taps))

def partial_rope(x, pos):
    half = ROT_DIM // 2
    freqs = ROPE_THETA ** (-jnp.arange(half, dtype=jnp.float32) / half)
    ang = pos.astype(jnp.float32)[..., None] * freqs
    cos = jnp.cos(ang)[:, :, None, :]
    sin = jnp.sin(ang)[:, :, None, :]
    xf = x.astype(jnp.float32)
    x1, x2, rest = xf[..., :half], xf[..., half:ROT_DIM], xf[..., ROT_DIM:]
    out = jnp.concatenate([x1 * cos - x2 * sin, x2 * cos + x1 * sin, rest], axis=-1)
    return out.astype(x.dtype)

def masked_softmax(s, mask):
    s = jnp.where(mask, s.astype(jnp.float32), -jnp.inf)
    m = jnp.max(s, axis=-1, keepdims=True)
    m = jnp.where(jnp.isfinite(m), m, 0.0)
    p = jnp.exp(s - m)
    return p / jnp.maximum(jnp.sum(p, axis=-1, keepdims=True), 1e-30)

def compress_blocks(tok, pe, w1, w2):
    b, hk, s, dh = tok.shape
    n_cmp = (s - CMP_LEN) // CMP_STRIDE + 1
    idx = jnp.arange(n_cmp)[:, None] * CMP_STRIDE + jnp.arange(CMP_LEN)[None, :]
    blk = tok[:, :, idx] + pe
    blk = blk.reshape(b, hk, n_cmp, CMP_LEN * dh)
    return jax.nn.silu(blk @ w1) @ w2

def nsa_attention(q, k_c, v_c, k_s, v_s, k_w, v_w, gates,
                  pe_k, w1_k, w2_k, pe_v, w1_v, w2_v):
    b, s = q.shape[0], q.shape[1]
    scale = HEAD_DIM ** -0.5
    qh = q.reshape(b, s, N_KV, GROUP, HEAD_DIM).transpose(0, 2, 3, 1, 4)
    gh = jax.nn.sigmoid(gates.astype(jnp.float32)).reshape(b, s, N_KV, GROUP, N_BRANCH)
    gh = gh.transpose(0, 2, 3, 1, 4)

    kc = compress_blocks(k_c, pe_k, w1_k, w2_k)
    vc = compress_blocks(v_c, pe_v, w1_v, w2_v)
    n_cmp = kc.shape[2]
    cmp_start = jnp.arange(n_cmp) * CMP_STRIDE
    cmp_end = cmp_start + CMP_LEN - 1
    n_slc = s // SEL_BLOCK
    n_sel = min(N_SEL, n_slc)
    slc_start = jnp.arange(n_slc) * SEL_BLOCK
    overlap = ((cmp_start[:, None] < slc_start[None, :] + SEL_BLOCK)
               & (cmp_start[:, None] + CMP_LEN > slc_start[None, :])).astype(jnp.float32)

    ks_blk = k_s.reshape(b, N_KV, n_slc, SEL_BLOCK, HEAD_DIM)
    vs_blk = v_s.reshape(b, N_KV, n_slc, SEL_BLOCK, HEAD_DIM)
    kw_pad = jnp.pad(k_w, ((0, 0), (0, 0), (WINDOW, 0), (0, 0)))
    vw_pad = jnp.pad(v_w, ((0, 0), (0, 0), (WINDOW, 0), (0, 0)))
    gather_blocks = jax.vmap(jax.vmap(lambda kb, ix: kb[ix]))
    j_blk = jnp.arange(n_slc)

    def query_block(qi):
        t0 = qi * Q_BLOCK
        pos = t0 + jnp.arange(Q_BLOCK)
        qb = lax.dynamic_slice_in_dim(qh, t0, Q_BLOCK, axis=3) * scale
        gb = lax.dynamic_slice_in_dim(gh, t0, Q_BLOCK, axis=3)

        s_c = jnp.einsum('bhgqd,bhkd->bhgqk', qb, kc)
        p_c = masked_softmax(s_c, cmp_end[None, :] <= pos[:, None])
        o_c = jnp.einsum('bhgqk,bhkd->bhgqd', p_c.astype(vc.dtype), vc)

        imp = jnp.einsum('bhgqk,kj->bhqj', p_c, overlap)
        blk_q = pos // SEL_BLOCK
        causal = j_blk[None, :] <= blk_q[:, None]
        forced = causal & ((j_blk[None, :] == 0) | (j_blk[None, :] == blk_q[:, None])
                           | (j_blk[None, :] == blk_q[:, None] - 1))
        imp = jnp.where(forced, jnp.inf, jnp.where(causal, imp, -jnp.inf))
        top_val, top_idx = lax.top_k(imp, n_sel)
        kg = gather_blocks(ks_blk, top_idx)
        vg = gather_blocks(vs_blk, top_idx)
        kg = kg.reshape(b, N_KV, Q_BLOCK, n_sel * SEL_BLOCK, HEAD_DIM)
        vg = vg.reshape(b, N_KV, Q_BLOCK, n_sel * SEL_BLOCK, HEAD_DIM)
        tok_pos = top_idx[..., None] * SEL_BLOCK + jnp.arange(SEL_BLOCK)
        m_s = (tok_pos <= pos[None, None, :, None, None]) & (top_val > -jnp.inf)[..., None]
        m_s = m_s.reshape(b, N_KV, 1, Q_BLOCK, n_sel * SEL_BLOCK)
        s_s = jnp.einsum('bhgqd,bhqmd->bhgqm', qb, kg)
        p_s = masked_softmax(s_s, m_s)
        o_s = jnp.einsum('bhgqm,bhqmd->bhgqd', p_s.astype(vg.dtype), vg)

        kwb = lax.dynamic_slice_in_dim(kw_pad, t0, Q_BLOCK + WINDOW, axis=2)
        vwb = lax.dynamic_slice_in_dim(vw_pad, t0, Q_BLOCK + WINDOW, axis=2)
        key_pos = t0 - WINDOW + jnp.arange(Q_BLOCK + WINDOW)
        diff = pos[:, None] - key_pos[None, :]
        m_w = (key_pos[None, :] >= 0) & (diff >= 0) & (diff < WINDOW)
        s_w = jnp.einsum('bhgqd,bhkd->bhgqk', qb, kwb)
        p_w = masked_softmax(s_w, m_w)
        o_w = jnp.einsum('bhgqk,bhkd->bhgqd', p_w.astype(vwb.dtype), vwb)

        o = gb[..., 0:1] * o_c + gb[..., 1:2] * o_s + gb[..., 2:3] * o_w
        return o.transpose(0, 3, 1, 2, 4).reshape(b, Q_BLOCK, NSA_WIDTH).astype(q.dtype)

    out = lax.map(query_block, jnp.arange(s // Q_BLOCK))
    return out.transpose(1, 0, 2, 3).reshape(b, s, NSA_WIDTH)

def setup_inputs(seed: int = 0) -> dict:
    key = jax.random.key(seed)
    ks = jax.random.split(key, 24)
    f32 = jnp.float32

    def nrm(k, shape, scale):
        return jax.random.normal(k, shape, f32) * scale

    x = nrm(ks[0], (BATCH, SEQ, D_MODEL), 1.0)
    c = nrm(ks[1], (BATCH, D_MODEL), 1.0)
    offs = jax.random.randint(ks[2], (BATCH, 1), 0, 4096, dtype=jnp.int32)
    positions = (offs + jnp.arange(SEQ, dtype=jnp.int32)[None, :]).astype(jnp.int32)
    return {
        "x": x,
        "c": c,
        "positions": positions,
        "w_mod": nrm(ks[3], (DEPTH, D_MODEL, 6 * D_MODEL), 0.5 * D_MODEL ** -0.5),
        "b_mod": nrm(ks[4], (DEPTH, 6 * D_MODEL), 0.02),
        "norm1_g": 1.0 + nrm(ks[5], (DEPTH, D_MODEL), 0.02),
        "w_in": nrm(ks[6], (DEPTH, D_MODEL, N_IN), D_MODEL ** -0.5),
        "cmp_pe_k": nrm(ks[7], (DEPTH, CMP_LEN, HEAD_DIM), 0.1),
        "cmp_w1_k": nrm(ks[8], (DEPTH, CMP_LEN * HEAD_DIM, CMP_HIDDEN), (CMP_LEN * HEAD_DIM) ** -0.5),
        "cmp_w2_k": nrm(ks[9], (DEPTH, CMP_HIDDEN, HEAD_DIM), CMP_HIDDEN ** -0.5),
        "cmp_pe_v": nrm(ks[10], (DEPTH, CMP_LEN, HEAD_DIM), 0.1),
        "cmp_w1_v": nrm(ks[11], (DEPTH, CMP_LEN * HEAD_DIM, CMP_HIDDEN), (CMP_LEN * HEAD_DIM) ** -0.5),
        "cmp_w2_v": nrm(ks[12], (DEPTH, CMP_HIDDEN, HEAD_DIM), CMP_HIDDEN ** -0.5),
        "conv_w": nrm(ks[13], (DEPTH, CONV_K, CONV_WIDTH), CONV_K ** -0.5),
        "grp_g_attn": 1.0 + nrm(ks[14], (DEPTH, NSA_WIDTH), 0.02),
        "grp_g_conv": 1.0 + nrm(ks[15], (DEPTH, CONV_WIDTH), 0.02),
        "w_out": nrm(ks[16], (DEPTH, D_MIX, D_MODEL), D_MIX ** -0.5),
        "norm2_g": 1.0 + nrm(ks[17], (DEPTH, D_MODEL), 0.02),
        "ffn_up": nrm(ks[18], (DEPTH, D_MODEL, 2 * D_FF), D_MODEL ** -0.5),
        "ffn_conv": nrm(ks[19], (DEPTH, CONV_K, 2 * D_FF), CONV_K ** -0.5),
        "ffn_down": nrm(ks[20], (DEPTH, D_FF, D_MODEL), D_FF ** -0.5),
        "final_g": 1.0 + nrm(ks[21], (D_MODEL,), 0.02),
    }

def reference(x, c, positions, w_mod, b_mod, norm1_g, w_in,
              cmp_pe_k, cmp_w1_k, cmp_w2_k, cmp_pe_v, cmp_w1_v, cmp_w2_v,
              conv_w, grp_g_attn, grp_g_conv, w_out, norm2_g,
              ffn_up, ffn_conv, ffn_down, final_g):
    b, s, _ = x.shape
    sizes = [NSA_WIDTH] + [KV_W] * 6 + [N_HEADS * N_BRANCH] + [CONV_WIDTH] * 3
    split_at = np.cumsum(sizes)[:-1].tolist()
    c_act = jax.nn.silu(c)

    def heads(t, n):
        return t.reshape(b, s, n, HEAD_DIM)

    def kv_layout(t):
        return t.transpose(0, 2, 1, 3)

    for l in range(DEPTH):
        mod = c_act @ w_mod[l] + b_mod[l]
        sh1, sc1, g1, sh2, sc2, g2 = [m[:, None, :] for m in jnp.split(mod, 6, axis=-1)]

        h = rmsnorm(x, norm1_g[l]) * (1.0 + sc1) + sh1
        proj = h @ w_in[l]
        q, kc, vc, ksel, vsel, kwin, vwin, gts, cb, cc, ch = jnp.split(proj, split_at, axis=-1)
        q = partial_rope(heads(q, N_HEADS), positions)
        kc = kv_layout(partial_rope(heads(kc, N_KV), positions))
        ksel = kv_layout(partial_rope(heads(ksel, N_KV), positions))
        kwin = kv_layout(partial_rope(heads(kwin, N_KV), positions))
        vc = kv_layout(heads(vc, N_KV))
        vsel = kv_layout(heads(vsel, N_KV))
        vwin = kv_layout(heads(vwin, N_KV))
        attn = nsa_attention(q, kc, vc, ksel, vsel, kwin, vwin, gts,
                             cmp_pe_k[l], cmp_w1_k[l], cmp_w2_k[l],
                             cmp_pe_v[l], cmp_w1_v[l], cmp_w2_v[l])
        conv = cb * causal_dwconv(cc * ch, conv_w[l])
        mix = jnp.concatenate([rmsnorm(attn, grp_g_attn[l]), rmsnorm(conv, grp_g_conv[l])], axis=-1)
        x = x + g1 * (mix @ w_out[l])

        h = rmsnorm(x, norm2_g[l]) * (1.0 + sc2) + sh2
        u = causal_dwconv(h @ ffn_up[l], ffn_conv[l])
        a, v = jnp.split(u, 2, axis=-1)
        x = x + g2 * ((jax.nn.silu(a) * v) @ ffn_down[l])

    return rmsnorm(x, final_g)


_drawn_inputs = setup_inputs


def setup_inputs(seed=0):
    import zlib

    import numpy as np

    out = dict(_drawn_inputs(seed))
    spreads = {}
    factors = {'norm1_g': 4.631,
     'cmp_pe_k': 8.0,
     'grp_g_attn': 8.0,
     'grp_g_conv': 8.0,
     'norm2_g': 6.64,
     'final_g': 7.461,
     'cmp_pe_v': 2.969}
    for name, (base, spread) in spreads.items():
        noise = np.random.default_rng([zlib.crc32(name.encode()), seed]).standard_normal(out[name].shape)
        drawn = base * np.exp(spread * noise) if base else spread * noise
        out[name] = __import__('jax').numpy.asarray(drawn.astype(out[name].dtype))
    for name, factor in factors.items():
        out[name] = (out[name] * factor).astype(out[name].dtype)
    return out
```

```python
from contextlib import ExitStack

import concourse.bass as bass
from concourse import mybir

F32 = mybir.dt.float32
BF16 = mybir.dt.bfloat16
I32 = mybir.dt.int32
ALU = mybir.AluOpType
ACT = mybir.ActivationFunctionType
AX = mybir.AxisListType.X

P = 128
D = 1024
KD = D // P
S = 1024
HS = 512
NT = S // P
DEPTH = 2
HD = 64
NH = 8
NKV = 2
NC = NH // NKV
DFF = 2816
NF = DFF // P
ROUNDS = ((0, 8), (8, 7), (15, 7))
NCMP = 63
NBLK = 16
NSEL = 8
EPS = 1e-6
BIG = -1e30
SCALE = HD ** -0.5
ROUND = 1.5 * 2.0 ** 23
TWO_PI = 6.283185307179586
TWO_PI_PARTS = (6.28125, 0.0019350051879882812, 3.0199159819567e-07)
PI_BELOW = 3.1415925
COL_KC, COL_VC, COL_KS, COL_VS, COL_KW, COL_VW, COL_CONV = 512, 640, 768, 896, 1024, 1152, 1304
NVG = 2 * P + 3 * NH
GATE = 2 * P

PB_MOD, P_N1, P_N2, P_GA, P_GC, P_CW, P_T2 = 0, 48, 56, 64, 68, 72, 84
P_T0, P_T1 = 128, 172
P_PEK, P_PEV = 216, 248
NPRM = 280

W_LAYER = 52
W_Q, W_K, W_C1, W_CV, W_WO, W_UP = 0, 2, 4, 8, 14, (18, 30, 41)
M_LAYER = 24
M_FIRST = 8
JOBS = NT * NC * 4
GROUPS = 192
RING = 96
SQ_FIRST, SQ_LAYER = 8, 20
VEC_CONV = 88
VEC_LAYER = 440


class Chain:

    def __init__(self, eng, sem):
        self.eng, self.sem, self.base, self.k, self.stack = eng, sem, 0, 0, []

    def inc(self, ins):
        ins.then_inc(self.sem, 1)
        self.k += 1

    def wait(self):
        self.eng.wait_ge(self.sem, self.base + self.k)

    def enter(self, iv, per):
        self.stack.append((self.base, self.k, per))
        self.base, self.k = self.base + self.k + iv * per, 0

    def leave(self, n):
        base, k, per = self.stack.pop()
        assert self.k == per, f"{self.sem}: {self.k} increments in a body said to have {per}"
        self.base, self.k = base, k + n * per


def job_index(i, c, j):
    return 16 * i + 4 * c + j


def n_groups(i):
    return 1 if i < 4 else 2


def groups_through(i, c, j):
    return job_index(i, c, j) + 1 if i < 4 else 64 + 2 * (job_index(i, c, j) - 64) + 2


def ring_of(i, j, group):
    if i < 4:
        return j % 2, lambda c: 8 * i + 2 * c + j // 2
    return group, lambda c: 32 + 16 * (i - 4) + 4 * c + j


def two_before(i, c, j):
    if j >= 2:
        return i, c, j - 2
    if isinstance(c, int) and c == 0:
        return i - 1, NC - 1, j + 2
    return i, c - 1, j + 2


def key_tiles(i, window):
    return list(range(max(0, i - 4) if window else 0, i + 1))


def build(nc, x, c, positions, w_mod, b_mod, norm1_g, w_in, cmp_pe_k, cmp_w1_k, cmp_w2_k, cmp_pe_v,
          cmp_w1_v, cmp_w2_v, conv_w, grp_g_attn, grp_g_conv, w_out, norm2_g, ffn_up, ffn_conv,
          ffn_down, final_g, k_f32, k_mask, out):
    with ExitStack() as ctx:
        def sb(name, shape, dt=F32):
            return ctx.enter_context(nc.sbuf_tensor(name, shape, dt))

        def sem(name):
            return ctx.enter_context(nc.semaphore(name))

        ps = ctx.enter_context(nc.psum_tensor("ps", [P, 8, HS], F32))

        xT = sb("xT", [P, KD, S])
        hT = sb("hT", [P, KD, S])
        big = sb("big", [P, 20, S])
        qT = big[:, 0:4, :]
        kT = big[:, 4:7, :]
        vcT = big[:, 7, :]
        kvpe = big[:, 8:12, :]
        att = big[:, 8:12, :].rearrange("p a (b f) -> p (a b) f", b=2)
        mixc = big[:, 12:16, :]
        cc_s = big[:, 16, :]
        cprod = big[:, 17, :]
        probs = hT[:, 4:6, :]
        probsT = hT[:, 6, :].rearrange("p (r f) -> p r f", r=2)
        wv = big[:, 15:18, :].rearrange("p a f -> p (a f)")[:, 0:KD * NVG].rearrange(
            "p (k f) -> p k f", k=KD)
        vals = big[:, 6:8, :].rearrange("p a (b f) -> p (a b) f", f=2 * P)
        ycat = big[:, 0:8, :]
        cosT, sinT = big[:, 18, :], big[:, 19, :]
        gate = sb("gate", [P, NT, 3 * NH])
        wr = sb("wr", [P, 2, KD, P])
        wm = sb("wm", [P, 2, KD, P])
        raw = sb("raw", [P, 2, S])
        sq = sb("sq", [P, 2, S])
        acc = sb("acc", [P, S])
        rt = sb("rt", [P, S])
        kf = sb("kf", [P, k_f32.shape[1]])
        kb = sb("kb", [P, k_mask.shape[1]], BF16)
        qs = sb("qs", [P, NC, P])
        prow = sb("prow", [P, 3, P])
        prm = sb("prm", [P, NPRM])
        mod = sb("mod", [P, 48])
        gsc = sb("gsc", [P, 2, KD])
        crow = sb("crow", [16, P])
        cst = sb("cst", [P, 16])
        cact = sb("cact", [P, 3, KD])
        w2 = sb("w2", [P, 2, HD])
        hid = sb("hid", [P, 2, 2, HD])
        hidt = sb("hidt", [P, 2, HD])
        kcT = sb("kcT", [P, HD])
        vcN = sb("vcN", [P, HD])
        sc = raw[:, 1, 0:512].rearrange("p (c g n) -> p c g n", g=2, n=HD)
        pc = raw[:, 1, 512:1024].rearrange("p (c g n) -> p c g n", g=2, n=HD)
        pcT = rt[:, 0:512].rearrange("p (c n) -> p c n", n=P)
        cm = sb("cm", [P, 3, NH])
        pg = sb("pg", [P, 2, HD])
        imp = sb("imp", [P, 2, 2, NBLK])
        cmpa = raw[:, 0, 0:512].rearrange("p (g j i) -> p g j i", g=2, j=NBLK)
        cmpb = raw[:, 0, 512:1024].rearrange("p (g j i) -> p g j i", g=2, j=NBLK)
        rank = sb("rank", [P, 2, NBLK])
        selb = sb("selb", [P, 2, HD], BF16)
        selbT = sb("selbT", [P, NT, P], BF16)
        smax = sb("smax", [P, 2, 2])
        ssum = sb("ssum", [P, 2, 2, NH])
        fac = sb("fac", [P, 3, 2, NH])
        ssq = sb("ssq", [P, 2, NT])
        o_t = rt[:, :].rearrange("p (b f) -> p b f", b=2)

        ident = kf[:, 0:128]
        rope_r = kf[:, 128:256]
        ones = kf[:, 256:384]
        freq = kf[:, 384:385]
        cmask = kf[:, 385:897].rearrange("p (t n) -> p t n", t=NT)
        keep = kf[:, 897:1153].rearrange("p (t a j) -> p t a j", t=NT, a=2)
        ltm = kf[:, 1153:1409].rearrange("p (j i) -> p j i", j=NBLK)
        identb = kb[:, 0:128]
        diagm = kb[:, 128:256]
        tailm = kb[:, 256:384]
        blk = kb[:, 384:384 + S]

        const_in = sem("const_in")
        pos_in = sem("pos_in")
        x_in = [sem(f"x_in{i}") for i in range(2)]
        x_turned = sem("x_turned")
        x_kept = [sem(f"x_kept{i}") for i in range(2)]
        cst_turned = sem("cst_turned")
        c_exp = sem("c_exp")
        cst_ready = sem("cst_ready")
        cact_ready = sem("cact_ready")
        angle_ready = sem("angle_ready")
        trig_ready = sem("trig_ready")
        prow_in = sem("prow_in")
        prow_turned = sem("prow_turned")
        w_in_sem = [sem(f"w_in{i}") for i in range(2)]
        half_done = [sem(f"half_done{i}") for i in range(2)]
        w_used = [sem(f"w_used{i}") for i in range(2)]
        wm_in = [sem(f"wm_in{i}") for i in range(2)]
        wm_used = [sem(f"wm_used{i}") for i in range(2)]
        wv_in = sem("wv_in")
        w2_in = sem("w2_in")
        modA_read = sem("modA_read")
        modB_read = sem("modB_read")
        acc_zero = sem("acc_zero")
        sq_ready = sem("sq_ready")
        sq_added = sem("sq_added")
        ss_done = sem("ss_done")
        ms_ready = sem("ms_ready")
        rms_ready = sem("rms_ready")
        xn_ready = sem("xn_ready")
        h_ready = sem("h_ready")
        pj_copied = sem("pj_copied")
        rot_done = sem("rot_done")
        rope_done = sem("rope_done")
        pe_added = sem("pe_added")
        v_done = sem("v_done")
        v_copied = sem("v_copied")
        gate_exp = sem("gate_exp")
        hid_exp = sem("hid_exp")
        hid_ready = sem("hid_ready")
        kvc_done = sem("kvc_done")
        kvc_ready = sem("kvc_ready")
        cc_copied = sem("cc_copied")
        cv_prod = sem("cv_prod")
        cv_tap = sem("cv_tap")
        cv_out = sem("cv_out")
        qsc_ready = sem("qsc_ready")
        cs_done = sem("cs_done")
        cs_shifted = sem("cs_shifted")
        cs_exp = sem("cs_exp")
        pc_ready = sem("pc_ready")
        pcT_done = sem("pcT_done")
        pcT_ready = sem("pcT_ready")
        oc_done = sem("oc_done")
        oc_read = sem("oc_read")
        sel_ready = sem("sel_ready")
        selT_done = sem("selT_done")
        selT_ready = sem("selT_ready")
        mixc_ready = sem("mixc_ready")
        qs_ready = sem("qs_ready")
        s_done = sem("s_done")
        smax_ready = sem("smax_ready")
        p_ready = sem("p_ready")
        t_done = sem("t_done")
        pt_ready = [sem(f"pt_ready{i}") for i in range(2)]
        pv_done = sem("pv_done")
        o_read = sem("o_read")
        att_ready = sem("att_ready")
        att_ssq = sem("att_ssq")
        att_ms = sem("att_ms")
        att_rms = sem("att_rms")
        att_normed = sem("att_normed")
        attT_done = sem("attT_done")
        attT_ready = sem("attT_ready")
        wo_added = sem("wo_added")
        u_tap = sem("u_tap")
        u_ready = sem("u_ready")
        silu_ready = sem("silu_ready")
        y_ready = sem("y_ready")
        dn_added = sem("dn_added")
        fin_ready = sem("fin_ready")
        fin_turned = sem("fin_turned")
        fin_copied = [sem(f"fin_copied{i}") for i in range(2)]
        out_done = [sem(f"out_done{i}") for i in range(2)]
        vec = sem("vec")

        waited = sem("waited")

        N_PROW = 12

        block = ctx.enter_context(nc.Block())

        def apart(eng):
            eng.sem_inc(waited, 1)

        @block.sync
        def _(sp):
            def load_mod(l, m, slot, n):
                sp.wait_ge(wm_used[slot], n + 1)
                sp.dma_start(wm[:, slot, :, :], w_mod[l, :, bass.ds(m * P, P)].rearrange(
                    "(k p) f -> p k f", p=P)).then_inc(wm_in[slot], 16)

            def load_w(slot, n, w, l, col, row0=0, nk=KD):
                sp.wait_ge(w_used[slot], n + 1)
                src = w[l, row0:row0 + nk * P, bass.ds(col, P)].rearrange("(k p) f -> p k f", p=P)
                sp.dma_start(wr[:, slot, 0:4, :], src[:, 0:4, :]).then_inc(w_in_sem[slot], 16)
                sp.dma_start(wr[:, slot, 4:nk, :], src[:, 4:nk, :]).then_inc(w_in_sem[slot], 16)

            sp.dma_start(crow[0:8, :], c.rearrange("o (k f) -> (o k) f", f=P)).then_inc(const_in, 16)
            sp.dma_start(crow[8:16, :], final_g.rearrange("(k f) -> k f", f=P)).then_inc(const_in, 16)
            sp.dma_start(kf[:, :], k_f32).then_inc(const_in, 16)
            sp.dma_start(hT[:, 0:2, :].rearrange("p k f -> p (k f)")[:, 0:k_mask.shape[1]],
                         k_mask).then_inc(const_in, 16)
            with sp.Fori(0, 4) as t:
                for s in range(2):
                    sp.wait_ge(x_kept[s], t + 1)
                    sp.dma_start(raw[:, s, :], x[0, bass.ds((t * 2 + s) * P, P), :]).then_inc(x_in[s], 16)
            sp.dma_start(sq[:, 0, :].bitcast(I32), positions.to_broadcast([P, S])).then_inc(pos_in, 16)
            with sp.Fori(0, M_FIRST) as t:
                for s in range(2):
                    load_mod(0, t * 2 + s, s, t)

            with sp.Fori(0, DEPTH) as l:
                sp.wait_ge(prow_turned, l + 1)
                rows = [(0, PB_MOD, b_mod[l, :].rearrange("(r f) -> r f", f=P), 48),
                        (0, P_N1, norm1_g[l, :].rearrange("(r f) -> r f", f=P), 8),
                        (0, P_N2, norm2_g[l, :].rearrange("(r f) -> r f", f=P), 8),
                        (0, P_GA, grp_g_attn[l, :].rearrange("(r f) -> r f", f=P), 4),
                        (0, P_GC, grp_g_conv[l, :].rearrange("(r f) -> r f", f=P), 4),
                        (0, P_CW, conv_w[l, :, :].rearrange("t (r f) -> (t r) f", f=P), 12),
                        (0, P_T2, ffn_conv[l, 2, :].rearrange("(r f) -> r f", f=P), 44),
                        (1, 0, ffn_conv[l, 0:2, :].rearrange("t (r f) -> (t r) f", f=P), 88)]
                for a, r0, src, n in rows:
                    sp.dma_start(prow[r0:r0 + n, a, :], src).then_inc(prow_in, 16)
                for r0, src in ((0, cmp_pe_k), (32, cmp_pe_v)):
                    for h in range(2):
                        sp.dma_start(prow[r0:r0 + 32, 2, 64 * h:64 * h + 64], src[l, :, :]).then_inc(prow_in, 16)
                sp.dma_start(w2[:, 0, :], cmp_w2_k[l, :, :]).then_inc(w2_in, 16)
                sp.dma_start(w2[:, 1, :], cmp_w2_v[l, :, :]).then_inc(w2_in, 16)

                ml, wl = l * M_LAYER + M_FIRST, l * W_LAYER
                with sp.Fori(0, 2) as t:
                    for s in range(2):
                        sp.wait_ge(w_used[s], wl + W_Q + t + 1)
                        for g in range(2):
                            sp.dma_start(wr[:, s, :, 64 * g:64 * g + 64],
                                         w_in[l, :, bass.ds((t * 2 + s) * HD + 256 * g, HD)].rearrange(
                                             "(k p) f -> p k f", p=P)).then_inc(w_in_sem[s], 16)
                        for b in range(2):
                            load_mod(l, t * 4 + (16 + 2 * s + b), b, ml + t * 2 + s)
                for n, col in enumerate((COL_KC, COL_VC, COL_KS, COL_KW)):
                    load_w(n % 2, wl + W_K + n // 2, w_in, l, col)
                    for b in range(2):
                        load_mod(l, 24 + 2 * n + b, b, ml + 4 + n)
                for n in range(8):
                    s, w1 = n % 2, (cmp_w1_k, cmp_w1_v)[n // 4]
                    sp.wait_ge(w_used[s], wl + W_C1 + n // 2 + 1)
                    for h in range(2):
                        sp.dma_start(wr[64 * h:64 * h + 64, s, :, :],
                                     w1[l, (n % 4) * 512:(n % 4) * 512 + 512, :].rearrange(
                                         "(t d) f -> d t f", d=HD)).then_inc(w_in_sem[s], 16)
                sp.dma_start(wv[:, :, 0:P], w_in[l, :, COL_VS:COL_VS + P].rearrange(
                    "(k p) f -> p k f", p=P)).then_inc(wv_in, 16)
                sp.dma_start(wv[:, :, P:NVG], w_in[l, :, COL_VW:COL_VW + NVG - P].rearrange(
                    "(k p) f -> p k f", p=P)).then_inc(wv_in, 16)
                with sp.Fori(0, 2) as t:
                    for n in range(6):
                        col = COL_CONV + (512, 1024, 0)[n % 3] + (n // 3) * P
                        load_w(n % 2, wl + t * 3 + (W_CV + n // 2), w_in, l, t * (2 * P) + col)
                        if n < 4:
                            for b in range(2):
                                load_mod(l, t * 8 + (32 + 2 * n + b), b, ml + t * 4 + (8 + n))
                with sp.Fori(0, 4) as t:
                    for s in range(2):
                        load_w(s, wl + W_WO + t, w_out, l, (t * 2 + s) * P)
                for r, (f0, nf) in enumerate(ROUNDS):
                    with sp.Fori(0, nf) as t:
                        for s in range(2):
                            load_w(s, wl + W_UP[r] + t, ffn_up, l, t * P + (f0 * P + s * DFF))
                    with sp.Fori(0, 4) as t:
                        for s in range(2):
                            load_w(s, wl + W_UP[r] + nf + t, ffn_down, l, (t * 2 + s) * P, f0 * P, nf)
                            if r == len(ROUNDS) - 1:
                                for b in range(2):
                                    load_mod(l * -1 + 1, t * 4 + (2 * s + b), b, ml + 16 + t * 2 + s)

            with sp.Fori(0, 4) as t:
                for s in range(2):
                    sp.wait_ge(fin_copied[s], t + 1)
                    sp.dma_start(out[0, bass.ds((t * 2 + s) * P, P), :], raw[:, s, :]).then_inc(out_done[s], 16)
            for s in range(2):
                sp.wait_ge(out_done[s], 16 * 4)

        @block.tensor
        def _(pe):
            for s in range(2):
                pe.sem_inc(w_used[s], 1)
                pe.sem_inc(wm_used[s], 1)
            pe.sem_inc(prow_turned, 1)
            pe.sem_inc(t_done, 1)
            pe.sem_inc(pv_done, 1)
            pe.sem_inc(cs_done, 1)

            def mod_pair(n, col0):
                for s in range(2):
                    pe.wait_ge(wm_in[s], (n + 1) * 16)
                    for k in range(KD):
                        mm = pe.matmul(ps[:, 7, bass.ds(col0 + s, 1)], wm[:, s, k, :], cact[:, 2, k:k + 1],
                                       start=(k == 0), stop=(k == KD - 1))
                    mm.then_inc(wm_used[s], 1)

            def gemm(slot, n, rhs, nk=KD, before=None, after=None):
                pe.wait_ge(w_in_sem[slot], (n + 1) * 32)
                for hf in range(2):
                    for k in range(nk):
                        if before is not None and hf == 0:
                            before(k)
                        mm = pe.matmul(ps[:, 2 * slot + hf, :], wr[:, slot, k, :],
                                       rhs(k)[:, hf * HS:hf * HS + HS], start=(k == 0), stop=(k == nk - 1))
                    mm.then_inc((half_done, w_used)[hf][slot], 1)
                    if after is not None:
                        after(hf)

            def sum_squares(n):
                pe.wait_ge(sq_added, n + 2)
                for hf in range(2):
                    mm = pe.matmul(ps[:, 4 + hf, :], ones, acc[:, hf * HS:hf * HS + HS], start=True, stop=True)
                mm.then_inc(ss_done, 1)

            pe.wait_ge(const_in, 64)
            pe.transpose(ps[:, 6, 0:16], crow[:, :], ident[0:16, 0:16]).then_inc(cst_turned, 1)
            with pe.Fori(0, 4) as t:
                for s in range(2):
                    pe.wait_ge(x_in[s], t * 16 + 16)
                    pe.wait_ge(x_kept[s], t + 1)
                    for k in range(KD):
                        mm = pe.transpose(ps[:, 2 * s + k // 4, (k % 4) * P:(k % 4) * P + P],
                                          raw[:, s, k * P:k * P + P], ident)
                    mm.then_inc(x_turned, 1)
            pe.wait_ge(cact_ready, 1)
            with pe.Fori(0, M_FIRST) as t:
                mod_pair(t, t * 2)

            def scores(l, i, c, j):
                g, window = j % 2, j // 2
                tiles = key_tiles(i, window)
                nk = len(tiles) * P
                lo, hi = 64 * g, 64 * g + 64
                if j == 0:
                    pe.wait_ge(qs_ready, l * 32 + c + (4 * i + 1))
                pe.wait_ge(p_ready, l * JOBS + c * 4 + (16 * i + j + 1))
                for b in range((nk + HS - 1) // HS):
                    w = min(HS, nk - b * HS)
                    bank = ps[:, 2 * g + b, :]
                    masks = []
                    if i >= 4 and not window:
                        masks.append((0, w, selbT[lo:hi, i, :], blk[lo:hi, b * HS:b * HS + w]))
                    if i >= 4 and window and b == 0:
                        masks.append((0, P, identb, tailm))
                    if (len(tiles) - 1) // 4 == b:
                        d = (len(tiles) - 1) % 4 * P
                        masks.append((d, P, identb, diagm))
                    for m, (at, n, lhs, rhs) in enumerate(masks):
                        pe.matmul(bank[:, at:at + n], lhs, rhs, start=(m == 0), stop=False,
                                  skip_group_check=True)
                    mm = pe.matmul(bank[:, 0:w], qs[lo:hi, 0, :],
                                   kT[lo:hi, window, tiles[0] * P + b * HS:tiles[0] * P + b * HS + w],
                                   start=not masks, stop=True, skip_group_check=True)
                mm.then_inc(s_done, 1)

            def turn(l, i, c, j):
                tiles = key_tiles(i, j // 2)
                pe.wait_ge(p_ready, l * JOBS + c * 4 + (16 * i + j + 3))
                for group in range(n_groups(i)):
                    r, before = ring_of(i, j, group)
                    pe.wait_ge(pt_ready[r], l * RING + before(c) + 1)
                    for a in range(4 * group, min(4 * group + 4, len(tiles))):
                        mm = pe.transpose(ps[:, 4 + r, (a % 4) * P:(a % 4) * P + P],
                                          probs[:, j % 2, a * P:a * P + P], ident)
                    mm.then_inc(t_done, 1)

            def weigh(l, i, c, j):
                g, window = j % 2, j // 2
                tiles = key_tiles(i, window)
                pe.wait_ge(o_read, l * NT + (i + 1))
                for group in range(n_groups(i)):
                    r, before = ring_of(i, j, group)
                    pe.wait_ge(pt_ready[r], l * RING + before(c) + 2)
                    for a in range(4 * group, min(4 * group + 4, len(tiles))):
                        mm = pe.matmul(ps[:, 6 + window, bass.ds(c * HD + 256 * g, HD)],
                                       probsT[:, r, (a % 4) * P:(a % 4) * P + P],
                                       vals[:, tiles[a], P * window + HD * g:P * window + HD * g + HD],
                                       start=(a == 0), stop=(a == len(tiles) - 1))
                mm.then_inc(pv_done, 1)

            with pe.Fori(0, DEPTH) as l:
                wl, ml = l * W_LAYER, l * M_LAYER + M_FIRST
                pe.wait_ge(prow_in, l * (16 * N_PROW) + 16 * N_PROW)
                for a, n, col in ((0, P, 0), (1, 88, P_T0), (2, 64, P_PEK)):
                    mm = pe.transpose(ps[:, 6, col:col + n], prow[0:n, a, :], ident[0:n, 0:n])
                mm.then_inc(prow_turned, 1)
                sum_squares(l * SQ_LAYER + SQ_FIRST)
                pe.wait_ge(modA_read, l + 1)
                apart(pe)

                def project(slot, n, chunk, rope, first, pair, col):
                    pe.wait_ge(pj_copied, l * 16 + chunk * 2 + 1)

                    def rotate(hf):
                        pe.wait_ge(pj_copied, l * 16 + chunk * 2 + (hf + 1 + 3))
                        pe.wait_ge(rope_done, l * 14 + rope * 2 + 1)
                        pe.matmul(ps[:, 4 + hf, :], rope_r, raw[:, slot, hf * HS:hf * HS + HS],
                                  start=True, stop=True).then_inc(rot_done, 1)

                    gemm(slot, n, lambda k: hT[:, k, :], before=first)
                    if rope is not None:
                        rotate(0)
                    mod_pair(pair, col)
                    if rope is not None:
                        rotate(1)

                with pe.Fori(0, 2) as t:
                    for s in range(2):
                        project(s, wl + W_Q + t, t * 2 + s, t * 2 + s,
                                (lambda k: pe.wait_ge(h_ready, l * 16 + (k + 1))) if s == 0 else None,
                                ml + t * 2 + s, t * 4 + (16 + 2 * s))
                for n, rope in enumerate((4, None, 5, 6)):
                    project(n % 2, wl + W_K + n // 2, 4 + n, rope, None, ml + 4 + n, 24 + 2 * n)

                pe.wait_ge(pj_copied, l * 16 + 16 + 3)
                for n in range(8):
                    s, kv = n % 2, n // 4
                    pe.wait_ge(w_in_sem[s], (wl + W_C1 + n // 2 + 1) * 32)
                    if n % 4 == 0:
                        pe.wait_ge(pe_added, l * 2 + kv + 1)
                    for g in range(2):
                        for a in range(8):
                            tok = 8 * (n % 4) + a
                            mm = pe.matmul(ps[:, 2 * kv + g, 0:NCMP], wr[64 * g:64 * g + 64, s, a, :],
                                           kvpe[64 * g:64 * g + 64, 2 * kv + tok // 16,
                                                tok:tok + 16 * (NCMP - 1) + 1:16],
                                           start=(tok == 0), stop=(tok == 31))
                        mm.then_inc((half_done, w_used)[g][s], 1)

                pe.wait_ge(hid_ready, l * 2 + 2)
                pe.wait_ge(wv_in, l * 32 + 32)
                for t in range(NT):
                    if t >= 4:
                        pe.wait_ge(v_copied, l * NT + (t - 3))
                    for k in range(KD):
                        mm = pe.matmul(ps[:, t % 4, 0:NVG], hT[:, k, t * P:t * P + P], wv[:, k, :],
                                       start=(k == 0), stop=(k == KD - 1))
                    mm.then_inc(v_done, 1)

                pe.wait_ge(w2_in, l * 32 + 32)
                pe.wait_ge(rope_done, l * 14 + 14 + 1)
                for kv in range(2):
                    for g in range(2):
                        lhs, rhs = (w2[:, 0, :], hid[:, 0, g, :]) if kv == 0 else (hid[:, 1, g, :], w2[:, 1, :])
                        mm = pe.matmul(ps[64 * g:64 * g + 64, 4 + kv, 0:HD], lhs, rhs, start=True, stop=True)
                mm.then_inc(kvc_done, 1)
                pe.wait_ge(v_copied, l * NT + NT)
                pe.wait_ge(kvc_ready, l + 1)
                apart(pe)

                with pe.Fori(0, 2) as t:
                    def compressed(p):
                        u, step = p // 3, p % 3
                        n = l * NT + t * 4 + u
                        if step == 0:
                            pe.wait_ge(qsc_ready, n + 1)
                            pe.wait_ge(oc_read, n + 1)
                            for cc in range(NC):
                                for g in range(2):
                                    mm = pe.matmul(ps[:, 4 + g, cc * HD:cc * HD + HD],
                                                   qs[64 * g:64 * g + 64, cc, :], kcT[64 * g:64 * g + 64, :],
                                                   start=True, stop=True)
                            mm.then_inc(cs_done, 1)
                        elif step == 1:
                            pe.wait_ge(pc_ready, n + 1)
                            pe.wait_ge(selT_ready, n + 1)
                            for cc in range(NC):
                                mm = pe.transpose(ps[:, 6, cc * P:cc * P + P],
                                                  pc[:, cc, :, :].rearrange("p g n -> p (g n)"), ident)
                            mm.then_inc(pcT_done, 1)
                        else:
                            pe.wait_ge(pcT_ready, n + 1)
                            for cc in range(NC):
                                for g in range(2):
                                    mm = pe.matmul(ps[:, 4 + g, 256 + cc * HD:256 + cc * HD + HD],
                                                   pcT[64 * g:64 * g + 64, cc, :], vcN[64 * g:64 * g + 64, :],
                                                   start=True, stop=True)
                            mm.then_inc(oc_done, 1)
                            pe.wait_ge(sel_ready, n + 1)
                            pe.transpose(ps[:, 6, 0:HD].bitcast(BF16),
                                         selb[:, :, :].rearrange("p g n -> p (g n)"),
                                         identb).then_inc(selT_done, 1)

                    for n in range(6):
                        free, count = ((cv_prod, 1), (cv_out, 1), (cc_copied, 1), (cv_prod, 2),
                                       (cv_out, 2), (cc_copied, 2))[n]
                        pe.wait_ge(free, l * 4 + t * 2 + count)
                        gemm(n % 2, wl + t * 3 + (W_CV + n // 2), lambda k: hT[:, k, :],
                             after=lambda hf, n=n: compressed(2 * n + hf))
                        if n < 4:
                            mod_pair(ml + t * 4 + (8 + n), t * 8 + (32 + 2 * n))
                pe.wait_ge(oc_read, l * NT + NT + 1)
                sum_squares(l * SQ_LAYER + SQ_FIRST + 4)

                pe.wait_ge(cv_out, l * 4 + 4 + 1)
                pe.wait_ge(cv_prod, l * 4 + 4 + 1)
                pe.wait_ge(selT_ready, l * NT + NT + 1)
                pe.wait_ge(modB_read, l + 1)
                pe.wait_ge(ms_ready, l * 3 + 2)
                scores(l, 0, 0, 0)
                scores(l, 0, 0, 1)
                turn(l, 0, 0, 0)

                def steps(i, c, last):
                    for j in range(4):
                        if not (last and j >= 2 and i == NT - 1):
                            scores(l, *((i, c, j + 2) if j < 2 else (i + 1, 0, j - 2) if last else (i, c + 1, j - 2)))
                        weigh(l, i, c, j)
                        if not (last and j == 3 and i == NT - 1):
                            turn(l, *((i, c, j + 1) if j < 3 else (i + 1, 0, 0) if last else (i, c + 1, 0)))

                for i in range(NT):
                    with pe.Fori(0, NC - 1) as cc:
                        steps(i, cc, False)
                    steps(i, NC - 1, True)

                for k in range(4):
                    s = k % 2
                    if k >= 2:
                        pe.wait_ge(attT_ready, l * 4 + (k - 1))
                    for i in range(NT):
                        if k == 0:
                            pe.wait_ge(att_normed, l * NT + (i + 1))
                        mm = pe.transpose(ps[:, 2 * s + i // 4, (i % 4) * P:(i % 4) * P + P],
                                          att[:, i, k * P:k * P + P], ident)
                    mm.then_inc(attT_done, 1)

                pe.wait_ge(attT_ready, l * 4 + 4)
                pe.wait_ge(mixc_ready, l * 4 + 4)
                apart(pe)
                with pe.Fori(0, 4) as t:
                    for s in range(2):
                        pe.wait_ge(wo_added, l * 8 + t * 2 + (s + 1))
                        gemm(s, wl + W_WO + t, lambda k: hT[:, k, :] if k < 4 else mixc[:, k - 4, :])
                sum_squares(l * SQ_LAYER + SQ_FIRST + 12)

                for r, (f0, nf) in enumerate(ROUNDS):
                    pe.wait_ge(dn_added, l * 24 + (8 * r + 2))
                    apart(pe)
                    with pe.Fori(0, nf) as t:
                        for s in range(2):
                            pe.wait_ge(u_ready, l * (2 * NF) + t * 2 + (2 * f0 + s + 1))
                            gemm(s, wl + W_UP[r] + t, lambda k: hT[:, k, :],
                                 before=(lambda k: pe.wait_ge(h_ready, l * 16 + (8 + k + 1)))
                                 if s == 0 and r == 0 else None)
                    pe.wait_ge(u_ready, l * (2 * NF) + (2 * (f0 + nf) + 2))
                    pe.wait_ge(y_ready, l * NF + (f0 + nf + 1))
                    apart(pe)
                    with pe.Fori(0, 4) as t:
                        for s in range(2):
                            pe.wait_ge(dn_added, l * 24 + t * 2 + (8 * r + s + 1))
                            gemm(s, wl + W_UP[r] + nf + t, lambda k: ycat[:, k, :], nk=nf)
                            if r == len(ROUNDS) - 1:
                                mod_pair(ml + 16 + t * 2 + s, t * 4 + 2 * s)

            sum_squares(DEPTH * SQ_LAYER + SQ_FIRST)
            for t in range(NT):
                s = t % 2
                if t >= 2:
                    pe.wait_ge(fin_copied[s], t // 2)
                for k in range(KD):
                    if t == 0:
                        pe.wait_ge(fin_ready, k + 1)
                    mm = pe.transpose(ps[:, 2 * s + k // 4, (k % 4) * P:(k % 4) * P + P],
                                      hT[:, k, t * P:t * P + P], ident)
                mm.then_inc(fin_turned, 1)

        @block.scalar
        def _(act):
            act.sem_inc(x_kept[0], 1)
            act.sem_inc(pj_copied, 3)
            act.sem_inc(p_ready, 2)
            act.sem_inc(pt_ready[1], 1)

            def slot(s):
                return ps[:, 2 * s:2 * s + 2, :].rearrange("p b f -> p (b f)")

            def square(src, s, n, ready=None):
                if ready is not None:
                    act.wait_ge(*ready)
                act.wait_ge(sq_added, n + 1)
                apart(act)
                act.activation(sq[:, s, :], src, ACT.Square).then_inc(sq_ready, 1)

            def root(n):
                act.wait_ge(ms_ready, n + 1)
                act.activation(rt[:, :], rt[:, :], ACT.Sqrt).then_inc(rms_ready, 1)

            def shift(n, mod0):
                for k in range(KD):
                    act.wait_ge(xn_ready, n + (k + 1))
                    act.activation(hT[:, k, :], hT[:, k, :], ACT.Identity,
                                   bias=mod[:, mod0 + k:mod0 + k + 1]).then_inc(h_ready, 1)

            act.wait_ge(cst_ready, 1)
            act.activation(cact[:, 0, :], cst[:, 0:8], ACT.Exp, scale=-1.0).then_inc(c_exp, 1)
            with act.Fori(0, 4) as t:
                act.wait_ge(x_turned, t * 2 + 1)
                act.activation(xT[:, :, bass.ds(t * 2 * P, P)],
                               slot(0).rearrange("p (k f) -> p k f", f=P), ACT.Copy).then_inc(x_kept[0], 1)
            act.wait_ge(angle_ready, 2)
            act.activation(sinT, sinT, ACT.Sin).then_inc(trig_ready, 1)
            act.activation(cosT, cosT, ACT.Sin).then_inc(trig_ready, 1)
            act.wait_ge(x_kept[1], 5)
            act.wait_ge(x_kept[0], 5)
            for k in range(KD):
                square(xT[:, k, :], k % 2, k)

            def softmax(l, i, c, j):
                g, window = j % 2, j // 2
                nk = len(key_tiles(i, window)) * P
                n = l * JOBS + c * 4 + (16 * i + j)
                act.wait_ge(smax_ready, n + 1)
                if not (isinstance(c, int) and c == 0 and j < 2 and i == 0):
                    act.wait_ge(t_done, l * GROUPS + groups_through(*two_before(i, c, j)) + 1)
                apart(act)
                act.activation(probs[:, g, 0:nk], slot(g)[:, 0:nk], ACT.Exp, bias=smax[:, g, 1:2], scale=SCALE,
                               accum_out=ssum[:, i % 2, window, bass.ds(c + 4 * g, 1)]).then_inc(p_ready, 1)

            def keep_turned(l, i, c, j):
                for group in range(n_groups(i)):
                    r, _ = ring_of(i, j, group)
                    if r == 1:
                        w = (min(4 * group + 4, len(key_tiles(i, j // 2))) - 4 * group) * P
                        after = groups_through(i, c, j) - n_groups(i) + group + 1
                        act.wait_ge(t_done, l * GROUPS + after + 1)
                        act.wait_ge(pv_done, l * JOBS + c * 4 + (16 * i + j + 1))
                        act.activation(probsT[:, 1, 0:w], ps[:, 5, 0:w], ACT.Copy).then_inc(pt_ready[1], 1)

            with act.Fori(0, DEPTH) as l:
                wl, sl = l * W_LAYER, l * SQ_LAYER + SQ_FIRST
                root(l * 3)
                shift(l * 16, 0)

                def copy_chunk(s, n, chunk, dst, rope):
                    for hf in range(2):
                        act.wait_ge((half_done, w_used)[hf][s], n + 1 + hf)
                        if rope is not None and hf == 0:
                            act.wait_ge(rope_done, l * 14 + rope * 2 + 1)
                        act.activation(dst[:, hf * HS:hf * HS + HS], ps[:, 2 * s + hf, :],
                                       ACT.Copy).then_inc(pj_copied, 1)

                with act.Fori(0, 2) as t:
                    for s in range(2):
                        copy_chunk(s, wl + W_Q + t, t * 2 + s, raw[:, s, :], t * 2 + s - 1 if s else t * 2)
                for n, rope in enumerate((4, None, 5, 6)):
                    copy_chunk(n % 2, wl + W_K + n // 2, 4 + n, vcT if n == 1 else raw[:, n % 2, :], rope)

                for kv in range(2):
                    act.wait_ge(w_used[1], wl + W_C1 + 2 * kv + 2 + 1)
                    act.activation(hidt[:, :, 0:NCMP], ps[:, 2 * kv:2 * kv + 2, 0:NCMP], ACT.Exp,
                                   scale=-1.0).then_inc(hid_exp, 1)
                    act.wait_ge(hid_ready, l * 2 + kv + 1)
                for t in range(NT):
                    act.wait_ge(v_done, l * NT + (t + 1))
                    act.activation(gate[:, t, :], ps[:, t % 4, GATE:NVG], ACT.Exp, scale=-1.0).then_inc(gate_exp, 1)
                    act.activation(vals[:, t, :], ps[:, t % 4, 0:GATE], ACT.Copy).then_inc(v_copied, 1)

                with act.Fori(0, 2) as t:
                    for p in range(12):
                        n, m = p // 2, p // 2 // 3
                        mm = l * 4 + t * 2 + m
                        if p % 2:
                            if n % 3 == 0:
                                act.wait_ge(w_used[n % 2], wl + t * 3 + (W_CV + n // 2 + 2))
                                act.wait_ge(cv_prod, mm + 1)
                                act.activation(cc_s, slot(n % 2), ACT.Copy).then_inc(cc_copied, 1)
                            elif n % 3 == 1:
                                act.wait_ge(cv_prod, mm + 2)
                                apart(act)
                                act.activation(mixc[:, bass.ds(t * 2 + m, 1), :].rearrange("p a f -> p (a f)"),
                                               cprod, ACT.Identity,
                                               scale=prm[:, bass.ds(t * 2 + (P_CW + 8 + m), 1)]).then_inc(cv_tap, 1)
                            else:
                                square(mixc[:, bass.ds(t * 2 + m, 1), :].rearrange("p a f -> p (a f)"),
                                       m, sl + t * 2 + m, (cv_out, mm + 2))
                        u = l * NT + t * 4 + p // 3
                        if p % 3 == 0:
                            act.wait_ge(cs_shifted, u + 1)
                            act.activation(pc[:, :, :, :], sc[:, :, :, :], ACT.Exp, scale=SCALE).then_inc(cs_exp, 1)
                        elif p % 3 == 1:
                            act.wait_ge(pcT_done, u + 1)
                            act.activation(pcT[:, :, :].rearrange("p c q -> p (c q)"), ps[:, 6, :],
                                           ACT.Copy).then_inc(pcT_ready, 1)
                root(l * 3 + 1)

                def sum_attention(i):
                    act.wait_ge(att_ready, l * NT + (i + 1))
                    act.activation(raw[:, 1, 0:512], att[:, i, :], ACT.Square,
                                   accum_out=ssq[:, 0, i:i + 1]).then_inc(att_ssq, 1)

                softmax(l, 0, 0, 0)
                keep_turned(l, 0, 0, 0)
                softmax(l, 0, 0, 1)

                def steps(i, c, last):
                    for j in range(4):
                        if not (last and j == 3 and i == NT - 1):
                            keep_turned(l, *((i, c, j + 1) if j < 3 else (i + 1, 0, 0) if last else (i, c + 1, 0)))
                        if not (last and j >= 2 and i == NT - 1):
                            softmax(l, *((i, c, j + 2) if j < 2 else (i + 1, 0, j - 2) if last else (i, c + 1, j - 2)))

                for i in range(NT):
                    with act.Fori(0, NC - 1) as cc:
                        steps(i, cc, False)
                    if i >= 1:
                        sum_attention(i - 1)
                    steps(i, NC - 1, True)
                sum_attention(NT - 1)
                act.wait_ge(att_ms, l + 1)
                act.activation(ssq[:, 1, :], ssq[:, 1, :], ACT.Sqrt).then_inc(att_rms, 1)
                for k in range(4):
                    act.wait_ge(attT_done, l * 4 + (k + 1))
                    act.activation(hT[:, k, :], slot(k % 2), ACT.Identity,
                                   scale=prm[:, P_GA + k:P_GA + k + 1]).then_inc(attT_ready, 1)

                with act.Fori(0, 4) as t:
                    for s in range(2):
                        square(xT[:, bass.ds(t * 2 + s, 1), :].rearrange("p a f -> p (a f)"), s,
                               sl + 4 + t * 2 + s, (wo_added, l * 8 + t * 2 + (s + 3)))
                root(l * 3 + 2)
                shift(l * 16 + 8, 24)

                act.wait_ge(sq_added, sl + 12 + 2)
                for r, (f0, nf) in enumerate(ROUNDS):
                    with act.Fori(0, nf) as t:
                        for s in range(2):
                            if s == 0:
                                act.wait_ge(y_ready, l * NF + t + (f0 + 1))
                            act.wait_ge(w_used[s], wl + W_UP[r] + t + 2)
                            apart(act)
                            act.activation(raw[:, s, :], slot(s), ACT.Identity,
                                           scale=prm[:, bass.ds(t + (P_T2 + f0 + NF * s), 1)]).then_inc(u_tap, 1)
                        act.wait_ge(u_ready, l * (2 * NF) + t * 2 + (2 * f0 + 1 + 2))
                        act.activation(sq[:, 0, :], raw[:, 0, :], ACT.Silu).then_inc(silu_ready, 1)
                with act.Fori(0, 4) as t:
                    for s in range(2):
                        square(xT[:, bass.ds(t * 2 + s, 1), :].rearrange("p a f -> p (a f)"), s,
                               sl + 12 + t * 2 + s, (dn_added, l * 24 + t * 2 + (16 + s + 3)))

            root(DEPTH * 3)
            for t in range(0, NT, 2):
                act.wait_ge(fin_turned, t + 1)
                if t >= 2:
                    act.wait_ge(out_done[0], 16 * (t // 2))
                act.activation(raw[:, 0, :], slot(0), ACT.Copy).then_inc(fin_copied[0], 1)

        @block.gpsimd
        def _(pool):
            pool.sem_inc(sq_added, 2)

            def zero(n):
                if n is not None:
                    pool.wait_ge(ss_done, n)
                    apart(pool)
                pool.memset(acc[:, :], 0.0).then_inc(acc_zero, 1)

            def add(s, n, zeros):
                pool.wait_ge(sq_ready, n + 1)
                pool.wait_ge(sq_added, n + 2)
                pool.wait_ge(acc_zero, zeros)
                pool.tensor_tensor(acc[:, :], acc[:, :], sq[:, s, :], ALU.add).then_inc(sq_added, 1)

            zero(None)
            for k in range(KD):
                add(k % 2, k, 1)
            with pool.Fori(0, DEPTH) as l:
                sl, z = l * SQ_LAYER + SQ_FIRST, l * 3
                zero(z + 1)
                with pool.Fori(0, 2) as t:
                    for p in range(12):
                        if p % 3 == 0:
                            u = t * 4 + p // 3
                            pool.wait_ge(cs_done, l * NT + u + 1)
                            if p == 0:
                                pool.wait_ge(rope_done, l * 14 + 14 + 1)
                            pool.tensor_copy(qs[:, :, :], qT[:, :, bass.ds(u * P, P)]).then_inc(qsc_ready, 1)
                        if p in (5, 11):
                            add(p // 6, sl + t * 2 + p // 6, z + 2)
                pool.wait_ge(cs_done, l * NT + NT + 1)
                apart(pool)
                with pool.Fori(0, NT) as i:
                    with pool.Fori(0, NC) as cc:
                        pool.wait_ge(s_done, l * JOBS + i * 16 + cc * 4 + 1)
                        pool.tensor_copy(qs[:, 0, :], qT[:, bass.ds(cc, 1), bass.ds(i * P, P)].rearrange(
                            "p a f -> p (a f)")).then_inc(qs_ready, 1)
                zero(z + 2)
                with pool.Fori(0, 4) as t:
                    for s in range(2):
                        add(s, sl + 4 + t * 2 + s, z + 3)
                zero(z + 3)
                with pool.Fori(0, 4) as t:
                    for s in range(2):
                        add(s, sl + 12 + t * 2 + s, z + 4)

        @block.vector
        def _(dve):
            dve.sem_inc(x_kept[1], 1)
            dve.sem_inc(rope_done, 1)
            dve.sem_inc(cv_prod, 1)
            dve.sem_inc(cv_out, 1)
            dve.sem_inc(oc_read, 1)
            dve.sem_inc(selT_ready, 1)
            dve.sem_inc(pt_ready[0], 1)
            dve.sem_inc(o_read, 1)
            dve.sem_inc(s_done, 1)
            dve.sem_inc(wo_added, 2)
            dve.sem_inc(u_ready, 2)
            dve.sem_inc(y_ready, 1)
            dve.sem_inc(dn_added, 2)
            v = Chain(dve, vec)

            def own(ins):
                v.inc(ins)
                v.wait()

            def slot(s):
                return ps[:, 2 * s:2 * s + 2, :].rearrange("p b f -> p (b f)")

            def at(t3, k):
                return t3[:, bass.ds(k, 1), :].rearrange("p a f -> p (a f)")

            def inverse_rms(n, count):
                dve.wait_ge(ss_done, n + 1)
                dve.tensor_scalar(rt[:, :], ps[:, 4:6, :].rearrange("p b f -> p (b f)"), 1.0 / count, EPS,
                                  ALU.mult, ALU.add).then_inc(ms_ready, 1)
                dve.wait_ge(rms_ready, n + 1)
                own(dve.reciprocal(rt[:, :], rt[:, :]))

            dve.wait_ge(const_in, 64)
            own(dve.tensor_copy(kb[:, :], hT[:, 0:2, :].rearrange("p k f -> p (k f)")[:, 0:k_mask.shape[1]]))
            own(dve.memset(hid[:, :, :, :], 0.0))
            own(dve.memset(selb[:, :, :], 0.0))
            dve.wait_ge(cst_turned, 1)
            dve.tensor_copy(cst[:, :], ps[:, 6, 0:16]).then_inc(cst_ready, 1)
            dve.wait_ge(c_exp, 1)
            own(dve.tensor_scalar(cact[:, 1, :], cact[:, 0, :], 1.0, None, ALU.add))
            own(dve.reciprocal(cact[:, 0, :], cact[:, 1, :]))
            dve.tensor_tensor(cact[:, 2, :], cst[:, 0:8], cact[:, 0, :], ALU.mult).then_inc(cact_ready, 1)
            with dve.Fori(0, 4) as t:
                dve.wait_ge(x_turned, t * 2 + 2)
                dve.tensor_copy(xT[:, :, bass.ds((t * 2 + 1) * P, P)],
                                slot(1).rearrange("p (k f) -> p k f", f=P)).then_inc(x_kept[1], 1)
            dve.wait_ge(pos_in, 16)
            own(dve.tensor_scalar(sinT, sq[:, 0, :].bitcast(I32), freq, None, ALU.mult))
            own(dve.tensor_scalar(rt[:, :], sinT, 1.0 / TWO_PI, ROUND, ALU.mult, ALU.add))
            own(dve.tensor_scalar(rt[:, :], rt[:, :], -ROUND, None, ALU.add))
            for part in TWO_PI_PARTS:
                own(dve.scalar_tensor_tensor(out=sinT, in0=rt[:, :], scalar=-part, in1=sinT,
                                             op0=ALU.mult, op1=ALU.add))
            dve.tensor_scalar(sinT, sinT, PI_BELOW, -PI_BELOW, ALU.min, ALU.max).then_inc(angle_ready, 1)
            dve.wait_ge(angle_ready, 1)
            own(dve.tensor_scalar(rt[:, :], sinT, -1.0, None, ALU.mult))
            own(dve.tensor_tensor(rt[:, :], rt[:, :], sinT, ALU.max))
            dve.tensor_scalar(cosT, rt[:, :], -1.0, TWO_PI / 4, ALU.mult, ALU.add).then_inc(angle_ready, 1)
            dve.wait_ge(trig_ready, 2)

            def row_max(l, i, c, j):
                g = j % 2
                nk = len(key_tiles(i, j // 2)) * P
                dve.wait_ge(s_done, l * JOBS + c * 4 + (16 * i + j + 2))
                own(dve.tensor_reduce(smax[:, g, 0:1], slot(g)[:, 0:nk], AX, ALU.max))
                dve.tensor_scalar(smax[:, g, 1:2], smax[:, g, 0:1], -SCALE, None, ALU.mult).then_inc(smax_ready, 1)

            def keep_turned(l, i, c, j):
                for group in range(n_groups(i)):
                    r, _ = ring_of(i, j, group)
                    if r == 0:
                        w = (min(4 * group + 4, len(key_tiles(i, j // 2))) - 4 * group) * P
                        after = groups_through(i, c, j) - n_groups(i) + group + 1
                        dve.wait_ge(t_done, l * GROUPS + after + 1)
                        dve.wait_ge(pv_done, l * JOBS + c * 4 + (16 * i + j + 1))
                        dve.tensor_copy(probsT[:, 0, 0:w], ps[:, 4, 0:w]).then_inc(pt_ready[0], 1)

            def heads(a):
                return a.rearrange("p (h d) -> p h d", d=HD)

            def gates(i, branch):
                return gate[:, i, branch:3 * NH:3]

            def finish_tile(l, i):
                b = i % 2
                dve.wait_ge(pv_done, l * JOBS + (16 * i + 16 + 1))
                own(dve.tensor_scalar(fac[:, 0, :, :], ssum[:, b, :, :], 1e-30, None, ALU.max))
                own(dve.reciprocal(fac[:, 1, :, :], fac[:, 0, :, :]))
                for br in range(2):
                    own(dve.tensor_tensor(fac[:, 2, br, :], fac[:, 1, br, :], gates(i, 1 + br), ALU.mult))
                for br in range(2):
                    ins = dve.tensor_tensor(heads(o_t[:, br, :]), heads(ps[:, 6 + br, :]),
                                            fac[:, 2, br, :].unsqueeze(2).to_broadcast([P, NH, HD]), ALU.mult)
                    if br == 0:
                        own(ins)
                ins.then_inc(o_read, 1)
                own(dve.tensor_tensor(att[:, i, :], att[:, i, :], o_t[:, 0, :], ALU.add))
                dve.wait_ge(o_read, l * NT + (i + 2))
                dve.tensor_tensor(att[:, i, :], att[:, i, :], o_t[:, 1, :], ALU.add).then_inc(att_ready, 1)

            with dve.Fori(0, DEPTH) as l:
                v.enter(l, VEC_LAYER)
                wl, ml = l * W_LAYER, l * M_LAYER + M_FIRST
                dve.wait_ge(prow_turned, l + 2)
                own(dve.tensor_copy(prm[:, :], ps[:, 6, 0:NPRM]))
                dve.wait_ge(wm_used[0], ml + 1)
                dve.wait_ge(wm_used[1], ml + 1)
                dve.tensor_tensor(mod[:, 0:16], ps[:, 7, 0:16], prm[:, 0:16], ALU.add).then_inc(modA_read, 1)
                dve.wait_ge(modA_read, l + 1)
                own(dve.scalar_tensor_tensor(out=gsc[:, 0, :], in0=mod[:, 8:16], scalar=1.0,
                                             in1=prm[:, P_N1:P_N1 + 8], op0=ALU.add, op1=ALU.mult))
                inverse_rms(l * 3, D)
                for k in range(KD):
                    dve.scalar_tensor_tensor(out=hT[:, k, :], in0=xT[:, k, :], scalar=gsc[:, 0, k:k + 1],
                                             in1=rt[:, :], op0=ALU.mult, op1=ALU.mult).then_inc(xn_ready, 1)

                def rotary(s, chunk, rope, dst):
                    for hf in range(2):
                        h0, h1 = hf * HS, hf * HS + HS
                        dve.wait_ge(pj_copied, l * 16 + chunk * 2 + (hf + 1 + 3))
                        own(dve.tensor_tensor(dst[:, h0:h1], raw[:, s, h0:h1], cosT[:, h0:h1], ALU.mult))
                        dve.wait_ge(rot_done, l * 14 + rope * 2 + (hf + 1))
                        own(dve.tensor_tensor(sq[:, s, h0:h1], ps[:, 4 + hf, :], sinT[:, h0:h1], ALU.mult))
                        dve.tensor_tensor(dst[:, h0:h1], dst[:, h0:h1], sq[:, s, h0:h1],
                                          ALU.add).then_inc(rope_done, 1)

                with dve.Fori(0, 2) as t:
                    v.enter(t, 8)
                    for s in range(2):
                        rotary(s, t * 2 + s, t * 2 + s, at(qT, t * 2 + s))
                    v.leave(2)

                def add_positions(src, a, prm0):
                    for b in range(2):
                        ins = dve.tensor_tensor(
                            kvpe[:, a + b, :].rearrange("p (n t) -> p n t", t=16),
                            src.rearrange("p (n t) -> p n t", t=16),
                            prm[:, prm0 + 16 * b:prm0 + 16 * b + 16].unsqueeze(1).to_broadcast([P, 64, 16]),
                            ALU.add)
                        if b == 0:
                            own(ins)
                    ins.then_inc(pe_added, 1)

                rotary(0, 4, 4, kT[:, 2, :])
                dve.wait_ge(rope_done, l * 14 + 10 + 1)
                add_positions(kT[:, 2, :], 0, P_PEK)
                dve.wait_ge(pj_copied, l * 16 + 12 + 3)
                add_positions(vcT, 2, P_PEV)
                rotary(0, 6, 5, kT[:, 0, :])
                rotary(1, 7, 6, kT[:, 1, :])

                for kv in range(2):
                    dve.wait_ge(hid_exp, l * 2 + kv + 1)
                    own(dve.tensor_scalar(hidt[:, :, 0:NCMP], hidt[:, :, 0:NCMP], 1.0, None, ALU.add))
                    own(dve.reciprocal(hidt[:, :, 0:NCMP], hidt[:, :, 0:NCMP]))
                    dve.tensor_tensor(hid[:, kv, :, 0:NCMP], ps[:, 2 * kv:2 * kv + 2, 0:NCMP],
                                      hidt[:, :, 0:NCMP], ALU.mult).then_inc(hid_ready, 1)
                dve.wait_ge(gate_exp, l * NT + NT)
                own(dve.tensor_scalar(gate[:, :, :], gate[:, :, :], 1.0, None, ALU.add))
                own(dve.reciprocal(gate[:, :, :], gate[:, :, :]))
                dve.wait_ge(kvc_done, l + 1)
                own(dve.tensor_copy(kcT[:, :], ps[:, 4, 0:HD]))
                dve.tensor_copy(vcN[:, :], ps[:, 5, 0:HD]).then_inc(kvc_ready, 1)

                with dve.Fori(0, 2) as t:
                    v.enter(t, VEC_CONV)

                    def conv(n):
                        m = n // 3
                        mm = l * 4 + t * 2 + m
                        dst = at(mixc, t * 2 + m)
                        if n % 3 == 1:
                            dve.wait_ge(cc_copied, mm + 1)
                            dve.wait_ge(w_used[n % 2], wl + t * 3 + (W_CV + n // 2 + 2))
                            dve.tensor_tensor(cprod, slot(n % 2), cc_s, ALU.mult).then_inc(cv_prod, 1)
                            dve.wait_ge(cv_tap, mm + 1)
                            for back, tap in ((1, 1), (2, 0)):
                                own(dve.scalar_tensor_tensor(
                                    out=dst[:, back:S], in0=cprod[:, 0:S - back],
                                    scalar=prm[:, bass.ds(t * 2 + (P_CW + 4 * tap + m), 1)],
                                    in1=dst[:, back:S], op0=ALU.mult, op1=ALU.add))
                        elif n % 3 == 2:
                            dve.wait_ge(w_used[n % 2], wl + t * 3 + (W_CV + n // 2 + 2))
                            dve.tensor_tensor(dst, slot(n % 2), dst, ALU.mult).then_inc(cv_out, 1)

                    def bcast(a, n):
                        return a.unsqueeze(2).to_broadcast([P, NH, n])

                    def compressed_softmax(u):
                        n = l * NT + u
                        flat = lambda a: a.rearrange("p c g n -> p (c g) n")
                        dve.wait_ge(cs_done, n + 2)
                        for g in range(2):
                            own(dve.tensor_tensor(
                                sc[:, :, g, :], ps[:, 4 + g, 0:256].rearrange("p (c n) -> p c n", n=HD),
                                cmask[:, bass.ds(u, 1), :].to_broadcast([P, NC, HD]), ALU.add))
                        own(dve.tensor_reduce(cm[:, 0, :], flat(sc[:, :, :, :]), AX, ALU.max))
                        own(dve.tensor_scalar(cm[:, 1, :], cm[:, 0, :], BIG / 10, None, ALU.max))
                        dve.tensor_tensor(flat(sc[:, :, :, :]), flat(sc[:, :, :, :]), bcast(cm[:, 1, :], HD),
                                          ALU.subtract).then_inc(cs_shifted, 1)
                        dve.wait_ge(cs_exp, n + 1)
                        own(dve.tensor_reduce(cm[:, 0, :], flat(pc[:, :, :, :]), AX, ALU.add))
                        own(dve.tensor_scalar(cm[:, 1, :], cm[:, 0, :], 1e-30, None, ALU.max))
                        own(dve.reciprocal(cm[:, 2, :], cm[:, 1, :]))
                        dve.tensor_tensor(flat(pc[:, :, :, :]), flat(pc[:, :, :, :]), bcast(cm[:, 2, :], HD),
                                          ALU.mult).then_inc(pc_ready, 1)

                    def select_blocks(u):
                        n = l * NT + u
                        dve.wait_ge(pc_ready, n + 1)
                        own(dve.tensor_reduce(pg[:, :, :].rearrange("p g n -> p (g n)"),
                                              pc[:, :, :, :].rearrange("p c g n -> p (g n) c"), AX, ALU.add))
                        own(dve.tensor_reduce(imp[:, 0, :, :].rearrange("p g j -> p (g j)"),
                                              pg[:, :, :].rearrange("p g (j a) -> p (g j) a", a=4), AX, ALU.add))
                        own(dve.tensor_tensor(imp[:, 0, :, 1:NBLK], imp[:, 0, :, 1:NBLK],
                                              pg[:, :, 3:60:4], ALU.add))
                        for a, op in ((0, ALU.mult), (1, ALU.add)):
                            own(dve.tensor_tensor(imp[:, 0, :, :], imp[:, 0, :, :],
                                                  keep[:, bass.ds(u, 1), a, :].to_broadcast([P, 2, NBLK]), op))
                        for g in range(2):
                            me = imp[:, 0, g, :].unsqueeze(2).to_broadcast([P, NBLK, NBLK])
                            other = imp[:, 0, g, :].unsqueeze(1).to_broadcast([P, NBLK, NBLK])
                            own(dve.tensor_tensor(cmpa[:, g, :, :], other, me, ALU.is_gt))
                            own(dve.tensor_tensor(cmpb[:, g, :, :], other, me, ALU.is_equal))
                            own(dve.tensor_tensor(cmpb[:, g, :, :], cmpb[:, g, :, :], ltm, ALU.mult))
                        own(dve.tensor_tensor(raw[:, 0, 0:512], raw[:, 0, 0:512], raw[:, 0, 512:1024], ALU.add))
                        own(dve.tensor_reduce(rank[:, :, :].rearrange("p g j -> p (g j)"),
                                              cmpa.rearrange("p g j i -> p (g j) i"), AX, ALU.add))
                        dve.tensor_scalar(selb[:, :, 0:NBLK], rank[:, :, :], NSEL - 0.5, BIG,
                                          ALU.is_ge, ALU.mult).then_inc(sel_ready, 1)

                    def compressed_output(u):
                        n = l * NT + u
                        dve.wait_ge(oc_done, n + 1)
                        for g in range(2):
                            gated = gate[:, bass.ds(u, 1), 12 * g:12 * g + 10:3].rearrange(
                                "p a h -> p (a h)").unsqueeze(2).to_broadcast([P, NC, HD])
                            ins = dve.tensor_tensor(
                                at(att, u)[:, 256 * g:256 * g + 256].rearrange("p (h d) -> p h d", d=HD),
                                ps[:, 4 + g, 256:512].rearrange("p (h d) -> p h d", d=HD), gated, ALU.mult)
                            if g == 0:
                                own(ins)
                        ins.then_inc(oc_read, 1)
                        dve.wait_ge(selT_done, n + 1)
                        dve.tensor_copy(at(selbT, u), ps[:, 6, 0:HD].bitcast(BF16)).then_inc(selT_ready, 1)

                    for p in range(12):
                        if p % 2:
                            conv(p // 2)
                        u = t * 4 + p // 3
                        if p % 3 == 0:
                            compressed_softmax(u)
                            select_blocks(u)
                        elif p % 3 == 2:
                            compressed_output(u)
                    v.leave(2)

                inverse_rms(l * 3 + 1, 512)
                for k in range(4):
                    dve.scalar_tensor_tensor(out=mixc[:, k, :], in0=mixc[:, k, :],
                                             scalar=prm[:, P_GC + k:P_GC + k + 1], in1=rt[:, :],
                                             op0=ALU.mult, op1=ALU.mult).then_inc(mixc_ready, 1)
                dve.wait_ge(wm_used[0], ml + 16 + 1)
                dve.wait_ge(wm_used[1], ml + 16 + 1)
                dve.tensor_tensor(mod[:, 16:48], ps[:, 7, 16:48], prm[:, 16:48], ALU.add).then_inc(modB_read, 1)
                dve.wait_ge(modB_read, l + 1)
                own(dve.scalar_tensor_tensor(out=gsc[:, 1, :], in0=mod[:, 32:40], scalar=1.0,
                                             in1=prm[:, P_N2:P_N2 + 8], op0=ALU.add, op1=ALU.mult))

                row_max(l, 0, 0, 0)
                row_max(l, 0, 0, 1)
                keep_turned(l, 0, 0, 0)

                def steps(i, c, last):
                    for j in range(4):
                        if not (last and j >= 2 and i == NT - 1):
                            row_max(l, *((i, c, j + 2) if j < 2 else (i + 1, 0, j - 2) if last else (i, c + 1, j - 2)))
                        if not (last and j == 3 and i == NT - 1):
                            keep_turned(l, *((i, c, j + 1) if j < 3 else (i + 1, 0, 0) if last else (i, c + 1, 0)))

                for i in range(NT):
                    with dve.Fori(0, NC - 1) as cc:
                        v.enter(cc, 4)
                        steps(i, cc, False)
                        v.leave(NC - 1)
                    steps(i, NC - 1, True)
                    finish_tile(l, i)
                dve.wait_ge(att_ssq, l * NT + NT)
                dve.tensor_scalar(ssq[:, 1, :], ssq[:, 0, :], 1.0 / 512, EPS, ALU.mult, ALU.add).then_inc(att_ms, 1)
                dve.wait_ge(att_rms, l + 1)
                own(dve.reciprocal(ssq[:, 0, :], ssq[:, 1, :]))
                for i in range(NT):
                    dve.tensor_scalar(att[:, i, :], att[:, i, :], ssq[:, 0, i:i + 1], None,
                                      ALU.mult).then_inc(att_normed, 1)

                with dve.Fori(0, 4) as t:
                    for s in range(2):
                        dve.wait_ge(w_used[s], wl + W_WO + t + 2)
                        xd = at(xT, t * 2 + s)
                        dve.scalar_tensor_tensor(out=xd, in0=slot(s), scalar=mod[:, bass.ds(t * 2 + (16 + s), 1)],
                                                 in1=xd, op0=ALU.mult, op1=ALU.add).then_inc(wo_added, 1)
                inverse_rms(l * 3 + 2, D)
                for k in range(KD):
                    dve.scalar_tensor_tensor(out=hT[:, k, :], in0=xT[:, k, :], scalar=gsc[:, 1, k:k + 1],
                                             in1=rt[:, :], op0=ALU.mult, op1=ALU.mult).then_inc(xn_ready, 1)

                for r, (f0, nf) in enumerate(ROUNDS):
                    with dve.Fori(0, nf) as t:
                        v.enter(t, 2)
                        for s in range(2):
                            dve.wait_ge(u_tap, l * (2 * NF) + t * 2 + (2 * f0 + s + 1))
                            for back, tap0 in ((1, P_T1), (2, P_T0)):
                                ins = dve.scalar_tensor_tensor(
                                    out=raw[:, s, back:S], in0=slot(s)[:, 0:S - back],
                                    scalar=prm[:, bass.ds(t + (tap0 + f0 + NF * s), 1)],
                                    in1=raw[:, s, back:S], op0=ALU.mult, op1=ALU.add)
                                if back == 1:
                                    own(ins)
                            ins.then_inc(u_ready, 1)
                        dve.wait_ge(silu_ready, l * NF + t + (f0 + 1))
                        dve.wait_ge(u_ready, l * (2 * NF) + t * 2 + (2 * f0 + 2 + 2))
                        dve.tensor_tensor(at(ycat, t), sq[:, 0, :], raw[:, 1, :], ALU.mult).then_inc(y_ready, 1)
                        v.leave(nf)
                    with dve.Fori(0, 4) as t:
                        for s in range(2):
                            dve.wait_ge(w_used[s], wl + W_UP[r] + nf + t + 2)
                            dve.wait_ge(dn_added, l * 24 + (8 * r + 2))
                            xd = at(xT, t * 2 + s)
                            dve.scalar_tensor_tensor(out=xd, in0=slot(s),
                                                     scalar=mod[:, bass.ds(t * 2 + (40 + s), 1)],
                                                     in1=xd, op0=ALU.mult, op1=ALU.add).then_inc(dn_added, 1)
                v.leave(DEPTH)

            inverse_rms(DEPTH * 3, D)
            for k in range(KD):
                dve.scalar_tensor_tensor(out=hT[:, k, :], in0=xT[:, k, :], scalar=cst[:, 8 + k:9 + k],
                                         in1=rt[:, :], op0=ALU.mult, op1=ALU.mult).then_inc(fin_ready, 1)
            for t in range(1, NT, 2):
                dve.wait_ge(fin_turned, t + 1)
                if t >= 2:
                    dve.wait_ge(out_done[1], 16 * (t // 2))
                dve.tensor_copy(raw[:, 1, :], slot(1)).then_inc(fin_copied[1], 1)


def shape_constants():
    import numpy as np
    f32 = np.float32
    q, n = np.arange(P), np.arange(P)
    ident = np.eye(P, dtype=f32)
    rope = np.zeros((P, P), f32)
    for h in range(2):
        for d in range(8):
            rope[64 * h + d + 8, 64 * h + d] = -1.0
            rope[64 * h + d, 64 * h + d + 8] = 1.0
    freq = np.zeros((P, 1), f32)
    for h in range(2):
        for d in range(16):
            freq[64 * h + d, 0] = f32(500000.0) ** f32(-(d % 8) / 8)
    tok = np.arange(NT)[:, None] * P + q[None, :]
    cmask = np.where((np.arange(HD)[None, None, :] * 16 + 31 <= tok[:, :, None])
                     & (np.arange(HD) < NCMP)[None, None, :], 0.0, BIG).astype(f32)
    b, j = (tok // HD)[:, :, None], np.arange(NBLK)[None, None, :]
    causal = j <= b
    forced = causal & ((j == 0) | (j == b) | (j == b - 1))
    keep = np.stack([np.where(causal & ~forced, 1.0, 0.0),
                     np.where(forced, -BIG, np.where(causal, 0.0, BIG))], 2).astype(f32)
    lt = np.broadcast_to((np.arange(NBLK)[None, :] < np.arange(NBLK)[:, None]).astype(f32)[None],
                         (P, NBLK, NBLK))
    k_f32 = np.concatenate([ident, rope, np.ones((P, P), f32), freq,
                            cmask.transpose(1, 0, 2).reshape(P, -1), keep.transpose(1, 0, 2, 3).reshape(P, -1),
                            lt.reshape(P, -1)], axis=1)
    blk = np.zeros((P, S), f32)
    for h in range(2):
        for j in range(NBLK):
            blk[64 * h + j, HD * j:HD * j + HD] = 1.0
    diag = np.where(n[None, :] > q[:, None], BIG, 0.0)
    tail = np.where(n[None, :] <= q[:, None], BIG, 0.0)
    k_mask = np.concatenate([ident, diag, tail, blk], axis=1).astype(f32)
    return np.ascontiguousarray(k_f32), np.ascontiguousarray(k_mask)


_INS = ["x", "c", "positions", "w_mod", "b_mod", "norm1_g", "w_in", "cmp_pe_k", "cmp_w1_k", "cmp_w2_k",
        "cmp_pe_v", "cmp_w1_v", "cmp_w2_v", "conv_w", "grp_g_attn", "grp_g_conv", "w_out", "norm2_g",
        "ffn_up", "ffn_conv", "ffn_down", "final_g"]


def kernel(**inputs):
    import numpy as np
    import concourse.bacc as bacc
    from concourse.bass_utils import run_bass_kernel_spmd

    nc = bacc.Bacc("TRN2", target_bir_lowering=False, num_devices=1)
    arrays, args = {}, []
    named = [(name, np.ascontiguousarray(inputs[name])) for name in _INS]
    named += list(zip(("k_f32", "k_mask"), shape_constants()))
    for name, a in named:
        arrays[f"in_{name}"] = a
        args.append(nc.dram_tensor(f"in_{name}", a.shape, mybir.dt.from_np(a.dtype), kind="ExternalInput").ap())
    args.append(nc.dram_tensor("out_0", (1, S, D), F32, kind="ExternalOutput").ap())
    build(nc, *args)
    return run_bass_kernel_spmd(nc, [arrays], core_ids=[0]).results[0]["out_0"]
```

```python
from contextlib import ExitStack

import concourse.bass as bass
from concourse import mybir

F32 = mybir.dt.float32
F32R = mybir.dt.float32r
BF16 = mybir.dt.bfloat16
I32 = mybir.dt.int32
ALU = mybir.AluOpType
ACT = mybir.ActivationFunctionType
AX = mybir.AxisListType.X

P = 128
D = 1024
KD = D // P
S = 1024
HS = 512
NT = S // P
DEPTH = 2
HD = 64
NH = 8
NKV = 2
NC = NH // NKV
DFF = 2816
NF = DFF // P
ROUNDS = ((0, 4), (4, 4), (8, 4), (12, 4), (16, 3), (19, 3))
NCMP = 63
NBLK = 16
NSEL = 8
EPS = 1e-6
BIG = -1e30
SCALE = HD ** -0.5
ROUND = 1.5 * 2.0 ** 23
TWO_PI = 6.283185307179586
TWO_PI_PARTS = (6.28125, 0.0019350051879882812, 3.0199159819567e-07)
PI_BELOW = 3.1415925
COL_KC, COL_VC, COL_KS, COL_VS, COL_KW, COL_VW, COL_CONV = 512, 640, 768, 896, 1024, 1152, 1304
NVG = 2 * P + 3 * NH
GATE = 2 * P

PB_MOD, P_N1, P_N2, P_GA, P_GC, P_CW, P_T2 = 0, 48, 56, 64, 68, 72, 84
P_T0, P_T1 = 128, 172
P_PEK, P_PEV = 216, 248
NPRM = 280

W_LAYER = 52
W_Q, W_K, W_C1, W_CV, W_WO, W_FF = 0, 2, 4, 8, 14, 18
W_ROUND = tuple(sum(nf + 2 for _, nf in ROUNDS[:r]) for r in range(len(ROUNDS)))
W_FFN = W_LAYER - W_FF
ADDED = KD * len(ROUNDS)
M_LAYER = 24
M_FIRST = 8
JOBS = NT * NC * 4
GROUPS = 192
RING = 96
SQ_FIRST, SQ_LAYER = 8, 20
VEC_CONV = 88
VEC_LAYER = 440


class Chain:

    def __init__(self, eng, sem):
        self.eng, self.sem, self.base, self.k, self.stack = eng, sem, 0, 0, []

    def inc(self, ins):
        ins.then_inc(self.sem, 1)
        self.k += 1

    def wait(self):
        self.eng.wait_ge(self.sem, self.base + self.k)

    def enter(self, iv, per):
        self.stack.append((self.base, self.k, per))
        self.base, self.k = self.base + self.k + iv * per, 0

    def leave(self, n):
        base, k, per = self.stack.pop()
        assert self.k == per, f"{self.sem}: {self.k} increments in a body said to have {per}"
        self.base, self.k = base, k + n * per


def job_index(i, c, j):
    return 16 * i + 4 * c + j


def n_groups(i):
    return 1 if i < 4 else 2


def groups_through(i, c, j):
    return job_index(i, c, j) + 1 if i < 4 else 64 + 2 * (job_index(i, c, j) - 64) + 2


def ring_of(i, j, group):
    if i < 4:
        return j % 2, lambda c: 8 * i + 2 * c + j // 2
    return group, lambda c: 32 + 16 * (i - 4) + 4 * c + j


def two_before(i, c, j):
    if j >= 2:
        return i, c, j - 2
    if isinstance(c, int) and c == 0:
        return i - 1, NC - 1, j + 2
    return i, c - 1, j + 2


def key_tiles(i, window):
    return list(range(max(0, i - 4) if window else 0, i + 1))


def build(nc, x, c, positions, w_mod, b_mod, norm1_g, w_in, cmp_pe_k, cmp_w1_k, cmp_w2_k, cmp_pe_v,
          cmp_w1_v, cmp_w2_v, conv_w, grp_g_attn, grp_g_conv, w_out, norm2_g, ffn_up, ffn_conv,
          ffn_down, final_g, k_f32, k_mask, out):
    with ExitStack() as ctx:
        def sb(name, shape, dt=F32):
            return ctx.enter_context(nc.sbuf_tensor(name, shape, dt))

        def sem(name):
            return ctx.enter_context(nc.semaphore(name))

        ps = ctx.enter_context(nc.psum_tensor("ps", [P, 8, HS], F32))

        xT = sb("xT", [P, KD, S])
        with ExitStack() as over:
            def split(name, shape):
                return over.enter_context(nc.sbuf_tensor(name, shape, F32R))

            h_lo = split("h_lo", [P, KD, S])
            y_hi = split("y_hi", [P, 4, S])
            y_lo = split("y_lo", [P, 4, S])
            h_hi = split("h_hi", [P, KD, S])
            w_hi = split("w_hi", [P, 2, S])
            split("tables", [P, 2, S])
            w_lo = split("w_lo", [P, 2, S])
        hT = sb("hT", [P, KD, S])
        big = sb("big", [P, 20, S])
        qT = big[:, 0:4, :]
        kT = big[:, 4:7, :]
        vcT = big[:, 7, :]
        kvpe = big[:, 8:12, :]
        att = big[:, 8:12, :].rearrange("p a (b f) -> p (a b) f", b=2)
        mixc = big[:, 12:16, :]
        cc_s = big[:, 16, :]
        cprod = big[:, 17, :]
        probs = hT[:, 4:6, :]
        probsT = hT[:, 6, :].rearrange("p (r f) -> p r f", r=2)
        wv = big[:, 15:18, :].rearrange("p a f -> p (a f)")[:, 0:KD * NVG].rearrange(
            "p (k f) -> p k f", k=KD)
        vals = big[:, 6:8, :].rearrange("p a (b f) -> p (a b) f", f=2 * P)
        cosT, sinT = big[:, 18, :], big[:, 19, :]
        wr = sb("wr", [P, 2, KD, P])
        gate = sb("gate", [P, NT, 3 * NH])
        wm = sb("wm", [P, 2, KD // 2, 2 * P])
        accm = sb("accm", [P, 2 * P])
        raw = sb("raw", [P, 2, S])
        sq = sb("sq", [P, 2, S])
        acc = sb("acc", [P, S])
        rt = sb("rt", [P, S])
        kf = sb("kf", [P, k_f32.shape[1]])
        kb = sb("kb", [P, k_mask.shape[1]], BF16)
        qs = sb("qs", [P, NC, P])
        prow = sb("prow", [P, 3, P])
        prm = sb("prm", [P, NPRM])
        mod = sb("mod", [P, 48])
        gsc = sb("gsc", [P, 2, KD])
        crow = sb("crow", [16, P])
        cst = sb("cst", [P, 16])
        cact = sb("cact", [P, 3, KD])
        w2 = sb("w2", [P, 2, HD])
        hid = sb("hid", [P, 2, 2, HD])
        hidt = sb("hidt", [P, 2, HD])
        kcT = sb("kcT", [P, HD])
        vcN = sb("vcN", [P, HD])
        sc = raw[:, 1, 0:512].rearrange("p (c g n) -> p c g n", g=2, n=HD)
        pc = raw[:, 1, 512:1024].rearrange("p (c g n) -> p c g n", g=2, n=HD)
        pcT = rt[:, 0:512].rearrange("p (c n) -> p c n", n=P)
        cm = sb("cm", [P, 3, NH])
        pg = sb("pg", [P, 2, HD])
        imp = sb("imp", [P, 2, 2, NBLK])
        cmpa = raw[:, 0, 0:512].rearrange("p (g j i) -> p g j i", g=2, j=NBLK)
        cmpb = raw[:, 0, 512:1024].rearrange("p (g j i) -> p g j i", g=2, j=NBLK)
        rank = sb("rank", [P, 2, NBLK])
        selb = sb("selb", [P, 2, HD], BF16)
        selbT = sb("selbT", [P, NT, P], BF16)
        smax = sb("smax", [P, 2, 2])
        ssum = sb("ssum", [P, 2, 2, NH])
        fac = sb("fac", [P, 3, 2, NH])
        ssq = sb("ssq", [P, 2, NT])
        o_t = rt[:, :].rearrange("p (b f) -> p b f", b=2)

        ident = kf[:, 0:128]
        rope_r = kf[:, 128:256]
        ones = kf[:, 256:384]
        freq = kf[:, 384:385]
        cmask = kf[:, 385:897].rearrange("p (t n) -> p t n", t=NT)
        keep = kf[:, 897:1153].rearrange("p (t a j) -> p t a j", t=NT, a=2)
        ltm = kf[:, 1153:1409].rearrange("p (j i) -> p j i", j=NBLK)
        identb = kb[:, 0:128]
        diagm = kb[:, 128:256]
        tailm = kb[:, 256:384]
        blk = kb[:, 384:384 + S]

        const_in = sem("const_in")
        pos_in = sem("pos_in")
        x_in = [sem(f"x_in{i}") for i in range(2)]
        x_turned = sem("x_turned")
        x_kept = [sem(f"x_kept{i}") for i in range(2)]
        cst_turned = sem("cst_turned")
        c_exp = sem("c_exp")
        cst_ready = sem("cst_ready")
        cact_ready = sem("cact_ready")
        angle_ready = sem("angle_ready")
        trig_ready = sem("trig_ready")
        prow_in = sem("prow_in")
        prow_turned = sem("prow_turned")
        w_in_sem = [sem(f"w_in{i}") for i in range(2)]
        half_done = [sem(f"half_done{i}") for i in range(2)]
        w_used = [sem(f"w_used{i}") for i in range(2)]
        wm_in = [sem(f"wm_in{i}") for i in range(2)]
        wm_used = [sem(f"wm_used{i}") for i in range(2)]
        wv_in = sem("wv_in")
        w2_in = sem("w2_in")
        mod_done = sem("mod_done")
        modA_read = sem("modA_read")
        modB_read = sem("modB_read")
        acc_zero = sem("acc_zero")
        sq_ready = sem("sq_ready")
        sq_added = sem("sq_added")
        ss_done = sem("ss_done")
        ms_ready = sem("ms_ready")
        rms_ready = sem("rms_ready")
        xn_ready = sem("xn_ready")
        h_ready = sem("h_ready")
        pj_copied = sem("pj_copied")
        rot_done = sem("rot_done")
        rope_done = sem("rope_done")
        pe_added = sem("pe_added")
        v_done = sem("v_done")
        v_copied = sem("v_copied")
        gate_exp = sem("gate_exp")
        hid_exp = sem("hid_exp")
        hid_ready = sem("hid_ready")
        kvc_done = sem("kvc_done")
        kvc_ready = sem("kvc_ready")
        cc_copied = sem("cc_copied")
        cv_prod = sem("cv_prod")
        cv_tap = sem("cv_tap")
        cv_out = sem("cv_out")
        qsc_ready = sem("qsc_ready")
        cs_done = sem("cs_done")
        cs_shifted = sem("cs_shifted")
        cs_exp = sem("cs_exp")
        pc_ready = sem("pc_ready")
        pcT_done = sem("pcT_done")
        pcT_ready = sem("pcT_ready")
        oc_done = sem("oc_done")
        oc_read = sem("oc_read")
        sel_ready = sem("sel_ready")
        selT_done = sem("selT_done")
        selT_ready = sem("selT_ready")
        mixc_ready = sem("mixc_ready")
        qs_ready = sem("qs_ready")
        s_done = sem("s_done")
        smax_ready = sem("smax_ready")
        p_ready = sem("p_ready")
        t_done = sem("t_done")
        pt_ready = [sem(f"pt_ready{i}") for i in range(2)]
        pv_done = sem("pv_done")
        o_read = sem("o_read")
        att_ready = sem("att_ready")
        att_ssq = sem("att_ssq")
        att_ms = sem("att_ms")
        att_rms = sem("att_rms")
        att_normed = sem("att_normed")
        attT_done = sem("attT_done")
        attT_ready = sem("attT_ready")
        wo_added = sem("wo_added")
        u_tap = sem("u_tap")
        u_ready = sem("u_ready")
        silu_ready = sem("silu_ready")
        w_high = [sem(f"w_high{i}") for i in range(2)]
        w_split = [sem(f"w_split{i}") for i in range(2)]
        h_high = sem("h_high")
        prod_ready = sem("prod_ready")
        y_high = sem("y_high")
        dn_done = sem("dn_done")
        y_ready = sem("y_ready")
        dn_added = sem("dn_added")
        fin_ready = sem("fin_ready")
        fin_turned = sem("fin_turned")
        fin_copied = [sem(f"fin_copied{i}") for i in range(2)]
        out_done = [sem(f"out_done{i}") for i in range(2)]
        mod_part = sem("mod_part")
        vec = sem("vec")

        waited = sem("waited")

        N_PROW = 12

        block = ctx.enter_context(nc.Block())

        def apart(eng):
            eng.sem_inc(waited, 1)

        @block.sync
        def _(sp):
            def load_mod(l, m, n):
                for b in range(2):
                    sp.wait_ge(wm_used[b], n + 1)
                    sp.dma_start(wm[:, b, :, :], w_mod[l, b * HS:b * HS + HS, bass.ds(m * P, 2 * P)].rearrange(
                        "(k p) f -> p k f", p=P)).then_inc(wm_in[b], 16)

            def load_w(slot, n, w, l, col, row0=0, nk=KD):
                sp.wait_ge(w_used[slot], n + 1)
                src = w[l, row0:row0 + nk * P, bass.ds(col, P)].rearrange("(k p) f -> p k f", p=P)
                sp.dma_start(wr[:, slot, 0:4, :], src[:, 0:4, :]).then_inc(w_in_sem[slot], 16)
                sp.dma_start(wr[:, slot, 4:nk, :], src[:, 4:nk, :]).then_inc(w_in_sem[slot], 16)

            sp.dma_start(crow[0:8, :], c.rearrange("o (k f) -> (o k) f", f=P)).then_inc(const_in, 16)
            sp.dma_start(crow[8:16, :], final_g.rearrange("(k f) -> k f", f=P)).then_inc(const_in, 16)
            sp.dma_start(kf[:, :], k_f32).then_inc(const_in, 16)
            sp.dma_start(hT[:, 0:2, :].rearrange("p k f -> p (k f)")[:, 0:k_mask.shape[1]],
                         k_mask).then_inc(const_in, 16)
            with sp.Fori(0, 4) as t:
                for s in range(2):
                    sp.wait_ge(x_kept[s], t + 1)
                    sp.dma_start(raw[:, s, :], x[0, bass.ds((t * 2 + s) * P, P), :]).then_inc(x_in[s], 16)
            sp.dma_start(sq[:, 0, :].bitcast(I32), positions.to_broadcast([P, S])).then_inc(pos_in, 16)
            with sp.Fori(0, M_FIRST) as t:
                load_mod(0, t * 2, t)

            with sp.Fori(0, DEPTH) as l:
                sp.wait_ge(prow_turned, l + 1)
                rows = [(0, PB_MOD, b_mod[l, :].rearrange("(r f) -> r f", f=P), 48),
                        (0, P_N1, norm1_g[l, :].rearrange("(r f) -> r f", f=P), 8),
                        (0, P_N2, norm2_g[l, :].rearrange("(r f) -> r f", f=P), 8),
                        (0, P_GA, grp_g_attn[l, :].rearrange("(r f) -> r f", f=P), 4),
                        (0, P_GC, grp_g_conv[l, :].rearrange("(r f) -> r f", f=P), 4),
                        (0, P_CW, conv_w[l, :, :].rearrange("t (r f) -> (t r) f", f=P), 12),
                        (0, P_T2, ffn_conv[l, 2, :].rearrange("(r f) -> r f", f=P), 44),
                        (1, 0, ffn_conv[l, 0:2, :].rearrange("t (r f) -> (t r) f", f=P), 88)]
                for a, r0, src, n in rows:
                    sp.dma_start(prow[r0:r0 + n, a, :], src).then_inc(prow_in, 16)
                for r0, src in ((0, cmp_pe_k), (32, cmp_pe_v)):
                    for h in range(2):
                        sp.dma_start(prow[r0:r0 + 32, 2, 64 * h:64 * h + 64], src[l, :, :]).then_inc(prow_in, 16)
                sp.dma_start(w2[:, 0, :], cmp_w2_k[l, :, :]).then_inc(w2_in, 16)
                sp.dma_start(w2[:, 1, :], cmp_w2_v[l, :, :]).then_inc(w2_in, 16)

                ml, wl = l * M_LAYER + M_FIRST, l * W_LAYER
                with sp.Fori(0, 2) as t:
                    for s in range(2):
                        sp.wait_ge(w_used[s], wl + W_Q + t + 1)
                        for g in range(2):
                            sp.dma_start(wr[:, s, :, 64 * g:64 * g + 64],
                                         w_in[l, :, bass.ds((t * 2 + s) * HD + 256 * g, HD)].rearrange(
                                             "(k p) f -> p k f", p=P)).then_inc(w_in_sem[s], 16)
                        load_mod(l, t * 4 + (16 + 2 * s), ml + t * 2 + s)
                for n, col in enumerate((COL_KC, COL_VC, COL_KS, COL_KW)):
                    load_w(n % 2, wl + W_K + n // 2, w_in, l, col)
                    load_mod(l, 24 + 2 * n, ml + 4 + n)
                for n in range(8):
                    s, w1 = n % 2, (cmp_w1_k, cmp_w1_v)[n // 4]
                    sp.wait_ge(w_used[s], wl + W_C1 + n // 2 + 1)
                    for h in range(2):
                        sp.dma_start(wr[64 * h:64 * h + 64, s, :, :],
                                     w1[l, (n % 4) * 512:(n % 4) * 512 + 512, :].rearrange(
                                         "(t d) f -> d t f", d=HD)).then_inc(w_in_sem[s], 16)
                sp.dma_start(wv[:, :, 0:P], w_in[l, :, COL_VS:COL_VS + P].rearrange(
                    "(k p) f -> p k f", p=P)).then_inc(wv_in, 16)
                sp.dma_start(wv[:, :, P:NVG], w_in[l, :, COL_VW:COL_VW + NVG - P].rearrange(
                    "(k p) f -> p k f", p=P)).then_inc(wv_in, 16)
                with sp.Fori(0, 2) as t:
                    for n in range(6):
                        col = COL_CONV + (512, 1024, 0)[n % 3] + (n // 3) * P
                        load_w(n % 2, wl + t * 3 + (W_CV + n // 2), w_in, l, t * (2 * P) + col)
                        if n < 4:
                            load_mod(l, t * 8 + (32 + 2 * n), ml + t * 4 + (8 + n))
                with sp.Fori(0, 4) as t:
                    for s in range(2):
                        load_w(s, wl + W_WO + t, w_out, l, (t * 2 + s) * P)
                for r, (f0, nf) in enumerate(ROUNDS):
                    w0 = wl + W_FF + W_ROUND[r]
                    with sp.Fori(0, nf) as t:
                        for s in range(2):
                            load_w(s, w0 + t, ffn_up, l, t * P + (f0 * P + s * DFF))
                        if r < 2:
                            load_mod(l * -1 + 1, t * 2 + 8 * r, ml + 16 + 4 * r + t)
                    with sp.Fori(0, 2) as t:
                        for s in range(2):
                            sp.wait_ge(w_used[s], w0 + nf + t + 1)
                            src = ffn_down[l, f0 * P:f0 * P + nf * P, bass.ds((t * 2 + s) * (2 * P), 2 * P)].rearrange(
                                "(k p) f -> p k f", p=P)
                            dst = wr[:, s, :, :].rearrange("p (k b) f -> p k (b f)", b=2)
                            sp.dma_start(dst[:, 0:2, :], src[:, 0:2, :]).then_inc(w_in_sem[s], 16)
                            sp.dma_start(dst[:, 2:nf, :], src[:, 2:nf, :]).then_inc(w_in_sem[s], 16)

            with sp.Fori(0, 4) as t:
                for s in range(2):
                    sp.wait_ge(fin_copied[s], t + 1)
                    sp.dma_start(out[0, bass.ds((t * 2 + s) * P, P), :], raw[:, s, :]).then_inc(out_done[s], 16)
            for s in range(2):
                sp.wait_ge(out_done[s], 16 * 4)

        @block.tensor
        def _(pe):
            for s in range(2):
                pe.sem_inc(w_used[s], 1)
            pe.sem_inc(prow_turned, 1)
            pe.sem_inc(mod_done, 1)
            pe.sem_inc(t_done, 1)
            pe.sem_inc(pv_done, 1)
            pe.sem_inc(cs_done, 1)

            def mod_pair(n, col0):
                pe.wait_ge(wm_used[1], n + 2)
                for s in range(2):
                    mm = pe.matmul(ps[:, 7, bass.ds(col0 + s, 1)], accm[:, s * P:s * P + P], ones[:, 0:1],
                                   start=True, stop=True)
                mm.then_inc(mod_done, 1)

            def gemm(slot, n, rhs, nk=KD, before=None, after=None):
                pe.wait_ge(w_in_sem[slot], (n + 1) * 32)
                for hf in range(2):
                    for k in range(nk):
                        if before is not None and hf == 0:
                            before(k)
                        mm = pe.matmul(ps[:, 2 * slot + hf, :], wr[:, slot, k, :],
                                       rhs(k)[:, hf * HS:hf * HS + HS], start=(k == 0), stop=(k == nk - 1))
                    mm.then_inc((half_done, w_used)[hf][slot], 1)
                    if after is not None:
                        after(hf)

            def sum_squares(n):
                pe.wait_ge(sq_added, n + 2)
                for hf in range(2):
                    mm = pe.matmul(ps[:, 4 + hf, :], ones, acc[:, hf * HS:hf * HS + HS], start=True, stop=True)
                mm.then_inc(ss_done, 1)

            pe.wait_ge(const_in, 64)
            pe.transpose(ps[:, 6, 0:16], crow[:, :], ident[0:16, 0:16]).then_inc(cst_turned, 1)
            with pe.Fori(0, 4) as t:
                for s in range(2):
                    pe.wait_ge(x_in[s], t * 16 + 16)
                    pe.wait_ge(x_kept[s], t + 1)
                    for k in range(KD):
                        mm = pe.transpose(ps[:, 2 * s + k // 4, (k % 4) * P:(k % 4) * P + P],
                                          raw[:, s, k * P:k * P + P], ident)
                    mm.then_inc(x_turned, 1)
            with pe.Fori(0, M_FIRST) as t:
                mod_pair(t, t * 2)

            def scores(l, i, c, j):
                g, window = j % 2, j // 2
                tiles = key_tiles(i, window)
                nk = len(tiles) * P
                lo, hi = 64 * g, 64 * g + 64
                if j == 0:
                    pe.wait_ge(qs_ready, l * 32 + c + (4 * i + 1))
                pe.wait_ge(p_ready, l * JOBS + c * 4 + (16 * i + j + 1))
                for b in range((nk + HS - 1) // HS):
                    w = min(HS, nk - b * HS)
                    bank = ps[:, 2 * g + b, :]
                    masks = []
                    if i >= 4 and not window:
                        masks.append((0, w, selbT[lo:hi, i, :], blk[lo:hi, b * HS:b * HS + w]))
                    if i >= 4 and window and b == 0:
                        masks.append((0, P, identb, tailm))
                    if (len(tiles) - 1) // 4 == b:
                        d = (len(tiles) - 1) % 4 * P
                        masks.append((d, P, identb, diagm))
                    for m, (at, n, lhs, rhs) in enumerate(masks):
                        pe.matmul(bank[:, at:at + n], lhs, rhs, start=(m == 0), stop=False,
                                  skip_group_check=True)
                    mm = pe.matmul(bank[:, 0:w], qs[lo:hi, 0, :],
                                   kT[lo:hi, window, tiles[0] * P + b * HS:tiles[0] * P + b * HS + w],
                                   start=not masks, stop=True, skip_group_check=True)
                mm.then_inc(s_done, 1)

            def turn(l, i, c, j):
                tiles = key_tiles(i, j // 2)
                pe.wait_ge(p_ready, l * JOBS + c * 4 + (16 * i + j + 3))
                for group in range(n_groups(i)):
                    r, before = ring_of(i, j, group)
                    pe.wait_ge(pt_ready[r], l * RING + before(c) + 1)
                    for a in range(4 * group, min(4 * group + 4, len(tiles))):
                        mm = pe.transpose(ps[:, 4 + r, (a % 4) * P:(a % 4) * P + P],
                                          probs[:, j % 2, a * P:a * P + P], ident)
                    mm.then_inc(t_done, 1)

            def weigh(l, i, c, j):
                g, window = j % 2, j // 2
                tiles = key_tiles(i, window)
                pe.wait_ge(o_read, l * NT + (i + 1))
                for group in range(n_groups(i)):
                    r, before = ring_of(i, j, group)
                    pe.wait_ge(pt_ready[r], l * RING + before(c) + 2)
                    for a in range(4 * group, min(4 * group + 4, len(tiles))):
                        mm = pe.matmul(ps[:, 6 + window, bass.ds(c * HD + 256 * g, HD)],
                                       probsT[:, r, (a % 4) * P:(a % 4) * P + P],
                                       vals[:, tiles[a], P * window + HD * g:P * window + HD * g + HD],
                                       start=(a == 0), stop=(a == len(tiles) - 1))
                mm.then_inc(pv_done, 1)

            with pe.Fori(0, DEPTH) as l:
                wl, ml = l * W_LAYER, l * M_LAYER + M_FIRST
                pe.wait_ge(prow_in, l * (16 * N_PROW) + 16 * N_PROW)
                for a, n, col in ((0, P, 0), (1, 88, P_T0), (2, 64, P_PEK)):
                    mm = pe.transpose(ps[:, 6, col:col + n], prow[0:n, a, :], ident[0:n, 0:n])
                mm.then_inc(prow_turned, 1)
                sum_squares(l * SQ_LAYER + SQ_FIRST)
                pe.wait_ge(modA_read, l + 1)
                apart(pe)

                def project(slot, n, chunk, rope, first, pair, col):
                    pe.wait_ge(pj_copied, l * 16 + chunk * 2 + 1)

                    def rotate(hf):
                        pe.wait_ge(pj_copied, l * 16 + chunk * 2 + (hf + 1 + 3))
                        pe.wait_ge(rope_done, l * 14 + rope * 2 + 1)
                        pe.matmul(ps[:, 4 + hf, :], rope_r, raw[:, slot, hf * HS:hf * HS + HS],
                                  start=True, stop=True).then_inc(rot_done, 1)

                    gemm(slot, n, lambda k: hT[:, k, :], before=first)
                    if rope is not None:
                        rotate(0)
                    mod_pair(pair, col)
                    if rope is not None:
                        rotate(1)

                with pe.Fori(0, 2) as t:
                    for s in range(2):
                        project(s, wl + W_Q + t, t * 2 + s, t * 2 + s,
                                (lambda k: pe.wait_ge(h_ready, l * 16 + (k + 1))) if s == 0 else None,
                                ml + t * 2 + s, t * 4 + (16 + 2 * s))
                for n, rope in enumerate((4, None, 5, 6)):
                    project(n % 2, wl + W_K + n // 2, 4 + n, rope, None, ml + 4 + n, 24 + 2 * n)

                pe.wait_ge(pj_copied, l * 16 + 16 + 3)
                for n in range(8):
                    s, kv = n % 2, n // 4
                    pe.wait_ge(w_in_sem[s], (wl + W_C1 + n // 2 + 1) * 32)
                    if n % 4 == 0:
                        pe.wait_ge(pe_added, l * 2 + kv + 1)
                    for g in range(2):
                        for a in range(8):
                            tok = 8 * (n % 4) + a
                            mm = pe.matmul(ps[:, 2 * kv + g, 0:NCMP], wr[64 * g:64 * g + 64, s, a, :],
                                           kvpe[64 * g:64 * g + 64, 2 * kv + tok // 16,
                                                tok:tok + 16 * (NCMP - 1) + 1:16],
                                           start=(tok == 0), stop=(tok == 31))
                        mm.then_inc((half_done, w_used)[g][s], 1)

                pe.wait_ge(hid_ready, l * 2 + 2)
                pe.wait_ge(wv_in, l * 32 + 32)
                for t in range(NT):
                    if t >= 4:
                        pe.wait_ge(v_copied, l * NT + (t - 3))
                    for k in range(KD):
                        mm = pe.matmul(ps[:, t % 4, 0:NVG], hT[:, k, t * P:t * P + P], wv[:, k, :],
                                       start=(k == 0), stop=(k == KD - 1))
                    mm.then_inc(v_done, 1)

                pe.wait_ge(w2_in, l * 32 + 32)
                pe.wait_ge(rope_done, l * 14 + 14 + 1)
                for kv in range(2):
                    for g in range(2):
                        lhs, rhs = (w2[:, 0, :], hid[:, 0, g, :]) if kv == 0 else (hid[:, 1, g, :], w2[:, 1, :])
                        mm = pe.matmul(ps[64 * g:64 * g + 64, 4 + kv, 0:HD], lhs, rhs, start=True, stop=True)
                mm.then_inc(kvc_done, 1)
                pe.wait_ge(v_copied, l * NT + NT)
                pe.wait_ge(kvc_ready, l + 1)
                apart(pe)

                with pe.Fori(0, 2) as t:
                    def compressed(p):
                        u, step = p // 3, p % 3
                        n = l * NT + t * 4 + u
                        if step == 0:
                            pe.wait_ge(qsc_ready, n + 1)
                            pe.wait_ge(oc_read, n + 1)
                            for cc in range(NC):
                                for g in range(2):
                                    mm = pe.matmul(ps[:, 4 + g, cc * HD:cc * HD + HD],
                                                   qs[64 * g:64 * g + 64, cc, :], kcT[64 * g:64 * g + 64, :],
                                                   start=True, stop=True)
                            mm.then_inc(cs_done, 1)
                        elif step == 1:
                            pe.wait_ge(pc_ready, n + 1)
                            pe.wait_ge(selT_ready, n + 1)
                            for cc in range(NC):
                                mm = pe.transpose(ps[:, 6, cc * P:cc * P + P],
                                                  pc[:, cc, :, :].rearrange("p g n -> p (g n)"), ident)
                            mm.then_inc(pcT_done, 1)
                        else:
                            pe.wait_ge(pcT_ready, n + 1)
                            for cc in range(NC):
                                for g in range(2):
                                    mm = pe.matmul(ps[:, 4 + g, 256 + cc * HD:256 + cc * HD + HD],
                                                   pcT[64 * g:64 * g + 64, cc, :], vcN[64 * g:64 * g + 64, :],
                                                   start=True, stop=True)
                            mm.then_inc(oc_done, 1)
                            pe.wait_ge(sel_ready, n + 1)
                            pe.transpose(ps[:, 6, 0:HD].bitcast(BF16),
                                         selb[:, :, :].rearrange("p g n -> p (g n)"),
                                         identb).then_inc(selT_done, 1)

                    for n in range(6):
                        free, count = ((cv_prod, 1), (cv_out, 1), (cc_copied, 1), (cv_prod, 2),
                                       (cv_out, 2), (cc_copied, 2))[n]
                        pe.wait_ge(free, l * 4 + t * 2 + count)
                        gemm(n % 2, wl + t * 3 + (W_CV + n // 2), lambda k: hT[:, k, :],
                             after=lambda hf, n=n: compressed(2 * n + hf))
                        if n < 4:
                            mod_pair(ml + t * 4 + (8 + n), t * 8 + (32 + 2 * n))
                pe.wait_ge(oc_read, l * NT + NT + 1)
                sum_squares(l * SQ_LAYER + SQ_FIRST + 4)

                pe.wait_ge(cv_out, l * 4 + 4 + 1)
                pe.wait_ge(cv_prod, l * 4 + 4 + 1)
                pe.wait_ge(selT_ready, l * NT + NT + 1)
                pe.wait_ge(modB_read, l + 1)
                pe.wait_ge(ms_ready, l * 3 + 2)
                scores(l, 0, 0, 0)
                scores(l, 0, 0, 1)
                turn(l, 0, 0, 0)

                def steps(i, c, last):
                    for j in range(4):
                        if not (last and j >= 2 and i == NT - 1):
                            scores(l, *((i, c, j + 2) if j < 2 else (i + 1, 0, j - 2) if last else (i, c + 1, j - 2)))
                        weigh(l, i, c, j)
                        if not (last and j == 3 and i == NT - 1):
                            turn(l, *((i, c, j + 1) if j < 3 else (i + 1, 0, 0) if last else (i, c + 1, 0)))

                for i in range(NT):
                    with pe.Fori(0, NC - 1) as cc:
                        steps(i, cc, False)
                    steps(i, NC - 1, True)

                for k in range(4):
                    s = k % 2
                    if k >= 2:
                        pe.wait_ge(attT_ready, l * 4 + (k - 1))
                    for i in range(NT):
                        if k == 0:
                            pe.wait_ge(att_normed, l * NT + (i + 1))
                        mm = pe.transpose(ps[:, 2 * s + i // 4, (i % 4) * P:(i % 4) * P + P],
                                          att[:, i, k * P:k * P + P], ident)
                    mm.then_inc(attT_done, 1)

                pe.wait_ge(attT_ready, l * 4 + 4)
                pe.wait_ge(mixc_ready, l * 4 + 4)
                apart(pe)
                with pe.Fori(0, 4) as t:
                    for s in range(2):
                        pe.wait_ge(wo_added, l * 8 + t * 2 + (s + 1))
                        gemm(s, wl + W_WO + t, lambda k: hT[:, k, :] if k < 4 else mixc[:, k - 4, :])
                sum_squares(l * SQ_LAYER + SQ_FIRST + 12)

                def three(out, w, k, cols, hi, lo, first, last):
                    for m, (a, b) in enumerate(((w_hi, hi), (w_hi, lo), (w_lo, hi))):
                        mm = pe.matmul(out, a[:, w, k:k + P], b[:, cols], start=first and m == 0,
                                       stop=last and m == 2)
                    return mm

                def up(r, t, pair):
                    f0, nf = ROUNDS[r]
                    for s in range(2):
                        pe.wait_ge(w_split[s], l * W_FFN + t + (W_ROUND[r] + 1))
                        pe.wait_ge(u_ready, l * (2 * NF) + t * 2 + (2 * f0 + s + 1))
                        if s == 1 and r > 0:
                            pe.wait_ge(dn_added, l * ADDED + (KD * r + 2))
                        for hf in range(2):
                            cols = slice(hf * HS, hf * HS + HS)
                            for k in range(KD):
                                if s == 0 and hf == 0 and r == 0 and isinstance(t, int):
                                    pe.wait_ge(h_ready, l * 16 + (8 + k + 1))
                                mm = three(ps[:, 2 * s + hf, :], s, k * P, cols, h_hi[:, k, :], h_lo[:, k, :],
                                           k == 0, k == KD - 1)
                            if hf == 1:
                                mm.then_inc(w_used[s], 1)
                            elif s == 0 and pair is not None:
                                mod_pair(ml + 16 + pair, pair * 2)

                def down(r, t, s):
                    f0, nf = ROUNDS[r]
                    first = isinstance(t, int) and t == 0 and s == 0
                    pe.wait_ge(w_split[s], l * W_FFN + t + (W_ROUND[r] + nf + 1))
                    groups = [(k, b) for ks in (range(nf - 1), (nf - 1,)) for b in range(2) for k in ks]
                    for k, b in groups:
                        if k == 0:
                            if first:
                                pe.wait_ge(u_ready, l * (2 * NF) + (2 * (f0 + nf) + b + 1))
                            else:
                                pe.wait_ge(dn_added, l * ADDED + t * 4 + (KD * r + 2 * s + b + 1))
                        if first and k == nf - 1 and b == 0:
                            pe.wait_ge(y_ready, l * NF + (f0 + nf + 1))
                        for hf in range(2):
                            mm = three(ps[:, 2 * b + hf, :], s, (2 * k + b) * P, slice(hf * HS, hf * HS + HS),
                                       y_hi[:, k, :], y_lo[:, k, :], k == 0, k == nf - 1)
                        if k == nf - 1:
                            mm.then_inc((dn_done, w_used[s])[b], 1)

                for r, (f0, nf) in enumerate(ROUNDS):
                    pe.wait_ge(dn_added, l * ADDED + (KD * r + (1 if r else 2)))
                    apart(pe)
                    if r == 0 or r == 2:
                        up(r, 0, 7 if r == 2 else None)
                        with pe.Fori(1, nf) as t:
                            up(r, t, t - 1 if r == 0 else None)
                    else:
                        with pe.Fori(0, nf) as t:
                            up(r, t, t + 3 if r == 1 else None)
                    pe.wait_ge(y_ready, l * NF + (f0 + nf))
                    for t in range(2):
                        for s in range(2):
                            down(r, t, s)

            sum_squares(DEPTH * SQ_LAYER + SQ_FIRST)
            for t in range(NT):
                s = t % 2
                if t >= 2:
                    pe.wait_ge(fin_copied[s], t // 2)
                for k in range(KD):
                    if t == 0:
                        pe.wait_ge(fin_ready, k + 1)
                    mm = pe.transpose(ps[:, 2 * s + k // 4, (k % 4) * P:(k % 4) * P + P],
                                      hT[:, k, t * P:t * P + P], ident)
                mm.then_inc(fin_turned, 1)

        @block.scalar
        def _(act):
            act.sem_inc(x_kept[0], 1)
            act.sem_inc(pj_copied, 3)
            act.sem_inc(p_ready, 2)
            act.sem_inc(pt_ready[1], 1)

            def slot(s):
                return ps[:, 2 * s:2 * s + 2, :].rearrange("p b f -> p (b f)")

            def square(src, s, n, ready=None):
                if ready is not None:
                    act.wait_ge(*ready)
                act.wait_ge(sq_added, n + 1)
                apart(act)
                act.activation(sq[:, s, :], src, ACT.Square).then_inc(sq_ready, 1)

            def root(n):
                act.wait_ge(ms_ready, n + 1)
                act.activation(rt[:, :], rt[:, :], ACT.Sqrt).then_inc(rms_ready, 1)

            def shift(n, mod0, dst, done):
                for k in range(KD):
                    act.wait_ge(xn_ready, n + (k + 1))
                    act.activation(dst[:, k, :], hT[:, k, :], ACT.Identity,
                                   bias=mod[:, mod0 + k:mod0 + k + 1]).then_inc(done, 1)

            act.wait_ge(cst_ready, 1)
            act.activation(cact[:, 0, :], cst[:, 0:8], ACT.Exp, scale=-1.0).then_inc(c_exp, 1)
            with act.Fori(0, 4) as t:
                act.wait_ge(x_turned, t * 2 + 1)
                act.activation(xT[:, :, bass.ds(t * 2 * P, P)],
                               slot(0).rearrange("p (k f) -> p k f", f=P), ACT.Copy).then_inc(x_kept[0], 1)
            act.wait_ge(angle_ready, 2)
            act.activation(sinT, sinT, ACT.Sin).then_inc(trig_ready, 1)
            act.activation(cosT, cosT, ACT.Sin).then_inc(trig_ready, 1)
            act.wait_ge(x_kept[1], 5)
            act.wait_ge(x_kept[0], 5)
            for k in range(KD):
                square(xT[:, k, :], k % 2, k)

            def softmax(l, i, c, j):
                g, window = j % 2, j // 2
                nk = len(key_tiles(i, window)) * P
                n = l * JOBS + c * 4 + (16 * i + j)
                act.wait_ge(smax_ready, n + 1)
                if not (isinstance(c, int) and c == 0 and j < 2 and i == 0):
                    act.wait_ge(t_done, l * GROUPS + groups_through(*two_before(i, c, j)) + 1)
                apart(act)
                act.activation(probs[:, g, 0:nk], slot(g)[:, 0:nk], ACT.Exp, bias=smax[:, g, 1:2], scale=SCALE,
                               accum_out=ssum[:, i % 2, window, bass.ds(c + 4 * g, 1)]).then_inc(p_ready, 1)

            def keep_turned(l, i, c, j):
                for group in range(n_groups(i)):
                    r, _ = ring_of(i, j, group)
                    if r == 1:
                        w = (min(4 * group + 4, len(key_tiles(i, j // 2))) - 4 * group) * P
                        after = groups_through(i, c, j) - n_groups(i) + group + 1
                        act.wait_ge(t_done, l * GROUPS + after + 1)
                        act.wait_ge(pv_done, l * JOBS + c * 4 + (16 * i + j + 1))
                        act.activation(probsT[:, 1, 0:w], ps[:, 5, 0:w], ACT.Copy).then_inc(pt_ready[1], 1)

            with act.Fori(0, DEPTH) as l:
                wl, sl = l * W_LAYER, l * SQ_LAYER + SQ_FIRST
                root(l * 3)
                shift(l * 16, 0, hT, h_ready)

                def copy_chunk(s, n, chunk, dst, rope):
                    for hf in range(2):
                        if hf == 0:
                            act.wait_ge(half_done[s], l * W_FF + n + 1)
                        else:
                            act.wait_ge(w_used[s], wl + n + 2)
                        if rope is not None and hf == 0:
                            act.wait_ge(rope_done, l * 14 + rope * 2 + 1)
                        act.activation(dst[:, hf * HS:hf * HS + HS], ps[:, 2 * s + hf, :],
                                       ACT.Copy).then_inc(pj_copied, 1)

                with act.Fori(0, 2) as t:
                    for s in range(2):
                        copy_chunk(s, t + W_Q, t * 2 + s, raw[:, s, :], t * 2 + s - 1 if s else t * 2)
                for n, rope in enumerate((4, None, 5, 6)):
                    copy_chunk(n % 2, W_K + n // 2, 4 + n, vcT if n == 1 else raw[:, n % 2, :], rope)

                for kv in range(2):
                    act.wait_ge(w_used[1], wl + W_C1 + 2 * kv + 2 + 1)
                    act.activation(hidt[:, :, 0:NCMP], ps[:, 2 * kv:2 * kv + 2, 0:NCMP], ACT.Exp,
                                   scale=-1.0).then_inc(hid_exp, 1)
                    act.wait_ge(hid_ready, l * 2 + kv + 1)
                for t in range(NT):
                    act.wait_ge(v_done, l * NT + (t + 1))
                    act.activation(gate[:, t, :], ps[:, t % 4, GATE:NVG], ACT.Exp, scale=-1.0).then_inc(gate_exp, 1)
                    act.activation(vals[:, t, :], ps[:, t % 4, 0:GATE], ACT.Copy).then_inc(v_copied, 1)

                with act.Fori(0, 2) as t:
                    for p in range(12):
                        n, m = p // 2, p // 2 // 3
                        mm = l * 4 + t * 2 + m
                        if p % 2:
                            if n % 3 == 0:
                                act.wait_ge(w_used[n % 2], wl + t * 3 + (W_CV + n // 2 + 2))
                                act.wait_ge(cv_prod, mm + 1)
                                act.activation(cc_s, slot(n % 2), ACT.Copy).then_inc(cc_copied, 1)
                            elif n % 3 == 1:
                                act.wait_ge(cv_prod, mm + 2)
                                apart(act)
                                act.activation(mixc[:, bass.ds(t * 2 + m, 1), :].rearrange("p a f -> p (a f)"),
                                               cprod, ACT.Identity,
                                               scale=prm[:, bass.ds(t * 2 + (P_CW + 8 + m), 1)]).then_inc(cv_tap, 1)
                            else:
                                square(mixc[:, bass.ds(t * 2 + m, 1), :].rearrange("p a f -> p (a f)"),
                                       m, sl + t * 2 + m, (cv_out, mm + 2))
                        u = l * NT + t * 4 + p // 3
                        if p % 3 == 0:
                            act.wait_ge(cs_shifted, u + 1)
                            act.activation(pc[:, :, :, :], sc[:, :, :, :], ACT.Exp, scale=SCALE).then_inc(cs_exp, 1)
                        elif p % 3 == 1:
                            act.wait_ge(pcT_done, u + 1)
                            act.activation(pcT[:, :, :].rearrange("p c q -> p (c q)"), ps[:, 6, :],
                                           ACT.Copy).then_inc(pcT_ready, 1)
                root(l * 3 + 1)

                def sum_attention(i):
                    act.wait_ge(att_ready, l * NT + (i + 1))
                    act.activation(raw[:, 1, 0:512], att[:, i, :], ACT.Square,
                                   accum_out=ssq[:, 0, i:i + 1]).then_inc(att_ssq, 1)

                softmax(l, 0, 0, 0)
                keep_turned(l, 0, 0, 0)
                softmax(l, 0, 0, 1)

                def steps(i, c, last):
                    for j in range(4):
                        if not (last and j == 3 and i == NT - 1):
                            keep_turned(l, *((i, c, j + 1) if j < 3 else (i + 1, 0, 0) if last else (i, c + 1, 0)))
                        if not (last and j >= 2 and i == NT - 1):
                            softmax(l, *((i, c, j + 2) if j < 2 else (i + 1, 0, j - 2) if last else (i, c + 1, j - 2)))

                for i in range(NT):
                    with act.Fori(0, NC - 1) as cc:
                        steps(i, cc, False)
                    if i >= 1:
                        sum_attention(i - 1)
                    steps(i, NC - 1, True)
                sum_attention(NT - 1)
                act.wait_ge(att_ms, l + 1)
                act.activation(ssq[:, 1, :], ssq[:, 1, :], ACT.Sqrt).then_inc(att_rms, 1)
                for k in range(4):
                    act.wait_ge(attT_done, l * 4 + (k + 1))
                    act.activation(hT[:, k, :], slot(k % 2), ACT.Identity,
                                   scale=prm[:, P_GA + k:P_GA + k + 1]).then_inc(attT_ready, 1)

                with act.Fori(0, 4) as t:
                    for s in range(2):
                        square(xT[:, bass.ds(t * 2 + s, 1), :].rearrange("p a f -> p (a f)"), s,
                               sl + 4 + t * 2 + s, (wo_added, l * 8 + t * 2 + (s + 3)))
                root(l * 3 + 2)

                def high_weights(s, n, width=S):
                    act.wait_ge(w_in_sem[s], (wl + W_FF + n + 1) * 32)
                    apart(act)
                    act.activation(w_hi[:, s, 0:width], wr[:, s, :, :].rearrange("p k f -> p (k f)")[:, 0:width],
                                   ACT.Copy).then_inc(w_high[s], 1)

                for s in range(2):
                    high_weights(s, 0)
                shift(l * 16 + 8, 24, h_hi, h_high)
                act.wait_ge(sq_added, sl + 12 + 2)
                for r, (f0, nf) in enumerate(ROUNDS):
                    last = r == len(ROUNDS) - 1
                    w0 = W_ROUND[r]

                    def up(t, width):
                        for s in range(2):
                            if s == 0:
                                act.wait_ge(prod_ready, l * NF + t + (f0 + 1))
                            act.wait_ge(w_used[s], wl + t + (W_FF + w0 + 2))
                            apart(act)
                            act.activation(raw[:, s, :], slot(s), ACT.Identity,
                                           scale=prm[:, bass.ds(t + (P_T2 + f0 + NF * s), 1)]).then_inc(u_tap, 1)
                            high_weights(s, t + (w0 + 1), width)
                        act.wait_ge(u_ready, l * (2 * NF) + t * 2 + (2 * f0 + 1 + 2))
                        act.wait_ge(y_ready, l * NF + t + (f0 + 1))
                        apart(act)
                        act.activation(sq[:, 0, :], raw[:, 0, :], ACT.Silu).then_inc(silu_ready, 1)
                        act.wait_ge(prod_ready, l * NF + t + (f0 + 2))
                        apart(act)
                        act.activation(y_hi[:, bass.ds(t, 1), :].rearrange("p a f -> p (a f)"), sq[:, 0, :],
                                       ACT.Copy).then_inc(y_high, 1)

                    with act.Fori(0, nf - 1) as t:
                        up(t, S)
                    up(nf - 1, nf * 2 * P)
                    for t in range(2):
                        for s in range(2):
                            if not (last and t == 1):
                                high_weights(s, w0 + nf + t + 1, S if t else nf * 2 * P)
                            if last:
                                for b in range(2):
                                    m = 4 * t + 2 * s + b
                                    square(xT[:, m, :], b, sl + 12 + m, (dn_added, l * ADDED + (KD * r + m + 3)))

            root(DEPTH * 3)
            for t in range(0, NT, 2):
                act.wait_ge(fin_turned, t + 1)
                if t >= 2:
                    act.wait_ge(out_done[0], 16 * (t // 2))
                act.activation(raw[:, 0, :], slot(0), ACT.Copy).then_inc(fin_copied[0], 1)

        @block.gpsimd
        def _(pool):
            pool.sem_inc(sq_added, 2)
            for b in range(2):
                pool.sem_inc(wm_used[b], 1)
            summed = Chain(pool, mod_part)

            def mod_products(n, halves=(0, 1)):
                if 0 in halves:
                    pool.wait_ge(mod_done, n + 1)
                for b in halves:
                    pool.wait_ge(wm_in[b], n * 16 + 16)
                    apart(pool)
                    w = wm[:, b, :, :]
                    steps = [(w, w, cact[:, 2, 4 * b:4 * b + 4].unsqueeze(2).to_broadcast([P, 4, 2 * P]), ALU.mult),
                             (w[:, 0:2, :], w[:, 0:2, :], w[:, 2:4, :], ALU.add)]
                    if b == 0:
                        steps += [(accm[:, :], w[:, 0, :], w[:, 1, :], ALU.add)]
                    else:
                        steps += [(w[:, 0, :], w[:, 0, :], w[:, 1, :], ALU.add),
                                  (accm[:, :], accm[:, :], w[:, 0, :], ALU.add)]
                    for dst, in0, in1, op in steps[:-1]:
                        summed.inc(pool.tensor_tensor(dst, in0, in1, op))
                        summed.wait()
                    if b == 1:
                        pool.wait_ge(wm_used[0], n + 2)
                    dst, in0, in1, op = steps[-1]
                    ins = pool.tensor_tensor(dst, in0, in1, op)
                    ins.then_inc(wm_used[b], 1)

            def zero(n):
                if n is not None:
                    pool.wait_ge(ss_done, n)
                    apart(pool)
                pool.memset(acc[:, :], 0.0).then_inc(acc_zero, 1)

            def add(s, n, zeros):
                pool.wait_ge(sq_ready, n + 1)
                pool.wait_ge(sq_added, n + 2)
                pool.wait_ge(acc_zero, zeros)
                pool.tensor_tensor(acc[:, :], acc[:, :], sq[:, s, :], ALU.add).then_inc(sq_added, 1)

            zero(None)
            pool.wait_ge(cact_ready, 1)
            with pool.Fori(0, M_FIRST) as t:
                summed.enter(t, 5)
                mod_products(t)
                summed.leave(M_FIRST)
            for k in range(KD):
                add(k % 2, k, 1)
            with pool.Fori(0, DEPTH) as l:
                summed.enter(l, 5 * M_LAYER)
                sl, z, ml = l * SQ_LAYER + SQ_FIRST, l * 3, l * M_LAYER + M_FIRST
                zero(z + 1)
                with pool.Fori(0, 8) as t:
                    summed.enter(t, 5)
                    mod_products(ml + t)
                    summed.leave(8)
                with pool.Fori(0, 2) as t:
                    summed.enter(t, 5 * 4)
                    for p in range(12):
                        if p % 3 == 0:
                            u = t * 4 + p // 3
                            pool.wait_ge(cs_done, l * NT + u + 1)
                            if p == 0:
                                pool.wait_ge(rope_done, l * 14 + 14 + 1)
                            pool.tensor_copy(qs[:, :, :], qT[:, :, bass.ds(u * P, P)]).then_inc(qsc_ready, 1)
                        if p in (5, 11):
                            add(p // 6, sl + t * 2 + p // 6, z + 2)
                        if p in (0, 3, 6, 9):
                            mod_products(ml + t * 4 + (8 + p // 3))
                    summed.leave(2)
                pool.wait_ge(cs_done, l * NT + NT + 1)
                apart(pool)
                with pool.Fori(0, NT) as i:
                    with pool.Fori(0, NC) as cc:
                        pool.wait_ge(s_done, l * JOBS + i * 16 + cc * 4 + 1)
                        pool.tensor_copy(qs[:, 0, :], qT[:, bass.ds(cc, 1), bass.ds(i * P, P)].rearrange(
                            "p a f -> p (a f)")).then_inc(qs_ready, 1)
                zero(z + 2)
                with pool.Fori(0, 4) as t:
                    for s in range(2):
                        add(s, sl + 4 + t * 2 + s, z + 3)
                zero(z + 3)
                def low(out, whole, high, ready, count, done):
                    pool.wait_ge(ready, count)
                    apart(pool)
                    pool.tensor_tensor(out, whole, high, ALU.subtract).then_inc(done, 1)

                def low_weights(s, n, width=S):
                    low(w_lo[:, s, 0:width], wr[:, s, :, :].rearrange("p k f -> p (k f)")[:, 0:width],
                        w_hi[:, s, 0:width],
                        w_high[s], l * W_FFN + n + 1, w_split[s])

                for s in range(2):
                    low_weights(s, 0)
                for r, (f0, nf) in enumerate(ROUNDS):
                    last = r == len(ROUNDS) - 1

                    def up(t, width):
                        for s in range(2):
                            if r < 2:
                                mod_products(ml + 16 + 4 * r + t, (s,))
                            low_weights(s, t + (W_ROUND[r] + 1), width)
                        low(y_lo[:, bass.ds(t, 1), :].rearrange("p a f -> p (a f)"), sq[:, 0, :],
                            y_hi[:, bass.ds(t, 1), :].rearrange("p a f -> p (a f)"),
                            y_high, l * NF + t + (f0 + 1), y_ready)

                    with pool.Fori(0, nf - 1) as t:
                        summed.enter(t, 5 if r < 2 else 0)
                        up(t, S)
                        summed.leave(nf - 1)
                    up(nf - 1, nf * 2 * P)
                    for t in range(2):
                        for s in range(2):
                            if not (last and t == 1):
                                low_weights(s, W_ROUND[r] + nf + t + 1, S if t else nf * 2 * P)
                            if last:
                                for b in range(2):
                                    add(b, sl + 12 + 4 * t + 2 * s + b, z + 4)
                summed.leave(DEPTH)

        @block.vector
        def _(dve):
            dve.sem_inc(x_kept[1], 1)
            dve.sem_inc(rope_done, 1)
            dve.sem_inc(cv_prod, 1)
            dve.sem_inc(cv_out, 1)
            dve.sem_inc(oc_read, 1)
            dve.sem_inc(selT_ready, 1)
            dve.sem_inc(pt_ready[0], 1)
            dve.sem_inc(o_read, 1)
            dve.sem_inc(s_done, 1)
            dve.sem_inc(wo_added, 2)
            dve.sem_inc(u_ready, 2)
            dve.sem_inc(y_ready, 1)
            dve.sem_inc(prod_ready, 1)
            dve.sem_inc(dn_added, 2)
            v = Chain(dve, vec)

            def own(ins):
                v.inc(ins)
                v.wait()

            def slot(s):
                return ps[:, 2 * s:2 * s + 2, :].rearrange("p b f -> p (b f)")

            def at(t3, k):
                return t3[:, bass.ds(k, 1), :].rearrange("p a f -> p (a f)")

            def inverse_rms(n, count):
                dve.wait_ge(ss_done, n + 1)
                dve.tensor_scalar(rt[:, :], ps[:, 4:6, :].rearrange("p b f -> p (b f)"), 1.0 / count, EPS,
                                  ALU.mult, ALU.add).then_inc(ms_ready, 1)
                dve.wait_ge(rms_ready, n + 1)
                own(dve.reciprocal(rt[:, :], rt[:, :]))

            dve.wait_ge(const_in, 64)
            own(dve.tensor_copy(kb[:, :], hT[:, 0:2, :].rearrange("p k f -> p (k f)")[:, 0:k_mask.shape[1]]))
            own(dve.memset(hid[:, :, :, :], 0.0))
            own(dve.memset(selb[:, :, :], 0.0))
            dve.wait_ge(cst_turned, 1)
            dve.tensor_copy(cst[:, :], ps[:, 6, 0:16]).then_inc(cst_ready, 1)
            dve.wait_ge(c_exp, 1)
            own(dve.tensor_scalar(cact[:, 1, :], cact[:, 0, :], 1.0, None, ALU.add))
            own(dve.reciprocal(cact[:, 0, :], cact[:, 1, :]))
            dve.tensor_tensor(cact[:, 2, :], cst[:, 0:8], cact[:, 0, :], ALU.mult).then_inc(cact_ready, 1)
            with dve.Fori(0, 4) as t:
                dve.wait_ge(x_turned, t * 2 + 2)
                dve.tensor_copy(xT[:, :, bass.ds((t * 2 + 1) * P, P)],
                                slot(1).rearrange("p (k f) -> p k f", f=P)).then_inc(x_kept[1], 1)
            dve.wait_ge(pos_in, 16)
            own(dve.tensor_scalar(sinT, sq[:, 0, :].bitcast(I32), freq, None, ALU.mult))
            own(dve.tensor_scalar(rt[:, :], sinT, 1.0 / TWO_PI, ROUND, ALU.mult, ALU.add))
            own(dve.tensor_scalar(rt[:, :], rt[:, :], -ROUND, None, ALU.add))
            for part in TWO_PI_PARTS:
                own(dve.scalar_tensor_tensor(out=sinT, in0=rt[:, :], scalar=-part, in1=sinT,
                                             op0=ALU.mult, op1=ALU.add))
            dve.tensor_scalar(sinT, sinT, PI_BELOW, -PI_BELOW, ALU.min, ALU.max).then_inc(angle_ready, 1)
            dve.wait_ge(angle_ready, 1)
            own(dve.tensor_scalar(rt[:, :], sinT, -1.0, None, ALU.mult))
            own(dve.tensor_tensor(rt[:, :], rt[:, :], sinT, ALU.max))
            dve.tensor_scalar(cosT, rt[:, :], -1.0, TWO_PI / 4, ALU.mult, ALU.add).then_inc(angle_ready, 1)
            dve.wait_ge(trig_ready, 2)

            def row_max(l, i, c, j):
                g = j % 2
                nk = len(key_tiles(i, j // 2)) * P
                dve.wait_ge(s_done, l * JOBS + c * 4 + (16 * i + j + 2))
                own(dve.tensor_reduce(smax[:, g, 0:1], slot(g)[:, 0:nk], AX, ALU.max))
                dve.tensor_scalar(smax[:, g, 1:2], smax[:, g, 0:1], -SCALE, None, ALU.mult).then_inc(smax_ready, 1)

            def keep_turned(l, i, c, j):
                for group in range(n_groups(i)):
                    r, _ = ring_of(i, j, group)
                    if r == 0:
                        w = (min(4 * group + 4, len(key_tiles(i, j // 2))) - 4 * group) * P
                        after = groups_through(i, c, j) - n_groups(i) + group + 1
                        dve.wait_ge(t_done, l * GROUPS + after + 1)
                        dve.wait_ge(pv_done, l * JOBS + c * 4 + (16 * i + j + 1))
                        dve.tensor_copy(probsT[:, 0, 0:w], ps[:, 4, 0:w]).then_inc(pt_ready[0], 1)

            def heads(a):
                return a.rearrange("p (h d) -> p h d", d=HD)

            def gates(i, branch):
                return gate[:, i, branch:3 * NH:3]

            def finish_tile(l, i):
                b = i % 2
                dve.wait_ge(pv_done, l * JOBS + (16 * i + 16 + 1))
                own(dve.tensor_scalar(fac[:, 0, :, :], ssum[:, b, :, :], 1e-30, None, ALU.max))
                own(dve.reciprocal(fac[:, 1, :, :], fac[:, 0, :, :]))
                for br in range(2):
                    own(dve.tensor_tensor(fac[:, 2, br, :], fac[:, 1, br, :], gates(i, 1 + br), ALU.mult))
                for br in range(2):
                    ins = dve.tensor_tensor(heads(o_t[:, br, :]), heads(ps[:, 6 + br, :]),
                                            fac[:, 2, br, :].unsqueeze(2).to_broadcast([P, NH, HD]), ALU.mult)
                    if br == 0:
                        own(ins)
                ins.then_inc(o_read, 1)
                own(dve.tensor_tensor(att[:, i, :], att[:, i, :], o_t[:, 0, :], ALU.add))
                dve.wait_ge(o_read, l * NT + (i + 2))
                dve.tensor_tensor(att[:, i, :], att[:, i, :], o_t[:, 1, :], ALU.add).then_inc(att_ready, 1)

            with dve.Fori(0, DEPTH) as l:
                v.enter(l, VEC_LAYER)
                wl, ml = l * W_LAYER, l * M_LAYER + M_FIRST
                dve.wait_ge(prow_turned, l + 2)
                own(dve.tensor_copy(prm[:, :], ps[:, 6, 0:NPRM]))
                dve.wait_ge(mod_done, ml + 1)
                dve.tensor_tensor(mod[:, 0:16], ps[:, 7, 0:16], prm[:, 0:16], ALU.add).then_inc(modA_read, 1)
                dve.wait_ge(modA_read, l + 1)
                own(dve.scalar_tensor_tensor(out=gsc[:, 0, :], in0=mod[:, 8:16], scalar=1.0,
                                             in1=prm[:, P_N1:P_N1 + 8], op0=ALU.add, op1=ALU.mult))
                inverse_rms(l * 3, D)
                for k in range(KD):
                    dve.scalar_tensor_tensor(out=hT[:, k, :], in0=xT[:, k, :], scalar=gsc[:, 0, k:k + 1],
                                             in1=rt[:, :], op0=ALU.mult, op1=ALU.mult).then_inc(xn_ready, 1)

                def rotary(s, chunk, rope, dst):
                    for hf in range(2):
                        h0, h1 = hf * HS, hf * HS + HS
                        dve.wait_ge(pj_copied, l * 16 + chunk * 2 + (hf + 1 + 3))
                        own(dve.tensor_tensor(dst[:, h0:h1], raw[:, s, h0:h1], cosT[:, h0:h1], ALU.mult))
                        dve.wait_ge(rot_done, l * 14 + rope * 2 + (hf + 1))
                        own(dve.tensor_tensor(sq[:, s, h0:h1], ps[:, 4 + hf, :], sinT[:, h0:h1], ALU.mult))
                        dve.tensor_tensor(dst[:, h0:h1], dst[:, h0:h1], sq[:, s, h0:h1],
                                          ALU.add).then_inc(rope_done, 1)

                with dve.Fori(0, 2) as t:
                    v.enter(t, 8)
                    for s in range(2):
                        rotary(s, t * 2 + s, t * 2 + s, at(qT, t * 2 + s))
                    v.leave(2)

                def add_positions(src, a, prm0):
                    for b in range(2):
                        ins = dve.tensor_tensor(
                            kvpe[:, a + b, :].rearrange("p (n t) -> p n t", t=16),
                            src.rearrange("p (n t) -> p n t", t=16),
                            prm[:, prm0 + 16 * b:prm0 + 16 * b + 16].unsqueeze(1).to_broadcast([P, 64, 16]),
                            ALU.add)
                        if b == 0:
                            own(ins)
                    ins.then_inc(pe_added, 1)

                rotary(0, 4, 4, kT[:, 2, :])
                dve.wait_ge(rope_done, l * 14 + 10 + 1)
                add_positions(kT[:, 2, :], 0, P_PEK)
                dve.wait_ge(pj_copied, l * 16 + 12 + 3)
                add_positions(vcT, 2, P_PEV)
                rotary(0, 6, 5, kT[:, 0, :])
                rotary(1, 7, 6, kT[:, 1, :])

                for kv in range(2):
                    dve.wait_ge(hid_exp, l * 2 + kv + 1)
                    own(dve.tensor_scalar(hidt[:, :, 0:NCMP], hidt[:, :, 0:NCMP], 1.0, None, ALU.add))
                    own(dve.reciprocal(hidt[:, :, 0:NCMP], hidt[:, :, 0:NCMP]))
                    dve.tensor_tensor(hid[:, kv, :, 0:NCMP], ps[:, 2 * kv:2 * kv + 2, 0:NCMP],
                                      hidt[:, :, 0:NCMP], ALU.mult).then_inc(hid_ready, 1)
                dve.wait_ge(gate_exp, l * NT + NT)
                own(dve.tensor_scalar(gate[:, :, :], gate[:, :, :], 1.0, None, ALU.add))
                own(dve.reciprocal(gate[:, :, :], gate[:, :, :]))
                dve.wait_ge(kvc_done, l + 1)
                own(dve.tensor_copy(kcT[:, :], ps[:, 4, 0:HD]))
                dve.tensor_copy(vcN[:, :], ps[:, 5, 0:HD]).then_inc(kvc_ready, 1)

                with dve.Fori(0, 2) as t:
                    v.enter(t, VEC_CONV)

                    def conv(n):
                        m = n // 3
                        mm = l * 4 + t * 2 + m
                        dst = at(mixc, t * 2 + m)
                        if n % 3 == 1:
                            dve.wait_ge(cc_copied, mm + 1)
                            dve.wait_ge(w_used[n % 2], wl + t * 3 + (W_CV + n // 2 + 2))
                            dve.tensor_tensor(cprod, slot(n % 2), cc_s, ALU.mult).then_inc(cv_prod, 1)
                            dve.wait_ge(cv_tap, mm + 1)
                            for back, tap in ((1, 1), (2, 0)):
                                own(dve.scalar_tensor_tensor(
                                    out=dst[:, back:S], in0=cprod[:, 0:S - back],
                                    scalar=prm[:, bass.ds(t * 2 + (P_CW + 4 * tap + m), 1)],
                                    in1=dst[:, back:S], op0=ALU.mult, op1=ALU.add))
                        elif n % 3 == 2:
                            dve.wait_ge(w_used[n % 2], wl + t * 3 + (W_CV + n // 2 + 2))
                            dve.tensor_tensor(dst, slot(n % 2), dst, ALU.mult).then_inc(cv_out, 1)

                    def bcast(a, n):
                        return a.unsqueeze(2).to_broadcast([P, NH, n])

                    def compressed_softmax(u):
                        n = l * NT + u
                        flat = lambda a: a.rearrange("p c g n -> p (c g) n")
                        dve.wait_ge(cs_done, n + 2)
                        for g in range(2):
                            own(dve.tensor_tensor(
                                sc[:, :, g, :], ps[:, 4 + g, 0:256].rearrange("p (c n) -> p c n", n=HD),
                                cmask[:, bass.ds(u, 1), :].to_broadcast([P, NC, HD]), ALU.add))
                        own(dve.tensor_reduce(cm[:, 0, :], flat(sc[:, :, :, :]), AX, ALU.max))
                        own(dve.tensor_scalar(cm[:, 1, :], cm[:, 0, :], BIG / 10, None, ALU.max))
                        dve.tensor_tensor(flat(sc[:, :, :, :]), flat(sc[:, :, :, :]), bcast(cm[:, 1, :], HD),
                                          ALU.subtract).then_inc(cs_shifted, 1)
                        dve.wait_ge(cs_exp, n + 1)
                        own(dve.tensor_reduce(cm[:, 0, :], flat(pc[:, :, :, :]), AX, ALU.add))
                        own(dve.tensor_scalar(cm[:, 1, :], cm[:, 0, :], 1e-30, None, ALU.max))
                        own(dve.reciprocal(cm[:, 2, :], cm[:, 1, :]))
                        dve.tensor_tensor(flat(pc[:, :, :, :]), flat(pc[:, :, :, :]), bcast(cm[:, 2, :], HD),
                                          ALU.mult).then_inc(pc_ready, 1)

                    def select_blocks(u):
                        n = l * NT + u
                        dve.wait_ge(pc_ready, n + 1)
                        own(dve.tensor_reduce(pg[:, :, :].rearrange("p g n -> p (g n)"),
                                              pc[:, :, :, :].rearrange("p c g n -> p (g n) c"), AX, ALU.add))
                        own(dve.tensor_reduce(imp[:, 0, :, :].rearrange("p g j -> p (g j)"),
                                              pg[:, :, :].rearrange("p g (j a) -> p (g j) a", a=4), AX, ALU.add))
                        own(dve.tensor_tensor(imp[:, 0, :, 1:NBLK], imp[:, 0, :, 1:NBLK],
                                              pg[:, :, 3:60:4], ALU.add))
                        for a, op in ((0, ALU.mult), (1, ALU.add)):
                            own(dve.tensor_tensor(imp[:, 0, :, :], imp[:, 0, :, :],
                                                  keep[:, bass.ds(u, 1), a, :].to_broadcast([P, 2, NBLK]), op))
                        for g in range(2):
                            me = imp[:, 0, g, :].unsqueeze(2).to_broadcast([P, NBLK, NBLK])
                            other = imp[:, 0, g, :].unsqueeze(1).to_broadcast([P, NBLK, NBLK])
                            own(dve.tensor_tensor(cmpa[:, g, :, :], other, me, ALU.is_gt))
                            own(dve.tensor_tensor(cmpb[:, g, :, :], other, me, ALU.is_equal))
                            own(dve.tensor_tensor(cmpb[:, g, :, :], cmpb[:, g, :, :], ltm, ALU.mult))
                        own(dve.tensor_tensor(raw[:, 0, 0:512], raw[:, 0, 0:512], raw[:, 0, 512:1024], ALU.add))
                        own(dve.tensor_reduce(rank[:, :, :].rearrange("p g j -> p (g j)"),
                                              cmpa.rearrange("p g j i -> p (g j) i"), AX, ALU.add))
                        dve.tensor_scalar(selb[:, :, 0:NBLK], rank[:, :, :], NSEL - 0.5, BIG,
                                          ALU.is_ge, ALU.mult).then_inc(sel_ready, 1)

                    def compressed_output(u):
                        n = l * NT + u
                        dve.wait_ge(oc_done, n + 1)
                        for g in range(2):
                            gated = gate[:, bass.ds(u, 1), 12 * g:12 * g + 10:3].rearrange(
                                "p a h -> p (a h)").unsqueeze(2).to_broadcast([P, NC, HD])
                            ins = dve.tensor_tensor(
                                at(att, u)[:, 256 * g:256 * g + 256].rearrange("p (h d) -> p h d", d=HD),
                                ps[:, 4 + g, 256:512].rearrange("p (h d) -> p h d", d=HD), gated, ALU.mult)
                            if g == 0:
                                own(ins)
                        ins.then_inc(oc_read, 1)
                        dve.wait_ge(selT_done, n + 1)
                        dve.tensor_copy(at(selbT, u), ps[:, 6, 0:HD].bitcast(BF16)).then_inc(selT_ready, 1)

                    for p in range(12):
                        if p % 2:
                            conv(p // 2)
                        u = t * 4 + p // 3
                        if p % 3 == 0:
                            compressed_softmax(u)
                            select_blocks(u)
                        elif p % 3 == 2:
                            compressed_output(u)
                    v.leave(2)

                inverse_rms(l * 3 + 1, 512)
                for k in range(4):
                    dve.scalar_tensor_tensor(out=mixc[:, k, :], in0=mixc[:, k, :],
                                             scalar=prm[:, P_GC + k:P_GC + k + 1], in1=rt[:, :],
                                             op0=ALU.mult, op1=ALU.mult).then_inc(mixc_ready, 1)
                dve.wait_ge(mod_done, ml + 16 + 1)
                dve.tensor_tensor(mod[:, 16:48], ps[:, 7, 16:48], prm[:, 16:48], ALU.add).then_inc(modB_read, 1)
                dve.wait_ge(modB_read, l + 1)
                own(dve.scalar_tensor_tensor(out=gsc[:, 1, :], in0=mod[:, 32:40], scalar=1.0,
                                             in1=prm[:, P_N2:P_N2 + 8], op0=ALU.add, op1=ALU.mult))

                row_max(l, 0, 0, 0)
                row_max(l, 0, 0, 1)
                keep_turned(l, 0, 0, 0)

                def steps(i, c, last):
                    for j in range(4):
                        if not (last and j >= 2 and i == NT - 1):
                            row_max(l, *((i, c, j + 2) if j < 2 else (i + 1, 0, j - 2) if last else (i, c + 1, j - 2)))
                        if not (last and j == 3 and i == NT - 1):
                            keep_turned(l, *((i, c, j + 1) if j < 3 else (i + 1, 0, 0) if last else (i, c + 1, 0)))

                for i in range(NT):
                    with dve.Fori(0, NC - 1) as cc:
                        v.enter(cc, 4)
                        steps(i, cc, False)
                        v.leave(NC - 1)
                    steps(i, NC - 1, True)
                    finish_tile(l, i)
                dve.wait_ge(att_ssq, l * NT + NT)
                dve.tensor_scalar(ssq[:, 1, :], ssq[:, 0, :], 1.0 / 512, EPS, ALU.mult, ALU.add).then_inc(att_ms, 1)
                dve.wait_ge(att_rms, l + 1)
                own(dve.reciprocal(ssq[:, 0, :], ssq[:, 1, :]))
                for i in range(NT):
                    dve.tensor_scalar(att[:, i, :], att[:, i, :], ssq[:, 0, i:i + 1], None,
                                      ALU.mult).then_inc(att_normed, 1)

                with dve.Fori(0, 4) as t:
                    for s in range(2):
                        dve.wait_ge(w_used[s], wl + W_WO + t + 2)
                        xd = at(xT, t * 2 + s)
                        dve.scalar_tensor_tensor(out=xd, in0=slot(s), scalar=mod[:, bass.ds(t * 2 + (16 + s), 1)],
                                                 in1=xd, op0=ALU.mult, op1=ALU.add).then_inc(wo_added, 1)
                inverse_rms(l * 3 + 2, D)

                def low_input(k):
                    dve.wait_ge(h_high, l * KD + k + 1)
                    dve.wait_ge(xn_ready, l * 16 + (8 + k + 1))
                    dve.scalar_tensor_tensor(out=h_lo[:, k, :], in0=hT[:, k, :], scalar=mod[:, 24 + k:25 + k],
                                             in1=h_hi[:, k, :], op0=ALU.add, op1=ALU.subtract).then_inc(h_ready, 1)

                for k in range(KD):
                    dve.scalar_tensor_tensor(out=hT[:, k, :], in0=xT[:, k, :], scalar=gsc[:, 1, k:k + 1],
                                             in1=rt[:, :], op0=ALU.mult, op1=ALU.mult).then_inc(xn_ready, 1)
                    if k:
                        low_input(k - 1)
                low_input(KD - 1)

                for r, (f0, nf) in enumerate(ROUNDS):
                    with dve.Fori(0, nf) as t:
                        v.enter(t, 2)
                        for s in range(2):
                            dve.wait_ge(u_tap, l * (2 * NF) + t * 2 + (2 * f0 + s + 1))
                            for back, tap0 in ((1, P_T1), (2, P_T0)):
                                ins = dve.scalar_tensor_tensor(
                                    out=raw[:, s, back:S], in0=slot(s)[:, 0:S - back],
                                    scalar=prm[:, bass.ds(t + (tap0 + f0 + NF * s), 1)],
                                    in1=raw[:, s, back:S], op0=ALU.mult, op1=ALU.add)
                                if back == 1:
                                    own(ins)
                            ins.then_inc(u_ready, 1)
                        dve.wait_ge(silu_ready, l * NF + t + (f0 + 1))
                        dve.wait_ge(u_ready, l * (2 * NF) + t * 2 + (2 * f0 + 2 + 2))
                        dve.tensor_tensor(sq[:, 0, :], sq[:, 0, :], raw[:, 1, :], ALU.mult).then_inc(prod_ready, 1)
                        v.leave(nf)
                    with dve.Fori(0, 2) as t:
                        for s in range(2):
                            for b in range(2):
                                if b == 0:
                                    dve.wait_ge(dn_done, l * (ADDED // 2) + t * 2 + (KD // 2 * r + s + 1))
                                else:
                                    dve.wait_ge(w_used[s], wl + t + (W_FF + W_ROUND[r] + nf + 2))
                                dve.wait_ge(dn_added, l * ADDED + (KD * r + 2))
                                xd = at(xT, t * 4 + (2 * s + b))
                                dve.scalar_tensor_tensor(out=xd, in0=slot(b),
                                                         scalar=mod[:, bass.ds(t * 4 + (40 + 2 * s + b), 1)],
                                                         in1=xd, op0=ALU.mult, op1=ALU.add).then_inc(dn_added, 1)
                v.leave(DEPTH)

            inverse_rms(DEPTH * 3, D)
            for k in range(KD):
                dve.scalar_tensor_tensor(out=hT[:, k, :], in0=xT[:, k, :], scalar=cst[:, 8 + k:9 + k],
                                         in1=rt[:, :], op0=ALU.mult, op1=ALU.mult).then_inc(fin_ready, 1)
            for t in range(1, NT, 2):
                dve.wait_ge(fin_turned, t + 1)
                if t >= 2:
                    dve.wait_ge(out_done[1], 16 * (t // 2))
                dve.tensor_copy(raw[:, 1, :], slot(1)).then_inc(fin_copied[1], 1)


def shape_constants():
    import numpy as np
    f32 = np.float32
    q, n = np.arange(P), np.arange(P)
    ident = np.eye(P, dtype=f32)
    rope = np.zeros((P, P), f32)
    for h in range(2):
        for d in range(8):
            rope[64 * h + d + 8, 64 * h + d] = -1.0
            rope[64 * h + d, 64 * h + d + 8] = 1.0
    freq = np.zeros((P, 1), f32)
    for h in range(2):
        for d in range(16):
            freq[64 * h + d, 0] = f32(500000.0) ** f32(-(d % 8) / 8)
    tok = np.arange(NT)[:, None] * P + q[None, :]
    cmask = np.where((np.arange(HD)[None, None, :] * 16 + 31 <= tok[:, :, None])
                     & (np.arange(HD) < NCMP)[None, None, :], 0.0, BIG).astype(f32)
    b, j = (tok // HD)[:, :, None], np.arange(NBLK)[None, None, :]
    causal = j <= b
    forced = causal & ((j == 0) | (j == b) | (j == b - 1))
    keep = np.stack([np.where(causal & ~forced, 1.0, 0.0),
                     np.where(forced, -BIG, np.where(causal, 0.0, BIG))], 2).astype(f32)
    lt = np.broadcast_to((np.arange(NBLK)[None, :] < np.arange(NBLK)[:, None]).astype(f32)[None],
                         (P, NBLK, NBLK))
    k_f32 = np.concatenate([ident, rope, np.ones((P, P), f32), freq,
                            cmask.transpose(1, 0, 2).reshape(P, -1), keep.transpose(1, 0, 2, 3).reshape(P, -1),
                            lt.reshape(P, -1)], axis=1)
    blk = np.zeros((P, S), f32)
    for h in range(2):
        for j in range(NBLK):
            blk[64 * h + j, HD * j:HD * j + HD] = 1.0
    diag = np.where(n[None, :] > q[:, None], BIG, 0.0)
    tail = np.where(n[None, :] <= q[:, None], BIG, 0.0)
    k_mask = np.concatenate([ident, diag, tail, blk], axis=1).astype(f32)
    return np.ascontiguousarray(k_f32), np.ascontiguousarray(k_mask)


_INS = ["x", "c", "positions", "w_mod", "b_mod", "norm1_g", "w_in", "cmp_pe_k", "cmp_w1_k", "cmp_w2_k",
        "cmp_pe_v", "cmp_w1_v", "cmp_w2_v", "conv_w", "grp_g_attn", "grp_g_conv", "w_out", "norm2_g",
        "ffn_up", "ffn_conv", "ffn_down", "final_g"]


def kernel(**inputs):
    import numpy as np
    import concourse.bacc as bacc
    from concourse.bass_utils import run_bass_kernel_spmd

    nc = bacc.Bacc("TRN2", target_bir_lowering=False, num_devices=1)
    arrays, args = {}, []
    named = [(name, np.ascontiguousarray(inputs[name])) for name in _INS]
    named += list(zip(("k_f32", "k_mask"), shape_constants()))
    for name, a in named:
        arrays[f"in_{name}"] = a
        args.append(nc.dram_tensor(f"in_{name}", a.shape, mybir.dt.from_np(a.dtype), kind="ExternalInput").ap())
    args.append(nc.dram_tensor("out_0", (1, S, D), F32, kind="ExternalOutput").ap())
    build(nc, *args)
    return run_bass_kernel_spmd(nc, [arrays], core_ids=[0]).results[0]["out_0"]
```

```python
from contextlib import ExitStack

import concourse.bass as bass
from concourse import mybir

F32 = mybir.dt.float32
F32R = mybir.dt.float32r
BF16 = mybir.dt.bfloat16
I32 = mybir.dt.int32
ALU = mybir.AluOpType
ACT = mybir.ActivationFunctionType
AX = mybir.AxisListType.X

P = 128
D = 1024
KD = D // P
S = 1024
HS = 512
NT = S // P
DEPTH = 2
HD = 64
NH = 8
NKV = 2
NC = NH // NKV
DFF = 2816
NF = DFF // P
ROUNDS = ((0, 4), (4, 4), (8, 4), (12, 4), (16, 3), (19, 3))
NCMP = 63
NBLK = 16
NSEL = 8
EPS = 1e-6
BIG = -1e30
SCALE = HD ** -0.5
ROUND = 1.5 * 2.0 ** 23
TWO_PI = 6.283185307179586
TWO_PI_PARTS = (6.28125, 0.0019350051879882812, 3.0199159819567e-07)
PI_BELOW = 3.1415925
COL_KC, COL_VC, COL_KS, COL_VS, COL_KW, COL_VW, COL_CONV = 512, 640, 768, 896, 1024, 1152, 1304
NVG = 2 * P + 3 * NH
GATE = 2 * P

PB_MOD, P_N1, P_N2, P_GA, P_GC, P_CW, P_T2 = 0, 48, 56, 64, 68, 72, 84
P_T0, P_T1 = 128, 172
P_PEK, P_PEV = 216, 248
NPRM = 280

W_LAYER = 50
W_Q, W_K, W_C1, W_CV, W_WO, W_FF = 0, 2, 4, 6, 12, 16
W_ROUND = tuple(sum(nf + 2 for _, nf in ROUNDS[:r]) for r in range(len(ROUNDS)))
W_FFN = W_LAYER - W_FF
ADDED = KD * len(ROUNDS)
M_LAYER = 24
M_FIRST = 8
JOBS = NT * NC * 4
GROUPS = 192
SQ_FIRST, SQ_LAYER = 8, 20
VEC_CONV = 72
VEC_LAYER = 619


class Chain:

    def __init__(self, eng, sem):
        self.eng, self.sem, self.base, self.k, self.stack = eng, sem, 0, 0, []

    def inc(self, ins):
        ins.then_inc(self.sem, 1)
        self.k += 1

    def wait(self):
        self.eng.wait_ge(self.sem, self.base + self.k)

    def enter(self, iv, per):
        self.stack.append((self.base, self.k, per))
        self.base, self.k = self.base + self.k + iv * per, 0

    def leave(self, n):
        base, k, per = self.stack.pop()
        assert self.k == per, f"{self.sem}: {self.k} increments in a body said to have {per}"
        self.base, self.k = base, k + n * per


def n_groups(i):
    return 1 if i < 4 else 2


def groups_before(i, c, j, back=0):
    n = 16 * i + j - back
    if i >= 4 and not (isinstance(c, int) and n + 4 * c < 64):
        return c * 8 + (2 * n - 64)
    return c * 4 + n


def ahead(i, c, last, j, n):
    if j + n < 4:
        return i, c, j + n
    return (i + 1, 0, j + n - 4) if last else (i, c + 1, j + n - 4)


def ends(i, last, j, n):
    return last and j + n >= 4 and i == NT - 1


def key_tiles(i, window):
    return list(range(max(0, i - 4) if window else 0, i + 1))


def build(nc, x, c, positions, w_mod, b_mod, norm1_g, w_in, cmp_pe_k, cmp_w1_k, cmp_w2_k, cmp_pe_v,
          cmp_w1_v, cmp_w2_v, conv_w, grp_g_attn, grp_g_conv, w_out, norm2_g, ffn_up, ffn_conv,
          ffn_down, final_g, k_f32, k_mask, out):
    with ExitStack() as ctx:
        def sb(name, shape, dt=F32):
            return ctx.enter_context(nc.sbuf_tensor(name, shape, dt))

        def sem(name):
            return ctx.enter_context(nc.semaphore(name))

        ps = ctx.enter_context(nc.psum_tensor("ps", [P, 8, HS], F32))

        xT = sb("xT", [P, KD, S])
        with ExitStack() as over:
            def split(name, shape):
                return over.enter_context(nc.sbuf_tensor(name, shape, F32R))

            h_lo = split("h_lo", [P, KD, S])
            y_hi = split("y_hi", [P, 4, S])
            y_lo = split("y_lo", [P, 4, S])
            h_hi = split("h_hi", [P, KD, S])
            w_hi = split("w_hi", [P, 2, S])
            split("tables", [P, 2, S])
            w_lo = split("w_lo", [P, 2, S])
        hT = sb("hT", [P, KD, S])
        big = sb("big", [P, 20, S])
        qT = big[:, 0:4, :]
        kT = big[:, 4:7, :]
        vcT = big[:, 7, :]
        kvpe = big[:, 8:12, :]
        mixa = big[:, 8:12, :]
        mixc = big[:, 12:16, :]
        cc_s = big[:, 16, :]
        cprod = big[:, 17, :]
        probs = hT[:, 0:4, :]
        probsT = hT[:, 4, :].rearrange("p (r f) -> p r f", r=2)
        wv = big[:, 15:18, :].rearrange("p a f -> p (a f)")[:, 0:KD * NVG].rearrange(
            "p (k f) -> p k f", k=KD)
        vals = big[:, 6:8, :].rearrange("p a (b f) -> p (a b) f", f=2 * P)
        cosT, sinT = big[:, 18, :], big[:, 19, :]
        wr = sb("wr", [P, 2, KD, P])
        gate = sb("gate", [P, NT, 3 * NH])
        wm = sb("wm", [P, 2, KD // 2, 2 * P])
        accm = sb("accm", [P, 2 * P])
        raw = sb("raw", [P, 2, S])
        sq = sb("sq", [P, 2, S])
        acc = sb("acc", [P, S])
        rt = sb("rt", [P, S])
        w1k = [a.rearrange("p (a f) -> p a f", f=P) for a in (big[:, 12, :], big[:, 13, :], big[:, 14, :], rt[:, :])]
        kf = sb("kf", [P, k_f32.shape[1]])
        kb = sb("kb", [P, k_mask.shape[1]], BF16)
        qs = sb("qs", [P, NC, P])
        q_parts = w_hi[:, :, :].rearrange("p b (a c q) -> p b a c q", a=2, q=P)
        k_hi = h_lo[:, 5:7, :]
        k_lo = y_lo[:, 0:2, :]
        prow = sb("prow", [P, 3, P])
        prm = sb("prm", [P, NPRM])
        mod = sb("mod", [P, 48])
        gsc = sb("gsc", [P, 2, KD])
        crow = sb("crow", [16, P])
        cst = sb("cst", [P, 16])
        cact = sb("cact", [P, 3, KD])
        w2 = sb("w2", [P, 2, HD])
        hid = sb("hid", [P, 2, 2, HD])
        hidt = sb("hidt", [P, 2, HD])
        kcT = sb("kcT", [P, HD])
        vcN = sb("vcN", [P, HD])
        sc = raw[:, 1, 0:512].rearrange("p (c g n) -> p c g n", g=2, n=HD)
        pc = raw[:, 1, 512:1024].rearrange("p (c g n) -> p c g n", g=2, n=HD)
        pcT = rt[:, 0:512].rearrange("p (c n) -> p c n", n=P)
        cm = sb("cm", [P, 3, NH])
        pg = sb("pg", [P, 2, HD])
        imp = sb("imp", [P, 2, 2, NBLK])
        cmpa = raw[:, 0, 0:512].rearrange("p (g j i) -> p g j i", g=2, j=NBLK)
        cmpb = raw[:, 0, 512:1024].rearrange("p (g j i) -> p g j i", g=2, j=NBLK)
        rank = sb("rank", [P, 2, NBLK])
        selb = sb("selb", [P, 2, HD], BF16)
        selbT = sb("selbT", [P, NT, P], BF16)
        smax = sb("smax", [P, 2, 2])
        ssum = sb("ssum", [P, 4])
        rsum = sb("rsum", [P, 2, 4])
        rms = sb("rms", [P, 2, NT])

        ident = kf[:, 0:128]
        rope_r = kf[:, 128:256]
        ones = kf[:, 256:384]
        freq = kf[:, 384:385]
        cmask = kf[:, 385:897].rearrange("p (t n) -> p t n", t=NT)
        keep = kf[:, 897:1153].rearrange("p (t a j) -> p t a j", t=NT, a=2)
        ltm = kf[:, 1153:1409].rearrange("p (j i) -> p j i", j=NBLK)
        identb = kb[:, 0:128]
        diagm = kb[:, 128:256]
        tailm = kb[:, 256:384]
        blk = kb[:, 384:384 + S]

        const_in = sem("const_in")
        pos_in = sem("pos_in")
        x_in = [sem(f"x_in{i}") for i in range(2)]
        x_turned = sem("x_turned")
        x_kept = [sem(f"x_kept{i}") for i in range(2)]
        cst_turned = sem("cst_turned")
        c_exp = sem("c_exp")
        cst_ready = sem("cst_ready")
        cact_ready = sem("cact_ready")
        angle_ready = sem("angle_ready")
        trig_ready = sem("trig_ready")
        prow_in = sem("prow_in")
        prow_turned = sem("prow_turned")
        w_in_sem = [sem(f"w_in{i}") for i in range(2)]
        half_done = [sem(f"half_done{i}") for i in range(2)]
        w_used = [sem(f"w_used{i}") for i in range(2)]
        wm_in = [sem(f"wm_in{i}") for i in range(2)]
        wm_used = [sem(f"wm_used{i}") for i in range(2)]
        wv_in = sem("wv_in")
        w2_in = sem("w2_in")
        w1k_in = sem("w1k_in")
        w1k_used = sem("w1k_used")
        mod_done = sem("mod_done")
        modA_read = sem("modA_read")
        modB_read = sem("modB_read")
        acc_zero = sem("acc_zero")
        sq_ready = sem("sq_ready")
        sq_added = sem("sq_added")
        ss_done = sem("ss_done")
        ms_ready = sem("ms_ready")
        rms_ready = sem("rms_ready")
        diag_ready = sem("diag_ready")
        spread_done = sem("spread_done")
        xn_ready = sem("xn_ready")
        h_ready = sem("h_ready")
        pj_copied = sem("pj_copied")
        rot_done = sem("rot_done")
        rope_done = sem("rope_done")
        pe_added = sem("pe_added")
        v_done = sem("v_done")
        v_copied = sem("v_copied")
        gate_exp = sem("gate_exp")
        hid_exp = sem("hid_exp")
        hid_ready = sem("hid_ready")
        kvc_done = sem("kvc_done")
        kvc_ready = sem("kvc_ready")
        cc_copied = sem("cc_copied")
        cv_prod = sem("cv_prod")
        cv_tap = sem("cv_tap")
        cv_out = sem("cv_out")
        qsc_ready = sem("qsc_ready")
        cs_done = sem("cs_done")
        cs_shifted = sem("cs_shifted")
        cs_exp = sem("cs_exp")
        pc_ready = sem("pc_ready")
        pcT_done = sem("pcT_done")
        pcT_ready = sem("pcT_ready")
        oc_done = sem("oc_done")
        oc_read = sem("oc_read")
        sel_ready = sem("sel_ready")
        selT_done = sem("selT_done")
        selT_ready = sem("selT_ready")
        mixc_ready = sem("mixc_ready")
        q_high = sem("q_high")
        qs_ready = sem("qs_ready")
        k_high = sem("k_high")
        k_split = sem("k_split")
        s_done = sem("s_done")
        smax_ready = sem("smax_ready")
        p_ready = sem("p_ready")
        t_done = sem("t_done")
        pt_ready = sem("pt_ready")
        pn_ready = sem("pn_ready")
        pv_done = sem("pv_done")
        o_read = sem("o_read")
        att_sq = sem("att_sq")
        att_part = sem("att_part")
        att_added = sem("att_added")
        mixa_ready = sem("mixa_ready")
        wo_in = [sem(f"wo_in{i}") for i in range(2)]
        wo_added = sem("wo_added")
        u_tap = sem("u_tap")
        u_ready = sem("u_ready")
        silu_ready = sem("silu_ready")
        w_high = [sem(f"w_high{i}") for i in range(2)]
        w_split = [sem(f"w_split{i}") for i in range(2)]
        h_high = sem("h_high")
        prod_ready = sem("prod_ready")
        y_high = sem("y_high")
        dn_done = sem("dn_done")
        y_ready = sem("y_ready")
        dn_added = sem("dn_added")
        fin_ready = sem("fin_ready")
        fin_turned = sem("fin_turned")
        fin_copied = [sem(f"fin_copied{i}") for i in range(2)]
        out_done = [sem(f"out_done{i}") for i in range(2)]
        mod_part = sem("mod_part")
        vec = sem("vec")

        waited = sem("waited")

        N_PROW = 13

        block = ctx.enter_context(nc.Block())

        def apart(eng):
            eng.sem_inc(waited, 1)

        @block.sync
        def _(sp):
            def load_mod(l, m, n):
                for b in range(2):
                    sp.wait_ge(wm_used[b], n + 1)
                    apart(sp)
                    sp.dma_start(wm[:, b, :, :], w_mod[l, b * HS:b * HS + HS, bass.ds(m * P, 2 * P)].rearrange(
                        "(k p) f -> p k f", p=P)).then_inc(wm_in[b], 16)

            def load_w(slot, n, w, l, col, row0=0, nk=KD):
                sp.wait_ge(w_used[slot], n + 1)
                src = w[l, row0:row0 + nk * P, bass.ds(col, P)].rearrange("(k p) f -> p k f", p=P)
                sp.dma_start(wr[:, slot, 0:4, :], src[:, 0:4, :]).then_inc(w_in_sem[slot], 16)
                sp.dma_start(wr[:, slot, 4:nk, :], src[:, 4:nk, :]).then_inc(w_in_sem[slot], 16)

            def load_w1(dst, w, l, n, done):
                for h in range(2):
                    sp.dma_start(dst[64 * h:64 * h + 64, :, :], w[l, n * 512:n * 512 + 512, :].rearrange(
                        "(t d) f -> d t f", d=HD)).then_inc(done, 16)

            sp.dma_start(crow[0:8, :], c.rearrange("o (k f) -> (o k) f", f=P)).then_inc(const_in, 16)
            sp.dma_start(crow[8:16, :], final_g.rearrange("(k f) -> k f", f=P)).then_inc(const_in, 16)
            sp.dma_start(kf[:, :], k_f32).then_inc(const_in, 16)
            sp.dma_start(hT[:, 0:2, :].rearrange("p k f -> p (k f)")[:, 0:k_mask.shape[1]],
                         k_mask).then_inc(const_in, 16)
            sp.dma_start(sq[:, 0, :].bitcast(I32), positions.to_broadcast([P, S])).then_inc(pos_in, 16)
            with sp.Fori(0, 4) as t:
                for s in range(2):
                    sp.wait_ge(x_kept[s], t + 1)
                    sp.dma_start(raw[:, s, :], x[0, bass.ds((t * 2 + s) * P, P), :]).then_inc(x_in[s], 16)
                load_mod(0, t * 2, t)
            with sp.Fori(4, M_FIRST) as t:
                load_mod(0, t * 2, t)

            with sp.Fori(0, DEPTH) as l:
                sp.wait_ge(prow_turned, l + 1)
                rows = [(0, PB_MOD, b_mod[l, :].rearrange("(r f) -> r f", f=P), 48),
                        (0, P_N1, norm1_g[l, :].rearrange("(r f) -> r f", f=P), 8),
                        (0, P_N2, norm2_g[l, :].rearrange("(r f) -> r f", f=P), 8),
                        (0, P_GC, grp_g_conv[l, :].rearrange("(r f) -> r f", f=P), 4),
                        (0, P_CW, conv_w[l, :, :].rearrange("t (r f) -> (t r) f", f=P), 12),
                        (0, P_T2, ffn_conv[l, 2, :].rearrange("(r f) -> r f", f=P), 44),
                        (1, 0, ffn_conv[l, 0:2, :].rearrange("t (r f) -> (t r) f", f=P), 88)]
                for a, r0, src, n in rows:
                    sp.dma_start(prow[r0:r0 + n, a, :], src).then_inc(prow_in, 16)
                for g in range(2):
                    sp.dma_start(prow[P_GA:P_GA + 4, 0, HD * g:HD * g + HD],
                                 grp_g_attn[l, 256 * g:256 * g + 256].rearrange("(r f) -> r f", f=HD)).then_inc(
                                     prow_in, 16)
                for r0, src in ((0, cmp_pe_k), (32, cmp_pe_v)):
                    for h in range(2):
                        sp.dma_start(prow[r0:r0 + 32, 2, 64 * h:64 * h + 64], src[l, :, :]).then_inc(prow_in, 16)
                sp.dma_start(w2[:, 0, :], cmp_w2_k[l, :, :]).then_inc(w2_in, 16)
                sp.dma_start(w2[:, 1, :], cmp_w2_v[l, :, :]).then_inc(w2_in, 16)

                ml, wl = l * M_LAYER + M_FIRST, l * W_LAYER
                with sp.Fori(0, 2) as t:
                    for s in range(2):
                        sp.wait_ge(w_used[s], wl + W_Q + t + 1)
                        for g in range(2):
                            sp.dma_start(wr[:, s, :, 64 * g:64 * g + 64],
                                         w_in[l, :, bass.ds((t * 2 + s) * HD + 256 * g, HD)].rearrange(
                                             "(k p) f -> p k f", p=P)).then_inc(w_in_sem[s], 16)
                        load_mod(l, t * 4 + (16 + 2 * s), ml + t * 2 + s)
                for n in range(4):
                    load_w1(w1k[n], cmp_w1_k, l, n, w1k_in)
                for n, col in enumerate((COL_KC, COL_VC, COL_KS, COL_KW)):
                    load_w(n % 2, wl + W_K + n // 2, w_in, l, col)
                    load_mod(l, 24 + 2 * n, ml + 4 + n)
                sp.dma_start(wv[:, :, 0:P], w_in[l, :, COL_VS:COL_VS + P].rearrange(
                    "(k p) f -> p k f", p=P)).then_inc(wv_in, 16)
                sp.dma_start(wv[:, :, P:NVG], w_in[l, :, COL_VW:COL_VW + NVG - P].rearrange(
                    "(k p) f -> p k f", p=P)).then_inc(wv_in, 16)
                for n in range(4):
                    s = n % 2
                    sp.wait_ge(w_used[s], wl + W_C1 + n // 2 + 1)
                    load_w1(wr[:, s, :, :], cmp_w1_v, l, n, w_in_sem[s])
                with sp.Fori(0, 2) as t:
                    for n in range(6):
                        col = COL_CONV + (512, 1024, 0)[n % 3] + (n // 3) * P
                        load_w(n % 2, wl + t * 3 + (W_CV + n // 2), w_in, l, t * (2 * P) + col)
                        if n < 4:
                            load_mod(l, t * 8 + (32 + 2 * n), ml + t * 4 + (8 + n))
                with sp.Fori(0, 4) as t:
                    for s in range(2):
                        sp.wait_ge(w_used[s], wl + W_WO + t + 1)
                        cols = bass.ds((t * 2 + s) * P, P)
                        sp.dma_start(wr[:, s, 4:KD, :], w_out[l, 512:D, cols].rearrange(
                            "(k p) f -> p k f", p=P)).then_inc(wo_in[s], 16)
                        for g in range(2):
                            sp.dma_start(wr[HD * g:HD * g + HD, s, 0:4, :],
                                         w_out[l, 256 * g:256 * g + 256, cols].rearrange(
                                             "(k p) f -> p k f", p=HD)).then_inc(w_in_sem[s], 16)
                for r, (f0, nf) in enumerate(ROUNDS):
                    w0 = wl + W_FF + W_ROUND[r]
                    with sp.Fori(0, nf) as t:
                        for s in range(2):
                            load_w(s, w0 + t, ffn_up, l, t * P + (f0 * P + s * DFF))
                        if r < 2:
                            load_mod(l * -1 + 1, t * 2 + 8 * r, ml + 16 + 4 * r + t)
                    with sp.Fori(0, 2) as t:
                        for s in range(2):
                            sp.wait_ge(w_used[s], w0 + nf + t + 1)
                            src = ffn_down[l, f0 * P:f0 * P + nf * P, bass.ds((t * 2 + s) * (2 * P), 2 * P)].rearrange(
                                "(k p) f -> p k f", p=P)
                            dst = wr[:, s, :, :].rearrange("p (k b) f -> p k (b f)", b=2)
                            sp.dma_start(dst[:, 0:2, :], src[:, 0:2, :]).then_inc(w_in_sem[s], 16)
                            sp.dma_start(dst[:, 2:nf, :], src[:, 2:nf, :]).then_inc(w_in_sem[s], 16)

            with sp.Fori(0, 4) as t:
                for s in range(2):
                    sp.wait_ge(fin_copied[s], t + 1)
                    sp.dma_start(out[0, bass.ds((t * 2 + s) * P, P), :], raw[:, s, :]).then_inc(out_done[s], 16)
            for s in range(2):
                sp.wait_ge(out_done[s], 16 * 4)

        @block.tensor
        def _(pe):
            for s in range(2):
                pe.sem_inc(w_used[s], 1)
                pe.sem_inc(wm_used[s], 1)
            pe.sem_inc(prow_turned, 1)
            pe.sem_inc(mod_done, 1)
            pe.sem_inc(t_done, 1)
            pe.sem_inc(pv_done, 1)
            pe.sem_inc(cs_done, 1)

            def mod_pair(n, col0):
                pe.wait_ge(wm_used[1], n + 2)
                for s in range(2):
                    mm = pe.matmul(ps[:, 7, bass.ds(col0 + s, 1)], accm[:, s * P:s * P + P], ones[:, 0:1],
                                   start=True, stop=True)
                mm.then_inc(mod_done, 1)

            def gemm(slot, n, rhs, ks=range(KD), before=None, during=None, after=None):
                pe.wait_ge(w_in_sem[slot], (n + 1) * 32)
                for hf in range(2):
                    for k in ks:
                        if before is not None and hf == 0:
                            before(k)
                        if during is not None and k == 4:
                            during(hf)
                        mm = pe.matmul(ps[:, 2 * slot + hf, :], wr[:, slot, k, :],
                                       rhs(k)[:, hf * HS:hf * HS + HS], start=(k == ks[0]), stop=(k == ks[-1]))
                    mm.then_inc((half_done, w_used)[hf][slot], 1)
                    if after is not None:
                        after(hf)

            def sum_squares(n):
                pe.wait_ge(sq_added, n + 2)
                for hf in range(2):
                    mm = pe.matmul(ps[:, 4 + hf, :], ones, acc[:, hf * HS:hf * HS + HS], start=True, stop=True)
                mm.then_inc(ss_done, 1)

            def norm_factors(norm, squares=None):
                if squares is not None:
                    pe.wait_ge(sq_added, squares + 1)
                parts = (acc[:, :],) if squares is None else (acc[:, :], sq[:, 1, :])
                for n, part in enumerate(parts):
                    if n == 1:
                        pe.wait_ge(sq_ready, squares)
                    for t in range(NT):
                        mm = pe.matmul(ps[:, 4, t:t + 1], part[:, t * P:t * P + P], ones[:, 0:1],
                                       start=(n == 0 and t == 0), stop=(n == len(parts) - 1),
                                       skip_group_check=True)
                mm.then_inc(ss_done, 1)
                pe.wait_ge(diag_ready, norm + 1)
                for hf in range(2):
                    mm = pe.matmul(ps[:, 4 + hf, :], ones, rt[:, hf * HS:hf * HS + HS], start=True, stop=True)
                mm.then_inc(spread_done, 1)

            pe.wait_ge(const_in, 64)
            pe.transpose(ps[:, 6, 0:16], crow[:, :], ident[0:16, 0:16]).then_inc(cst_turned, 1)

            def first_pair(n):
                for b in range(2):
                    pe.wait_ge(wm_in[b], n * 16 + 16)
                    for s in range(2):
                        for k in range(KD // 2):
                            mm = pe.matmul(ps[:, 7, bass.ds(n * 2 + s, 1)], wm[:, b, k, s * P:s * P + P],
                                           cact[:, 2, 4 * b + k:4 * b + k + 1],
                                           start=(b == 0 and s == 0 and k == 0),
                                           stop=(b == 1 and k == KD // 2 - 1), skip_group_check=True)
                    mm.then_inc(wm_used[b], 1)

            pe.wait_ge(cact_ready, 1)
            with pe.Fori(0, 4) as t:
                for s in range(2):
                    pe.wait_ge(x_in[s], t * 16 + 16)
                    pe.wait_ge(x_kept[s], t + 1)
                    for k in range(KD):
                        mm = pe.transpose(ps[:, 2 * s + k // 4, (k % 4) * P:(k % 4) * P + P],
                                          raw[:, s, k * P:k * P + P], ident)
                    mm.then_inc(x_turned, 1)
                first_pair(t)
            with pe.Fori(4, M_FIRST) as t:
                first_pair(t)

            def scores(l, i, c, j):
                g, window = j % 2, j // 2
                tiles = key_tiles(i, window)
                nk = len(tiles) * P
                lo, hi = 64 * g, 64 * g + 64
                if j == 0:
                    if c == 0:
                        pe.wait_ge(k_split, l * NT + i + 1)
                        pe.wait_ge(qs_ready, l * NT + (i + 1))
                pe.wait_ge(p_ready, l * JOBS + c * 4 + (16 * i + j + 1))
                for b in range((nk + HS - 1) // HS):
                    w = min(HS, nk - b * HS)
                    bank = ps[:, 2 * g + b, :]
                    masks = []
                    if i >= 4 and not window:
                        masks.append((0, w, selbT[lo:hi, i, :], blk[lo:hi, b * HS:b * HS + w]))
                    if i >= 4 and window and b == 0:
                        masks.append((0, P, identb, tailm))
                    if (len(tiles) - 1) // 4 == b:
                        d = (len(tiles) - 1) % 4 * P
                        masks.append((d, P, identb, diagm))
                    for m, (at, n, lhs, rhs) in enumerate(masks):
                        pe.matmul(bank[:, at:at + n], lhs, rhs, start=(m == 0), stop=False,
                                  skip_group_check=True)
                    keys = slice(tiles[0] * P + b * HS, tiles[0] * P + b * HS + w)
                    for m, (q, k) in enumerate(((0, k_hi), (0, k_lo), (1, k_hi))):
                        mm = pe.matmul(bank[:, 0:w], q_parts[lo:hi, i % 2, q, c, :], k[lo:hi, window, keys],
                                       start=(m == 0 and not masks), stop=(m == 2), skip_group_check=True)
                mm.then_inc(s_done, 1)

            def turn(l, i, c, j):
                tiles = key_tiles(i, j // 2)
                pe.wait_ge(pn_ready, l * JOBS + c * 4 + (16 * i + j + 1))
                for group in range(n_groups(i)):
                    r = j % 2 if i < 4 else group
                    pe.wait_ge(pt_ready, l * GROUPS + groups_before(i, c, j) + (group + 1))
                    for a in range(4 * group, min(4 * group + 4, len(tiles))):
                        mm = pe.transpose(ps[:, 4 + r, (a % 4) * P:(a % 4) * P + P],
                                          probs[:, j, a * P:a * P + P], ident)
                    mm.then_inc(t_done, 1)

            def weigh(l, i, c, j):
                g, window = j % 2, j // 2
                tiles = key_tiles(i, window)
                if i >= 2:
                    pe.wait_ge(o_read, l * NT + i)
                for group in range(n_groups(i)):
                    r = j % 2 if i < 4 else group
                    pe.wait_ge(pt_ready, l * GROUPS + groups_before(i, c, j) + (group + 3))
                    for a in range(4 * group, min(4 * group + 4, len(tiles))):
                        mm = pe.matmul(ps[HD * g:HD * g + HD, 6 + i % 2, c * P:c * P + P],
                                       vals[:, tiles[a], P * window + HD * g:P * window + HD * g + HD],
                                       probsT[:, r, (a % 4) * P:(a % 4) * P + P],
                                       start=(a == 0 and not window), stop=(a == len(tiles) - 1 and window == 1),
                                       skip_group_check=True)
                mm.then_inc(pv_done, 1)

            with pe.Fori(0, DEPTH) as l:
                wl, ml = l * W_LAYER, l * M_LAYER + M_FIRST
                pe.wait_ge(prow_in, l * (16 * N_PROW) + 16 * N_PROW)
                for a, n, col in ((0, P, 0), (1, 88, P_T0), (2, 64, P_PEK)):
                    mm = pe.transpose(ps[:, 6, col:col + n], prow[0:n, a, :], ident[0:n, 0:n])
                mm.then_inc(prow_turned, 1)
                norm_factors(l * 3, l * SQ_LAYER + SQ_FIRST)
                pe.wait_ge(modA_read, l + 1)
                apart(pe)

                def project(slot, n, chunk, rope, first, pair, col):
                    pe.wait_ge(pj_copied, l * 16 + chunk * 2 + 1)

                    def rotate(hf):
                        pe.wait_ge(pj_copied, l * 16 + chunk * 2 + (hf + 1 + 3))
                        pe.wait_ge(rope_done, l * 14 + rope * 2 + 1)
                        pe.matmul(ps[:, 4 + hf, :], rope_r, raw[:, slot, hf * HS:hf * HS + HS],
                                  start=True, stop=True).then_inc(rot_done, 1)

                    gemm(slot, n, lambda k: hT[:, k, :], before=first)
                    if rope is not None:
                        rotate(0)
                    mod_pair(pair, col)
                    if rope is not None:
                        rotate(1)

                with pe.Fori(0, 2) as t:
                    for s in range(2):
                        project(s, wl + W_Q + t, t * 2 + s, t * 2 + s,
                                (lambda k: pe.wait_ge(h_ready, l * 16 + (k + 1))) if s == 0 else None,
                                ml + t * 2 + s, t * 4 + (16 + 2 * s))
                for n, rope in enumerate((4, None, 5, 6)):
                    project(n % 2, wl + W_K + n // 2, 4 + n, rope, None, ml + 4 + n, 24 + 2 * n)

                pe.wait_ge(pj_copied, l * 16 + 16 + 3)
                for n in range(8):
                    s, kv = n % 2, n // 4
                    if kv == 0:
                        if n == 0:
                            pe.wait_ge(w1k_in, l * 128 + 128)
                        w = w1k[n]
                    else:
                        pe.wait_ge(w_in_sem[s], (wl + W_C1 + (n - 4) // 2 + 1) * 32)
                        w = wr[:, s, :, :]
                    if n % 4 == 0:
                        pe.wait_ge(pe_added, l * 2 + kv + 1)
                    for g in range(2):
                        for a in range(8):
                            tok = 8 * (n % 4) + a
                            mm = pe.matmul(ps[:, 2 * kv + g, 0:NCMP], w[64 * g:64 * g + 64, a, :],
                                           kvpe[64 * g:64 * g + 64, 2 * kv + tok // 16,
                                                tok:tok + 16 * (NCMP - 1) + 1:16],
                                           start=(tok == 0), stop=(tok == 31))
                        if kv == 1:
                            mm.then_inc((half_done, w_used)[g][s], 1)
                        elif n == 3 and g == 1:
                            mm.then_inc(w1k_used, 1)

                pe.wait_ge(hid_ready, l * 2 + 2)
                pe.wait_ge(wv_in, l * 32 + 32)
                for t in range(NT):
                    if t >= 4:
                        pe.wait_ge(v_copied, l * NT + (t - 3))
                    for k in range(KD):
                        mm = pe.matmul(ps[:, t % 4, 0:NVG], hT[:, k, t * P:t * P + P], wv[:, k, :],
                                       start=(k == 0), stop=(k == KD - 1))
                    mm.then_inc(v_done, 1)

                pe.wait_ge(w2_in, l * 32 + 32)
                pe.wait_ge(rope_done, l * 14 + 14 + 1)
                for kv in range(2):
                    for g in range(2):
                        lhs, rhs = (w2[:, 0, :], hid[:, 0, g, :]) if kv == 0 else (hid[:, 1, g, :], w2[:, 1, :])
                        mm = pe.matmul(ps[64 * g:64 * g + 64, 4 + kv, 0:HD], lhs, rhs, start=True, stop=True)
                mm.then_inc(kvc_done, 1)
                pe.wait_ge(v_copied, l * NT + NT)
                pe.wait_ge(kvc_ready, l + 1)
                apart(pe)

                with pe.Fori(0, 2) as t:
                    def turn_selection(u):
                        n = l * NT + t * 4 + u
                        pe.wait_ge(sel_ready, n + 1)
                        pe.transpose(ps[:, 6, 0:HD].bitcast(BF16), selb[:, :, :].rearrange("p g n -> p (g n)"),
                                     identb).then_inc(selT_done, 1)

                    def compressed(p, middle):
                        u, step = p // 3, (p % 3 if not middle else 3)
                        n = l * NT + t * 4 + u
                        if step == 0:
                            if u:
                                turn_selection(u - 1)
                            pe.wait_ge(qsc_ready, n + 1)
                            pe.wait_ge(oc_read, n + 1)
                            for cc in range(NC):
                                for g in range(2):
                                    mm = pe.matmul(ps[:, 4 + g, cc * HD:cc * HD + HD],
                                                   qs[64 * g:64 * g + 64, cc, :], kcT[64 * g:64 * g + 64, :],
                                                   start=True, stop=True)
                            mm.then_inc(cs_done, 1)
                        elif step == 3 and p % 3 == 2:
                            pe.wait_ge(pc_ready, n + 1)
                            pe.wait_ge(selT_ready, n + 1)
                            for cc in range(NC):
                                mm = pe.transpose(ps[:, 6, cc * P:cc * P + P],
                                                  sc[:, cc, :, :].rearrange("p g n -> p (g n)"), ident)
                            mm.then_inc(pcT_done, 1)
                        elif step == 2:
                            pe.wait_ge(pcT_ready, n + 1)
                            apart(pe)
                            for g in range(2):
                                mm = pe.matmul(ps[64 * g:64 * g + 64, 4, :], vcN[64 * g:64 * g + 64, :],
                                               pcT[64 * g:64 * g + 64, :, :].rearrange("p c q -> p (c q)"),
                                               start=True, stop=True)
                            mm.then_inc(oc_done, 1)

                    for n in range(6):
                        free, count = ((cv_prod, 1), (cv_out, 1), (cc_copied, 1), (cv_prod, 2),
                                       (cv_out, 2), (cc_copied, 2))[n]
                        pe.wait_ge(free, l * 4 + t * 2 + count)
                        gemm(n % 2, wl + t * 3 + (W_CV + n // 2), lambda k: hT[:, k, :],
                             during=lambda hf, n=n: compressed(2 * n + hf, True),
                             after=lambda hf, n=n: compressed(2 * n + hf, False))
                        if 1 <= n < 5:
                            mod_pair(ml + t * 4 + (7 + n), t * 8 + (30 + 2 * n))
                    turn_selection(3)
                pe.wait_ge(cv_out, l * 4 + 4 + 1)
                pe.wait_ge(cv_prod, l * 4 + 4 + 1)
                pe.wait_ge(selT_ready, l * NT + NT + 1)
                pe.wait_ge(modB_read, l + 1)
                pe.wait_ge(oc_read, l * NT + NT + 1)
                for j in range(2):
                    scores(l, 0, 0, j)
                sum_squares(l * SQ_LAYER + SQ_FIRST + 4)
                scores(l, 0, 0, 2)
                pe.wait_ge(ms_ready, l * 4 + 2)
                turn(l, 0, 0, 0)

                def steps(i, c, last):
                    for j in range(4):
                        if not ends(i, last, j, 3):
                            scores(l, *ahead(i, c, last, j, 3))
                        weigh(l, i, c, j)
                        if not ends(i, last, j, 1):
                            turn(l, *ahead(i, c, last, j, 1))

                for i in range(NT):
                    for cc in range(NC):
                        steps(i, cc, cc == NC - 1)

                pe.wait_ge(pt_ready, l * GROUPS + GROUPS + 2)
                pe.wait_ge(att_added, l * NT + NT)
                norm_factors(l * 3 + 1)

                pe.wait_ge(mixc_ready, l * 4 + 4)
                apart(pe)

                with pe.Fori(0, 4) as t:
                    for s in range(2):
                        pe.wait_ge(wo_added, l * 8 + t * 2 + (s + 1))
                        pe.wait_ge(wo_in[s], l * 64 + t * 16 + 16)
                        gemm(s, wl + W_WO + t, lambda k: mixa[:, k, :] if k < 4 else mixc[:, k - 4, :],
                             ks=(4, 5, 6, 7, 0, 1, 2, 3),
                             before=lambda k: pe.wait_ge(mixa_ready, l * 4 + k + 1) if k < 4 else None)
                norm_factors(l * 3 + 2, l * SQ_LAYER + SQ_FIRST + 12)

                def three(out, w, k, cols, hi, lo, first, last):
                    for m, (a, b) in enumerate(((w_hi, hi), (w_hi, lo), (w_lo, hi))):
                        mm = pe.matmul(out, a[:, w, k:k + P], b[:, cols], start=first and m == 0,
                                       stop=last and m == 2)
                    return mm

                def up_first():
                    for s in range(2):
                        pe.wait_ge(w_split[s], l * W_FFN + 1)
                        for k in range(KD):
                            if s == 0:
                                pe.wait_ge(h_high, l * KD + (k + 1))
                            for w in (w_hi, w_lo):
                                for hf in range(2):
                                    pe.matmul(ps[:, 2 * s + hf, :], w[:, s, k * P:k * P + P],
                                              h_hi[:, k, hf * HS:hf * HS + HS], start=(k == 0 and w is w_hi),
                                              stop=False)
                    for s in range(2):
                        for k in range(KD):
                            if s == 0:
                                pe.wait_ge(h_ready, l * 16 + (8 + k + 1))
                            for hf in range(2):
                                mm = pe.matmul(ps[:, 2 * s + hf, :], w_hi[:, s, k * P:k * P + P],
                                               h_lo[:, k, hf * HS:hf * HS + HS], start=False, stop=(k == KD - 1))
                        mm.then_inc(w_used[s], 1)

                def up(r, t, pair):
                    f0, nf = ROUNDS[r]
                    for s in range(2):
                        pe.wait_ge(w_split[s], l * W_FFN + t + (W_ROUND[r] + 1))
                        pe.wait_ge(u_ready, l * (2 * NF) + t * 2 + (2 * f0 + s + 1))
                        if s == 1 and r > 0:
                            pe.wait_ge(dn_added, l * ADDED + (KD * r + 2))
                        for hf in range(2):
                            cols = slice(hf * HS, hf * HS + HS)
                            for k in range(KD):
                                mm = three(ps[:, 2 * s + hf, :], s, k * P, cols, h_hi[:, k, :], h_lo[:, k, :],
                                           k == 0, k == KD - 1)
                            if hf == 1:
                                mm.then_inc(w_used[s], 1)
                            elif s == 0 and pair is not None:
                                mod_pair(ml + 16 + pair, pair * 2)

                def down(r, t, s):
                    f0, nf = ROUNDS[r]
                    first = isinstance(t, int) and t == 0 and s == 0
                    pe.wait_ge(w_split[s], l * W_FFN + t + (W_ROUND[r] + nf + 1))
                    ks = (range(nf - 1), (nf - 1,)) if first else (range(nf),)
                    for k, b in [(k, b) for part in ks for b in range(2) for k in part]:
                        if k == 0:
                            if first:
                                pe.wait_ge(u_ready, l * (2 * NF) + (2 * (f0 + nf) + b + 1))
                            else:
                                pe.wait_ge(dn_added, l * ADDED + t * 4 + (KD * r + 2 * s + b + 1))
                        if first and k == nf - 1:
                            break
                        for hf in range(2):
                            mm = three(ps[:, 2 * b + hf, :], s, (2 * k + b) * P, slice(hf * HS, hf * HS + HS),
                                       y_hi[:, k, :], y_lo[:, k, :], k == 0, k == nf - 1)
                        if k == nf - 1:
                            mm.then_inc((dn_done, w_used[s])[b], 1)
                    if first:
                        k = nf - 1
                        pe.wait_ge(y_high, l * NF + (f0 + nf))
                        for w, y in ((w_hi, y_hi), (w_lo, y_hi), (w_hi, y_lo)):
                            if y is y_lo:
                                pe.wait_ge(y_ready, l * NF + (f0 + nf + 1))
                            for b in range(2):
                                for hf in range(2):
                                    at = (2 * k + b) * P
                                    mm = pe.matmul(ps[:, 2 * b + hf, :], w[:, s, at:at + P],
                                                   y[:, k, hf * HS:hf * HS + HS], start=False, stop=(y is y_lo))
                                if y is y_lo:
                                    mm.then_inc((dn_done, w_used[s])[b], 1)

                for r, (f0, nf) in enumerate(ROUNDS):
                    pe.wait_ge(dn_added, l * ADDED + (KD * r + (1 if r else 2)))
                    if r == 0:
                        pe.wait_ge(u_ready, l * (2 * NF) + 2)
                    apart(pe)
                    if r == 0 or r == 2:
                        if r == 0:
                            up_first()
                        else:
                            up(r, 0, 7)
                        with pe.Fori(1, nf) as t:
                            up(r, t, t - 1 if r == 0 else None)
                    else:
                        with pe.Fori(0, nf) as t:
                            up(r, t, t + 3 if r == 1 else None)
                    pe.wait_ge(y_ready, l * NF + (f0 + nf))
                    for t in range(2):
                        for s in range(2):
                            down(r, t, s)

            norm_factors(DEPTH * 3, DEPTH * SQ_LAYER + SQ_FIRST)
            for t in range(NT):
                s = t % 2
                if t >= 2:
                    pe.wait_ge(fin_copied[s], t // 2)
                for k in range(KD):
                    if t == 0:
                        pe.wait_ge(fin_ready, k + 1)
                    mm = pe.transpose(ps[:, 2 * s + k // 4, (k % 4) * P:(k % 4) * P + P],
                                      hT[:, k, t * P:t * P + P], ident)
                mm.then_inc(fin_turned, 1)

        @block.scalar
        def _(act):
            act.sem_inc(x_kept[0], 1)
            act.sem_inc(pj_copied, 3)
            act.sem_inc(p_ready, 2)
            act.sem_inc(pt_ready, 2)

            def slot(s):
                return ps[:, 2 * s:2 * s + 2, :].rearrange("p b f -> p (b f)")

            def square(src, s, n, ready=None):
                if ready is not None:
                    act.wait_ge(*ready)
                act.wait_ge(sq_added, n + 1)
                apart(act)
                act.activation(sq[:, s, :], src, ACT.Square).then_inc(sq_ready, 1)

            def root(n, dst=rms[:, 0, :]):
                act.wait_ge(ms_ready, n + 1)
                apart(act)
                act.activation(dst, dst, ACT.Sqrt).then_inc(rms_ready, 1)

            def shift(n, mod0, dst, done):
                for k in range(KD):
                    act.wait_ge(xn_ready, n + (k + 1))
                    act.activation(dst[:, k, :], hT[:, k, :], ACT.Identity,
                                   bias=mod[:, mod0 + k:mod0 + k + 1]).then_inc(done, 1)

            act.wait_ge(cst_ready, 1)
            act.activation(cact[:, 0, :], cst[:, 0:8], ACT.Exp, scale=-1.0).then_inc(c_exp, 1)
            with act.Fori(0, 4) as t:
                act.wait_ge(x_turned, t * 2 + 1)
                act.activation(xT[:, :, bass.ds(t * 2 * P, P)],
                               slot(0).rearrange("p (k f) -> p k f", f=P), ACT.Copy).then_inc(x_kept[0], 1)
            act.wait_ge(angle_ready, 2)
            act.activation(sinT, sinT, ACT.Sin).then_inc(trig_ready, 1)
            act.activation(cosT, cosT, ACT.Sin).then_inc(trig_ready, 1)
            act.wait_ge(x_kept[1], 5)
            act.wait_ge(x_kept[0], 5)
            for k in range(KD):
                square(xT[:, k, :], k % 2, k)

            def softmax(l, i, c, j):
                g, window = j % 2, j // 2
                nk = len(key_tiles(i, window)) * P
                n = l * JOBS + c * 4 + (16 * i + j)
                act.wait_ge(smax_ready, n + 1)
                if not (isinstance(c, int) and c == 0 and i == 0):
                    act.wait_ge(t_done, l * GROUPS + groups_before(i, c, j, 3) + 1)
                apart(act)
                act.activation(probs[:, j, 0:nk], slot(g)[:, 0:nk], ACT.Exp, bias=smax[:, g, 1:2], scale=SCALE,
                               accum_out=ssum[:, j:j + 1]).then_inc(p_ready, 1)

            def keep_turned(l, i, c, j):
                for group in range(n_groups(i)):
                    r = j % 2 if i < 4 else group
                    w = (min(4 * group + 4, len(key_tiles(i, j // 2))) - 4 * group) * P
                    act.wait_ge(t_done, l * GROUPS + groups_before(i, c, j) + (group + 2))
                    act.wait_ge(pv_done, l * JOBS + c * 4 + (16 * i + j + 1))
                    act.activation(probsT[:, r, 0:w], ps[:, 4 + r, 0:w], ACT.Copy).then_inc(pt_ready, 1)

            with act.Fori(0, DEPTH) as l:
                wl, sl = l * W_LAYER, l * SQ_LAYER + SQ_FIRST
                root(l * 4)
                shift(l * 16, 0, hT, h_ready)

                def copy_chunk(s, n, chunk, dst, rope):
                    for hf in range(2):
                        if hf == 0:
                            act.wait_ge(half_done[s], l * W_FF + n + 1)
                        else:
                            act.wait_ge(w_used[s], wl + n + 2)
                        if rope is not None and hf == 0:
                            act.wait_ge(rope_done, l * 14 + rope * 2 + 1)
                        act.activation(dst[:, hf * HS:hf * HS + HS], ps[:, 2 * s + hf, :],
                                       ACT.Copy).then_inc(pj_copied, 1)

                with act.Fori(0, 2) as t:
                    for s in range(2):
                        copy_chunk(s, t + W_Q, t * 2 + s, raw[:, s, :], t * 2 + s - 1 if s else t * 2)
                for n, rope in enumerate((4, None, 5, 6)):
                    copy_chunk(n % 2, W_K + n // 2, 4 + n, vcT if n == 1 else raw[:, n % 2, :], rope)

                for kv in range(2):
                    if kv == 0:
                        act.wait_ge(w1k_used, l + 1)
                    else:
                        act.wait_ge(w_used[1], wl + W_C1 + 2 + 1)
                    act.activation(hidt[:, :, 0:NCMP], ps[:, 2 * kv:2 * kv + 2, 0:NCMP], ACT.Exp,
                                   scale=-1.0).then_inc(hid_exp, 1)
                    act.wait_ge(hid_ready, l * 2 + kv + 1)
                for t in range(NT):
                    act.wait_ge(v_done, l * NT + (t + 1))
                    act.activation(gate[:, t, :], ps[:, t % 4, GATE:NVG], ACT.Exp, scale=-1.0).then_inc(gate_exp, 1)
                    act.activation(vals[:, t, :], ps[:, t % 4, 0:GATE], ACT.Copy).then_inc(v_copied, 1)

                with act.Fori(0, 2) as t:
                    for p in range(12):
                        n, m = p // 2, p // 2 // 3
                        mm = l * 4 + t * 2 + m
                        u = l * NT + t * 4 + p // 3
                        if p % 3 == 0:
                            act.wait_ge(cs_shifted, u + 1)
                            act.activation(pc[:, :, :, :], sc[:, :, :, :], ACT.Exp, scale=SCALE).then_inc(cs_exp, 1)
                        elif p % 3 == 2:
                            act.wait_ge(pcT_done, u + 1)
                            act.activation(pcT[:, :, :].rearrange("p c q -> p (c q)"), ps[:, 6, :],
                                           ACT.Copy).then_inc(pcT_ready, 1)
                        if p % 2:
                            if n % 3 == 0:
                                act.wait_ge(w_used[n % 2], wl + t * 3 + (W_CV + n // 2 + 2))
                                act.wait_ge(cv_prod, mm + 1)
                                act.activation(cc_s, slot(n % 2), ACT.Copy).then_inc(cc_copied, 1)
                            elif n % 3 == 1:
                                act.wait_ge(cv_prod, mm + 2)
                                apart(act)
                                act.activation(mixc[:, bass.ds(t * 2 + m, 1), :].rearrange("p a f -> p (a f)"),
                                               cprod, ACT.Identity,
                                               scale=prm[:, bass.ds(t * 2 + (P_CW + 8 + m), 1)]).then_inc(cv_tap, 1)
                            else:
                                square(mixc[:, bass.ds(t * 2 + m, 1), :].rearrange("p a f -> p (a f)"),
                                       m, sl + t * 2 + m, (cv_out, mm + 2))

                def square_attention(i):
                    act.wait_ge(o_read, l * NT + (i + 2))
                    if i:
                        act.wait_ge(att_added, l * NT + i)
                    act.activation(sq[:, 0, 0:512].rearrange("p (c q) -> p c q", q=P), mixa[:, :, i * P:i * P + P],
                                   ACT.Square).then_inc(att_sq, 1)

                def high_keys(i):
                    part = slice(i * P, i * P + P)
                    act.activation(k_hi[:, :, part], kT[:, 0:2, part], ACT.Copy).then_inc(k_high, 1)

                for s in range(2):
                    act.wait_ge(w_used[s], wl + W_CV + 6 + 1)
                apart(act)
                high_keys(0)
                softmax(l, 0, 0, 0)
                softmax(l, 0, 0, 1)
                root(l * 4 + 1, rt[:, :])
                softmax(l, 0, 0, 2)
                keep_turned(l, 0, 0, 0)

                def steps(i, c, last):
                    for j in range(4):
                        if not ends(i, last, j, 3):
                            softmax(l, *ahead(i, c, last, j, 3))
                        if not ends(i, last, j, 1):
                            keep_turned(l, *ahead(i, c, last, j, 1))

                for i in range(NT):
                    if i < NT - 1:
                        high_keys(i + 1)
                    with act.Fori(0, NC - 1) as cc:
                        steps(i, cc, False)
                    if i >= 1:
                        square_attention(i - 1)
                    steps(i, NC - 1, True)
                square_attention(NT - 1)
                root(l * 4 + 2)

                with act.Fori(0, 4) as t:
                    for s in range(2):
                        square(xT[:, bass.ds(t * 2 + s, 1), :].rearrange("p a f -> p (a f)"), s,
                               sl + 4 + t * 2 + s, (wo_added, l * 8 + t * 2 + (s + 3)))
                root(l * 4 + 3)

                def high_weights(s, n, width=S):
                    act.wait_ge(w_in_sem[s], (wl + W_FF + n + 1) * 32)
                    apart(act)
                    act.activation(w_hi[:, s, 0:width], wr[:, s, :, :].rearrange("p k f -> p (k f)")[:, 0:width],
                                   ACT.Copy).then_inc(w_high[s], 1)

                for s in range(2):
                    high_weights(s, 0)
                shift(l * 16 + 8, 24, h_hi, h_high)
                act.wait_ge(sq_added, sl + 12 + 2)
                for r, (f0, nf) in enumerate(ROUNDS):
                    last = r == len(ROUNDS) - 1
                    w0 = W_ROUND[r]

                    def up(t, width):
                        for s in range(2):
                            if s == 0:
                                act.wait_ge(prod_ready, l * NF + t + (f0 + 1))
                            act.wait_ge(w_used[s], wl + t + (W_FF + w0 + 2))
                            apart(act)
                            act.activation(raw[:, s, :], slot(s), ACT.Identity,
                                           scale=prm[:, bass.ds(t + (P_T2 + f0 + NF * s), 1)]).then_inc(u_tap, 1)
                            high_weights(s, t + (w0 + 1), width)
                        act.wait_ge(u_ready, l * (2 * NF) + t * 2 + (2 * f0 + 1 + 2))
                        act.wait_ge(y_ready, l * NF + t + (f0 + 1))
                        apart(act)
                        act.activation(sq[:, 0, :], raw[:, 0, :], ACT.Silu).then_inc(silu_ready, 1)
                        act.wait_ge(prod_ready, l * NF + t + (f0 + 2))
                        apart(act)
                        act.activation(y_hi[:, bass.ds(t, 1), :].rearrange("p a f -> p (a f)"), sq[:, 0, :],
                                       ACT.Copy).then_inc(y_high, 1)

                    with act.Fori(0, nf - 1) as t:
                        up(t, S)
                    up(nf - 1, nf * 2 * P)
                    for t in range(2):
                        for s in range(2):
                            if not (last and t == 1):
                                high_weights(s, w0 + nf + t + 1, S if t else nf * 2 * P)
                            if last:
                                for b in range(2):
                                    m = 4 * t + 2 * s + b
                                    square(xT[:, m, :], b, sl + 12 + m, (dn_added, l * ADDED + (KD * r + m + 3)))

            root(DEPTH * 4)
            for t in range(0, NT, 2):
                act.wait_ge(fin_turned, t + 1)
                if t >= 2:
                    act.wait_ge(out_done[0], 16 * (t // 2))
                act.activation(raw[:, 0, :], slot(0), ACT.Copy).then_inc(fin_copied[0], 1)

        @block.gpsimd
        def _(pool):
            pool.sem_inc(sq_added, 2)
            summed = Chain(pool, mod_part)

            def mod_products(n, halves=(0, 1)):
                if 0 in halves:
                    pool.wait_ge(mod_done, n + 1)
                n = n + M_FIRST
                for b in halves:
                    pool.wait_ge(wm_in[b], n * 16 + 16)
                    apart(pool)
                    w = wm[:, b, :, :]
                    steps = [(w, w, cact[:, 2, 4 * b:4 * b + 4].unsqueeze(2).to_broadcast([P, 4, 2 * P]), ALU.mult),
                             (w[:, 0:2, :], w[:, 0:2, :], w[:, 2:4, :], ALU.add)]
                    if b == 0:
                        steps += [(accm[:, :], w[:, 0, :], w[:, 1, :], ALU.add)]
                    else:
                        steps += [(w[:, 0, :], w[:, 0, :], w[:, 1, :], ALU.add),
                                  (accm[:, :], accm[:, :], w[:, 0, :], ALU.add)]
                    for dst, in0, in1, op in steps[:-1]:
                        summed.inc(pool.tensor_tensor(dst, in0, in1, op))
                        summed.wait()
                    if b == 1:
                        pool.wait_ge(wm_used[0], n + 2)
                    dst, in0, in1, op = steps[-1]
                    ins = pool.tensor_tensor(dst, in0, in1, op)
                    ins.then_inc(wm_used[b], 1)

            def zero(n, last=False):
                if n is not None:
                    pool.wait_ge(ss_done, n)
                    apart(pool)
                    if last:
                        pool.sem_inc(sq_added, 1)
                pool.memset(acc[:, :], 0.0).then_inc(acc_zero, 1)

            def add(s, n, zeros):
                pool.wait_ge(sq_ready, n + 1)
                pool.wait_ge(sq_added, n + 2)
                pool.wait_ge(acc_zero, zeros)
                pool.tensor_tensor(acc[:, :], acc[:, :], sq[:, s, :], ALU.add).then_inc(sq_added, 1)

            zero(None)
            for k in range(KD - 1):
                add(k % 2, k, 1)
            with pool.Fori(0, DEPTH) as l:
                summed.enter(l, 5 * M_LAYER)
                sl, z, ml = l * SQ_LAYER + SQ_FIRST, l * 3, l * M_LAYER
                zero(l * 4 + 1, last=True)
                with pool.Fori(0, 8) as t:
                    summed.enter(t, 5)
                    mod_products(ml + t)
                    summed.leave(8)

                def compressed_steps(t):
                    for step in range(4):
                        u = t * 4 + step
                        pool.wait_ge(cs_done, l * NT + u + 1)
                        if step == 0:
                            pool.wait_ge(rope_done, l * 14 + 14 + 1)
                        apart(pool)
                        pool.tensor_copy(qs[:, :, :], qT[:, :, bass.ds(u * P, P)]).then_inc(qsc_ready, 1)
                        mod_products(ml + t * 4 + (8 + step))
                        if step == 2 or (step == 3 and t == 0):
                            add(step - 2, sl + t * 2 + step - 2, z + 2)

                def stage_queries(i, b):
                    q = qT[:, :, bass.ds(i * P, P)]
                    pool.tensor_copy(q_parts[:, b, 0, :, :], q).then_inc(q_high, 1)
                    pool.wait_ge(q_high, l * NT + i + 1)
                    apart(pool)
                    pool.tensor_tensor(q_parts[:, b, 1, :, :], q, q_parts[:, b, 0, :, :],
                                       ALU.subtract).then_inc(qs_ready, 1)

                def low_keys(i):
                    pool.wait_ge(k_high, l * NT + i + 1)
                    apart(pool)
                    part = bass.ds(i * P, P)
                    pool.tensor_tensor(k_lo[:, :, part], kT[:, 0:2, part], k_hi[:, :, part],
                                       ALU.subtract).then_inc(k_split, 1)

                def add_attention(i):
                    pool.wait_ge(att_sq, l * NT + i + 1)
                    apart(pool)
                    pool.tensor_tensor(sq[:, 0, 0:256], sq[:, 0, 0:256], sq[:, 0, 256:512],
                                       ALU.add).then_inc(att_part, 1)
                    pool.wait_ge(att_part, l * NT + i + 1)
                    apart(pool)
                    pool.tensor_tensor(acc[:, bass.ds(i * P, P)], sq[:, 0, 0:128], sq[:, 0, 128:256],
                                       ALU.add).then_inc(att_added, 1)

                compressed_steps(0)
                compressed_steps(1)
                pool.wait_ge(cv_prod, l * 4 + 4 + 1)
                apart(pool)
                stage_queries(0, 0)
                low_keys(0)
                add(1, sl + 3, z + 2)
                pool.wait_ge(cv_out, l * 4 + 4 + 1)
                apart(pool)
                stage_queries(1, 1)
                low_keys(1)
                pool.wait_ge(ss_done, l * 4 + 2)
                apart(pool)
                with pool.Fori(0, NT // 2 - 1) as t:
                    for b in range(2):
                        low_keys(t * 2 + (b + 2))
                        pool.wait_ge(s_done, l * JOBS + t * 32 + (16 * b + 16 + 1))
                        apart(pool)
                        stage_queries(t * 2 + (b + 2), b)
                        add_attention(t * 2 + b)
                add_attention(NT - 2)
                add_attention(NT - 1)
                zero(l * 4 + 3)
                with pool.Fori(0, 3) as t:
                    for s in range(2):
                        add(s, sl + 4 + t * 2 + s, z + 3)
                add(0, sl + 10, z + 3)
                zero(l * 4 + 4, last=True)
                def low(out, whole, high, ready, count, done):
                    pool.wait_ge(ready, count)
                    apart(pool)
                    pool.tensor_tensor(out, whole, high, ALU.subtract).then_inc(done, 1)

                def low_weights(s, n, width=S):
                    low(w_lo[:, s, 0:width], wr[:, s, :, :].rearrange("p k f -> p (k f)")[:, 0:width],
                        w_hi[:, s, 0:width],
                        w_high[s], l * W_FFN + n + 1, w_split[s])

                for s in range(2):
                    low_weights(s, 0)
                for r, (f0, nf) in enumerate(ROUNDS):
                    last = r == len(ROUNDS) - 1

                    def up(t, width):
                        for s in range(2):
                            if r < 2:
                                mod_products(ml + 16 + 4 * r + t, (s,))
                            low_weights(s, t + (W_ROUND[r] + 1), width)
                        low(y_lo[:, bass.ds(t, 1), :].rearrange("p a f -> p (a f)"), sq[:, 0, :],
                            y_hi[:, bass.ds(t, 1), :].rearrange("p a f -> p (a f)"),
                            y_high, l * NF + t + (f0 + 1), y_ready)

                    with pool.Fori(0, nf - 1) as t:
                        summed.enter(t, 5 if r < 2 else 0)
                        up(t, S)
                        summed.leave(nf - 1)
                    up(nf - 1, nf * 2 * P)
                    for t in range(2):
                        for s in range(2):
                            if not (last and t == 1):
                                low_weights(s, W_ROUND[r] + nf + t + 1, S if t else nf * 2 * P)
                            if last:
                                for b in range(2):
                                    if (t, s, b) != (1, 1, 1):
                                        add(b, sl + 12 + 4 * t + 2 * s + b, z + 4)
                summed.leave(DEPTH)

        @block.vector
        def _(dve):
            dve.sem_inc(x_kept[1], 1)
            dve.sem_inc(rope_done, 1)
            dve.sem_inc(cv_prod, 1)
            dve.sem_inc(cv_out, 1)
            dve.sem_inc(oc_read, 1)
            dve.sem_inc(selT_ready, 1)
            dve.sem_inc(o_read, 1)
            dve.sem_inc(s_done, 1)
            dve.sem_inc(wo_added, 2)
            dve.sem_inc(u_ready, 2)
            dve.sem_inc(y_ready, 1)
            dve.sem_inc(prod_ready, 1)
            dve.sem_inc(dn_added, 2)
            v = Chain(dve, vec)

            def own(ins):
                v.inc(ins)
                v.wait()

            def slot(s):
                return ps[:, 2 * s:2 * s + 2, :].rearrange("p b f -> p (b f)")

            def at(t3, k):
                return t3[:, bass.ds(k, 1), :].rearrange("p a f -> p (a f)")

            def mean_square(n, count):
                dve.wait_ge(ss_done, n + 1)
                dve.tensor_scalar(rt[:, :], ps[:, 4:6, :].rearrange("p b f -> p (b f)"), 1.0 / count, EPS,
                                  ALU.mult, ALU.add).then_inc(ms_ready, 1)

            def invert(n):
                v.inc(dve.reciprocal(rt[:, n * 256:n * 256 + 256], rt[:, n * 256:n * 256 + 256]))

            def norm_factors(n, norm, count):
                dve.wait_ge(ss_done, n + 1)
                dve.tensor_scalar(rms[:, 0, :], ps[:, 4, 0:NT], 1.0 / count, EPS,
                                  ALU.mult, ALU.add).then_inc(ms_ready, 1)
                dve.wait_ge(rms_ready, n + 1)
                own(dve.reciprocal(rms[:, 1, :], rms[:, 0, :]))
                dve.tensor_tensor(rt[:, :].rearrange("p (t q) -> p t q", q=P),
                                  ident.unsqueeze(1).to_broadcast([P, NT, P]),
                                  rms[:, 1, :].unsqueeze(2).to_broadcast([P, NT, P]), ALU.mult).then_inc(diag_ready, 1)
                dve.wait_ge(spread_done, norm + 1)
                return ps[:, 4:6, :].rearrange("p b f -> p (b f)")

            dve.wait_ge(const_in, 64)
            own(dve.tensor_copy(kb[:, :], hT[:, 0:2, :].rearrange("p k f -> p (k f)")[:, 0:k_mask.shape[1]]))
            own(dve.memset(hid[:, :, :, :], 0.0))
            own(dve.memset(selb[:, :, :], 0.0))
            dve.wait_ge(cst_turned, 1)
            dve.tensor_copy(cst[:, :], ps[:, 6, 0:16]).then_inc(cst_ready, 1)
            dve.wait_ge(c_exp, 1)
            own(dve.tensor_scalar(cact[:, 1, :], cact[:, 0, :], 1.0, None, ALU.add))
            own(dve.reciprocal(cact[:, 0, :], cact[:, 1, :]))
            dve.tensor_tensor(cact[:, 2, :], cst[:, 0:8], cact[:, 0, :], ALU.mult).then_inc(cact_ready, 1)
            with dve.Fori(0, 4) as t:
                dve.wait_ge(x_turned, t * 2 + 2)
                dve.tensor_copy(xT[:, :, bass.ds((t * 2 + 1) * P, P)],
                                slot(1).rearrange("p (k f) -> p k f", f=P)).then_inc(x_kept[1], 1)
            dve.wait_ge(pos_in, 16)
            own(dve.tensor_scalar(sinT, sq[:, 0, :].bitcast(I32), freq, None, ALU.mult))
            own(dve.tensor_scalar(rt[:, :], sinT, 1.0 / TWO_PI, ROUND, ALU.mult, ALU.add))
            own(dve.tensor_scalar(rt[:, :], rt[:, :], -ROUND, None, ALU.add))
            for part in TWO_PI_PARTS:
                own(dve.scalar_tensor_tensor(out=sinT, in0=rt[:, :], scalar=-part, in1=sinT,
                                             op0=ALU.mult, op1=ALU.add))
            dve.tensor_scalar(sinT, sinT, PI_BELOW, -PI_BELOW, ALU.min, ALU.max).then_inc(angle_ready, 1)
            dve.wait_ge(angle_ready, 1)
            own(dve.tensor_scalar(rt[:, :], sinT, -1.0, None, ALU.mult))
            own(dve.tensor_tensor(rt[:, :], rt[:, :], sinT, ALU.max))
            dve.tensor_scalar(cosT, rt[:, :], -1.0, TWO_PI / 4, ALU.mult, ALU.add).then_inc(angle_ready, 1)
            dve.wait_ge(trig_ready, 2)

            def row_max(l, i, c, j):
                g = j % 2
                nk = len(key_tiles(i, j // 2)) * P
                dve.wait_ge(s_done, l * JOBS + c * 4 + (16 * i + j + 2))
                own(dve.tensor_reduce(smax[:, g, 0:1], slot(g)[:, 0:nk], AX, ALU.max))
                dve.tensor_scalar(smax[:, g, 1:2], smax[:, g, 0:1], -SCALE, None, ALU.mult).then_inc(smax_ready, 1)

            def normalise(l, i, c, j):
                g, window = j % 2, j // 2
                nk = len(key_tiles(i, window)) * P
                dve.wait_ge(p_ready, l * JOBS + c * 4 + (16 * i + j + 3))
                own(dve.tensor_scalar(rsum[:, 0, j:j + 1], ssum[:, j:j + 1], 1e-30, None, ALU.max))
                own(dve.reciprocal(rsum[:, 1, j:j + 1], rsum[:, 0, j:j + 1]))
                dve.tensor_scalar(probs[:, j, 0:nk], probs[:, j, 0:nk], rsum[:, 1, j:j + 1],
                                  gate[:, i, bass.ds(c * 3 + (12 * g + 1 + window), 1)],
                                  ALU.mult, ALU.mult).then_inc(pn_ready, 1)

            def finish_tile(l, i):
                dve.wait_ge(pv_done, l * JOBS + (16 * i + 16 + 1))
                dst = mixa[:, :, i * P:i * P + P]
                dve.tensor_tensor(dst, dst, ps[:, 6 + i % 2, :].rearrange("p (c q) -> p c q", q=P),
                                  ALU.add).then_inc(o_read, 1)

            with dve.Fori(0, DEPTH) as l:
                v.enter(l, VEC_LAYER)
                wl, ml = l * W_LAYER, l * M_LAYER + M_FIRST
                dve.wait_ge(prow_turned, l + 2)
                own(dve.tensor_copy(prm[:, :], ps[:, 6, 0:NPRM]))
                dve.wait_ge(mod_done, l * M_LAYER + 1)
                dve.wait_ge(wm_used[1], ml + 1)
                dve.tensor_tensor(mod[:, 0:16], ps[:, 7, 0:16], prm[:, 0:16], ALU.add).then_inc(modA_read, 1)
                dve.wait_ge(modA_read, l + 1)
                own(dve.scalar_tensor_tensor(out=gsc[:, 0, :], in0=mod[:, 8:16], scalar=1.0,
                                             in1=prm[:, P_N1:P_N1 + 8], op0=ALU.add, op1=ALU.mult))
                factors = norm_factors(l * 4, l * 3, D)
                for k in range(KD):
                    dve.scalar_tensor_tensor(out=hT[:, k, :], in0=xT[:, k, :], scalar=gsc[:, 0, k:k + 1],
                                             in1=factors, op0=ALU.mult, op1=ALU.mult).then_inc(xn_ready, 1)

                def rotary(s, chunk, rope, dst):
                    for hf in range(2):
                        h0, h1 = hf * HS, hf * HS + HS
                        dve.wait_ge(pj_copied, l * 16 + chunk * 2 + (hf + 1 + 3))
                        own(dve.tensor_tensor(dst[:, h0:h1], raw[:, s, h0:h1], cosT[:, h0:h1], ALU.mult))
                        dve.wait_ge(rot_done, l * 14 + rope * 2 + (hf + 1))
                        own(dve.tensor_tensor(sq[:, s, h0:h1], ps[:, 4 + hf, :], sinT[:, h0:h1], ALU.mult))
                        dve.tensor_tensor(dst[:, h0:h1], dst[:, h0:h1], sq[:, s, h0:h1],
                                          ALU.add).then_inc(rope_done, 1)

                with dve.Fori(0, 2) as t:
                    v.enter(t, 8)
                    for s in range(2):
                        rotary(s, t * 2 + s, t * 2 + s, at(qT, t * 2 + s))
                    v.leave(2)

                def add_positions(src, a, prm0):
                    for b in range(2):
                        ins = dve.tensor_tensor(
                            kvpe[:, a + b, :].rearrange("p (n t) -> p n t", t=16),
                            src.rearrange("p (n t) -> p n t", t=16),
                            prm[:, prm0 + 16 * b:prm0 + 16 * b + 16].unsqueeze(1).to_broadcast([P, 64, 16]),
                            ALU.add)
                        if b == 0:
                            own(ins)
                    ins.then_inc(pe_added, 1)

                rotary(0, 4, 4, kT[:, 2, :])
                dve.wait_ge(rope_done, l * 14 + 10 + 1)
                add_positions(kT[:, 2, :], 0, P_PEK)
                dve.wait_ge(pj_copied, l * 16 + 12 + 3)
                add_positions(vcT, 2, P_PEV)
                rotary(0, 6, 5, kT[:, 0, :])
                rotary(1, 7, 6, kT[:, 1, :])

                for kv in range(2):
                    dve.wait_ge(hid_exp, l * 2 + kv + 1)
                    own(dve.tensor_scalar(hidt[:, :, 0:NCMP], hidt[:, :, 0:NCMP], 1.0, None, ALU.add))
                    own(dve.reciprocal(hidt[:, :, 0:NCMP], hidt[:, :, 0:NCMP]))
                    dve.tensor_tensor(hid[:, kv, :, 0:NCMP], ps[:, 2 * kv:2 * kv + 2, 0:NCMP],
                                      hidt[:, :, 0:NCMP], ALU.mult).then_inc(hid_ready, 1)
                dve.wait_ge(gate_exp, l * NT + NT)
                own(dve.tensor_scalar(gate[:, :, :], gate[:, :, :], 1.0, None, ALU.add))
                own(dve.reciprocal(gate[:, :, :], gate[:, :, :]))
                dve.wait_ge(kvc_done, l + 1)
                own(dve.tensor_copy(kcT[:, :], ps[:, 4, 0:HD]))
                dve.tensor_copy(vcN[:, :], ps[:, 5, 0:HD]).then_inc(kvc_ready, 1)

                with dve.Fori(0, 2) as t:
                    v.enter(t, VEC_CONV)

                    def conv(n):
                        m = n // 3
                        mm = l * 4 + t * 2 + m
                        dst = at(mixc, t * 2 + m)
                        if n % 3 == 1:
                            dve.wait_ge(cc_copied, mm + 1)
                            dve.wait_ge(w_used[n % 2], wl + t * 3 + (W_CV + n // 2 + 2))
                            dve.tensor_tensor(cprod, slot(n % 2), cc_s, ALU.mult).then_inc(cv_prod, 1)
                            dve.wait_ge(cv_tap, mm + 1)
                            for back, tap in ((1, 1), (2, 0)):
                                own(dve.scalar_tensor_tensor(
                                    out=dst[:, back:S], in0=cprod[:, 0:S - back],
                                    scalar=prm[:, bass.ds(t * 2 + (P_CW + 4 * tap + m), 1)],
                                    in1=dst[:, back:S], op0=ALU.mult, op1=ALU.add))
                        elif n % 3 == 2:
                            dve.wait_ge(w_used[n % 2], wl + t * 3 + (W_CV + n // 2 + 2))
                            dve.tensor_tensor(dst, slot(n % 2), dst, ALU.mult).then_inc(cv_out, 1)

                    def bcast(a, n):
                        return a.unsqueeze(2).to_broadcast([P, NH, n])

                    def compressed_softmax(u):
                        n = l * NT + u
                        flat = lambda a: a.rearrange("p c g n -> p (c g) n")
                        dve.wait_ge(cs_done, n + 2)
                        own(dve.tensor_tensor(
                            sc[:, :, :, :].rearrange("p c g n -> p g c n"),
                            ps[:, 4:6, 0:256].rearrange("p g (c n) -> p g c n", n=HD),
                            cmask[:, bass.ds(u, 1), :].unsqueeze(1).to_broadcast([P, 2, NC, HD]), ALU.add))
                        own(dve.tensor_reduce(cm[:, 0, :], flat(sc[:, :, :, :]), AX, ALU.max))
                        own(dve.tensor_scalar(cm[:, 1, :], cm[:, 0, :], BIG / 10, None, ALU.max))
                        dve.tensor_tensor(flat(sc[:, :, :, :]), flat(sc[:, :, :, :]), bcast(cm[:, 1, :], HD),
                                          ALU.subtract).then_inc(cs_shifted, 1)
                        dve.wait_ge(cs_exp, n + 1)
                        own(dve.tensor_reduce(cm[:, 0, :], flat(pc[:, :, :, :]), AX, ALU.add))
                        own(dve.tensor_scalar(cm[:, 1, :], cm[:, 0, :], 1e-30, None, ALU.max))
                        own(dve.reciprocal(cm[:, 2, :], cm[:, 1, :]))
                        own(dve.tensor_tensor(flat(pc[:, :, :, :]), flat(pc[:, :, :, :]), bcast(cm[:, 2, :], HD),
                                              ALU.mult))
                        gated = gate[:, bass.ds(u, 1), 0:22:3].rearrange(
                            "p a (g c) -> p (a c) g", g=2).unsqueeze(3).to_broadcast([P, NC, 2, HD])
                        dve.tensor_tensor(sc[:, :, :, :], pc[:, :, :, :], gated, ALU.mult).then_inc(pc_ready, 1)

                    def select_blocks(u):
                        own(dve.tensor_reduce(pg[:, :, :].rearrange("p g n -> p (g n)"),
                                              pc[:, :, :, :].rearrange("p c g n -> p (g n) c"), AX, ALU.add))
                        own(dve.tensor_reduce(imp[:, 0, :, :].rearrange("p g j -> p (g j)"),
                                              pg[:, :, :].rearrange("p g (j a) -> p (g j) a", a=4), AX, ALU.add))
                        own(dve.tensor_tensor(imp[:, 0, :, 1:NBLK], imp[:, 0, :, 1:NBLK],
                                              pg[:, :, 3:60:4], ALU.add))
                        for a, op in ((0, ALU.mult), (1, ALU.add)):
                            own(dve.tensor_tensor(imp[:, 0, :, :], imp[:, 0, :, :],
                                                  keep[:, bass.ds(u, 1), a, :].to_broadcast([P, 2, NBLK]), op))
                        full = [P, 2, NBLK, NBLK]
                        me = imp[:, 0, :, :].unsqueeze(3).to_broadcast(full)
                        other = imp[:, 0, :, :].unsqueeze(2).to_broadcast(full)
                        own(dve.tensor_tensor(cmpa, other, me, ALU.is_gt))
                        own(dve.tensor_tensor(cmpb, other, me, ALU.is_equal))
                        own(dve.tensor_tensor(cmpb, cmpb, ltm.unsqueeze(1).to_broadcast(full), ALU.mult))
                        own(dve.tensor_tensor(raw[:, 0, 0:512], raw[:, 0, 0:512], raw[:, 0, 512:1024], ALU.add))
                        own(dve.tensor_reduce(rank[:, :, :].rearrange("p g j -> p (g j)"),
                                              cmpa.rearrange("p g j i -> p (g j) i"), AX, ALU.add))
                        dve.tensor_scalar(selb[:, :, 0:NBLK], rank[:, :, :], NSEL - 0.5, BIG,
                                          ALU.is_ge, ALU.mult).then_inc(sel_ready, 1)

                    def compressed_output(u):
                        n = l * NT + u
                        dve.wait_ge(oc_done, n + 1)
                        dve.tensor_copy(mixa[:, :, bass.ds(u * P, P)],
                                        ps[:, 4, :].rearrange("p (c q) -> p c q", q=P)).then_inc(oc_read, 1)

                    def keep_selection(u):
                        n = l * NT + u
                        dve.wait_ge(selT_done, n + 1)
                        dve.tensor_copy(at(selbT, u), ps[:, 6, 0:HD].bitcast(BF16)).then_inc(selT_ready, 1)

                    for p in range(12):
                        u = t * 4 + p // 3
                        if p % 3 == 0:
                            if p:
                                keep_selection(u - 1)
                            compressed_softmax(u)
                        if p % 2:
                            conv(p // 2)
                        if p % 3 == 0:
                            select_blocks(u)
                        elif p % 3 == 2:
                            compressed_output(u)
                    keep_selection(u)
                    v.leave(2)

                dve.wait_ge(mod_done, l * M_LAYER + 16 + 1)
                dve.tensor_tensor(mod[:, 16:48], ps[:, 7, 16:48], prm[:, 16:48], ALU.add).then_inc(modB_read, 1)
                dve.wait_ge(modB_read, l + 1)
                own(dve.scalar_tensor_tensor(out=gsc[:, 1, :], in0=mod[:, 32:40], scalar=1.0,
                                             in1=prm[:, P_N2:P_N2 + 8], op0=ALU.add, op1=ALU.mult))

                dve.wait_ge(oc_read, l * NT + NT + 1)
                row_max(l, 0, 0, 0)
                row_max(l, 0, 0, 1)
                mean_square(l * 4 + 1, 512)
                normalise(l, 0, 0, 0)
                row_max(l, 0, 0, 2)
                normalise(l, 0, 0, 1)

                def steps(i, c, last):
                    for j in range(4):
                        if not ends(i, last, j, 3):
                            row_max(l, *ahead(i, c, last, j, 3))
                        if not ends(i, last, j, 2):
                            normalise(l, *ahead(i, c, last, j, 2))

                for i in range(NT):
                    with dve.Fori(0, NC - 1) as cc:
                        v.enter(cc, 12)
                        steps(i, cc, False)
                        v.leave(NC - 1)
                    steps(i, NC - 1, True)
                    finish_tile(l, i)
                    if i < 4:
                        if i == 0:
                            dve.wait_ge(rms_ready, l * 4 + 2)
                        invert(i)
                    else:
                        k = i - 4
                        v.wait()
                        dve.scalar_tensor_tensor(out=mixc[:, k, :], in0=mixc[:, k, :],
                                                 scalar=prm[:, P_GC + k:P_GC + k + 1], in1=rt[:, :],
                                                 op0=ALU.mult, op1=ALU.mult).then_inc(mixc_ready, 1)

                factors = norm_factors(l * 4 + 2, l * 3 + 1, 512)
                for k in range(4):
                    dve.scalar_tensor_tensor(out=mixa[:, k, :], in0=mixa[:, k, :],
                                             scalar=prm[:, P_GA + k:P_GA + k + 1], in1=factors,
                                             op0=ALU.mult, op1=ALU.mult).then_inc(mixa_ready, 1)

                with dve.Fori(0, 4) as t:
                    for s in range(2):
                        dve.wait_ge(w_used[s], wl + W_WO + t + 2)
                        xd = at(xT, t * 2 + s)
                        dve.scalar_tensor_tensor(out=xd, in0=slot(s), scalar=mod[:, bass.ds(t * 2 + (16 + s), 1)],
                                                 in1=xd, op0=ALU.mult, op1=ALU.add).then_inc(wo_added, 1)
                factors = norm_factors(l * 4 + 3, l * 3 + 2, D)

                def low_input(k):
                    dve.wait_ge(h_high, l * KD + k + 1)
                    dve.wait_ge(xn_ready, l * 16 + (8 + k + 1))
                    dve.scalar_tensor_tensor(out=h_lo[:, k, :], in0=hT[:, k, :], scalar=mod[:, 24 + k:25 + k],
                                             in1=h_hi[:, k, :], op0=ALU.add, op1=ALU.subtract).then_inc(h_ready, 1)

                for k in range(KD):
                    dve.scalar_tensor_tensor(out=hT[:, k, :], in0=xT[:, k, :], scalar=gsc[:, 1, k:k + 1],
                                             in1=factors, op0=ALU.mult, op1=ALU.mult).then_inc(xn_ready, 1)
                for k in range(KD):
                    low_input(k)

                for r, (f0, nf) in enumerate(ROUNDS):
                    with dve.Fori(0, nf) as t:
                        v.enter(t, 2)
                        for s in range(2):
                            dve.wait_ge(u_tap, l * (2 * NF) + t * 2 + (2 * f0 + s + 1))
                            for back, tap0 in ((1, P_T1), (2, P_T0)):
                                ins = dve.scalar_tensor_tensor(
                                    out=raw[:, s, back:S], in0=slot(s)[:, 0:S - back],
                                    scalar=prm[:, bass.ds(t + (tap0 + f0 + NF * s), 1)],
                                    in1=raw[:, s, back:S], op0=ALU.mult, op1=ALU.add)
                                if back == 1:
                                    own(ins)
                            ins.then_inc(u_ready, 1)
                        dve.wait_ge(silu_ready, l * NF + t + (f0 + 1))
                        dve.wait_ge(u_ready, l * (2 * NF) + t * 2 + (2 * f0 + 2 + 2))
                        dve.tensor_tensor(sq[:, 0, :], sq[:, 0, :], raw[:, 1, :], ALU.mult).then_inc(prod_ready, 1)
                        v.leave(nf)
                    with dve.Fori(0, 2) as t:
                        for s in range(2):
                            for b in range(2):
                                if b == 0:
                                    dve.wait_ge(dn_done, l * (ADDED // 2) + t * 2 + (KD // 2 * r + s + 1))
                                else:
                                    dve.wait_ge(w_used[s], wl + t + (W_FF + W_ROUND[r] + nf + 2))
                                dve.wait_ge(dn_added, l * ADDED + (KD * r + 2))
                                xd = at(xT, t * 4 + (2 * s + b))
                                dve.scalar_tensor_tensor(out=xd, in0=slot(b),
                                                         scalar=mod[:, bass.ds(t * 4 + (40 + 2 * s + b), 1)],
                                                         in1=xd, op0=ALU.mult, op1=ALU.add).then_inc(dn_added, 1)
                v.leave(DEPTH)

            factors = norm_factors(DEPTH * 4, DEPTH * 3, D)
            for k in range(KD):
                dve.scalar_tensor_tensor(out=hT[:, k, :], in0=xT[:, k, :], scalar=cst[:, 8 + k:9 + k],
                                         in1=factors, op0=ALU.mult, op1=ALU.mult).then_inc(fin_ready, 1)
            for t in range(1, NT, 2):
                dve.wait_ge(fin_turned, t + 1)
                if t >= 2:
                    dve.wait_ge(out_done[1], 16 * (t // 2))
                dve.tensor_copy(raw[:, 1, :], slot(1)).then_inc(fin_copied[1], 1)


def shape_constants():
    import numpy as np
    f32 = np.float32
    q, n = np.arange(P), np.arange(P)
    ident = np.eye(P, dtype=f32)
    rope = np.zeros((P, P), f32)
    for h in range(2):
        for d in range(8):
            rope[64 * h + d + 8, 64 * h + d] = -1.0
            rope[64 * h + d, 64 * h + d + 8] = 1.0
    freq = np.zeros((P, 1), f32)
    for h in range(2):
        for d in range(16):
            freq[64 * h + d, 0] = f32(500000.0) ** f32(-(d % 8) / 8)
    tok = np.arange(NT)[:, None] * P + q[None, :]
    cmask = np.where((np.arange(HD)[None, None, :] * 16 + 31 <= tok[:, :, None])
                     & (np.arange(HD) < NCMP)[None, None, :], 0.0, BIG).astype(f32)
    b, j = (tok // HD)[:, :, None], np.arange(NBLK)[None, None, :]
    causal = j <= b
    forced = causal & ((j == 0) | (j == b) | (j == b - 1))
    keep = np.stack([np.where(causal & ~forced, 1.0, 0.0),
                     np.where(forced, -BIG, np.where(causal, 0.0, BIG))], 2).astype(f32)
    lt = np.broadcast_to((np.arange(NBLK)[None, :] < np.arange(NBLK)[:, None]).astype(f32)[None],
                         (P, NBLK, NBLK))
    k_f32 = np.concatenate([ident, rope, np.ones((P, P), f32), freq,
                            cmask.transpose(1, 0, 2).reshape(P, -1), keep.transpose(1, 0, 2, 3).reshape(P, -1),
                            lt.reshape(P, -1)], axis=1)
    blk = np.zeros((P, S), f32)
    for h in range(2):
        for j in range(NBLK):
            blk[64 * h + j, HD * j:HD * j + HD] = 1.0
    diag = np.where(n[None, :] > q[:, None], BIG, 0.0)
    tail = np.where(n[None, :] <= q[:, None], BIG, 0.0)
    k_mask = np.concatenate([ident, diag, tail, blk], axis=1).astype(f32)
    return np.ascontiguousarray(k_f32), np.ascontiguousarray(k_mask)


_INS = ["x", "c", "positions", "w_mod", "b_mod", "norm1_g", "w_in", "cmp_pe_k", "cmp_w1_k", "cmp_w2_k",
        "cmp_pe_v", "cmp_w1_v", "cmp_w2_v", "conv_w", "grp_g_attn", "grp_g_conv", "w_out", "norm2_g",
        "ffn_up", "ffn_conv", "ffn_down", "final_g"]


def kernel(**inputs):
    import numpy as np
    import concourse.bacc as bacc
    from concourse.bass_utils import run_bass_kernel_spmd

    nc = bacc.Bacc("TRN2", target_bir_lowering=False, num_devices=1)
    arrays, args = {}, []
    named = [(name, np.ascontiguousarray(inputs[name])) for name in _INS]
    named += list(zip(("k_f32", "k_mask"), shape_constants()))
    for name, a in named:
        arrays[f"in_{name}"] = a
        args.append(nc.dram_tensor(f"in_{name}", a.shape, mybir.dt.from_np(a.dtype), kind="ExternalInput").ap())
    args.append(nc.dram_tensor("out_0", (1, S, D), F32, kind="ExternalOutput").ap())
    build(nc, *args)
    return run_bass_kernel_spmd(nc, [arrays], core_ids=[0]).results[0]["out_0"]
```
